# Optimizing a Trainium2 kernel written in Bass

```python
import math
import jax, jax.numpy as jnp
from jax import lax
import numpy as np

D_MODEL = 1024
BATCH = 1
SEQ = 512
DEPTH = 1

MEM_TOKENS = 256
N_MEM_HEADS = 4
DH_MEM = 128
MEM_WIDTH = N_MEM_HEADS * DH_MEM
N_DIFF_HEADS = 8
DH_DIFF = 64
DIFF_Q_WIDTH = N_DIFF_HEADS * 2 * DH_DIFF
DIFF_V_WIDTH = N_DIFF_HEADS * 2 * DH_DIFF
Q_BLOCK = 128
POOL_WINDOWS = (2, 4, 8, 16)
POOL_GROUPS = len(POOL_WINDOWS)
POOL_GROUP_WIDTH = 128
POOL_WIDTH = POOL_GROUPS * POOL_GROUP_WIDTH
N_BRANCHES = 3
IN_COLS = 2 * DIFF_Q_WIDTH + DIFF_V_WIDTH + POOL_WIDTH + MEM_WIDTH + N_BRANCHES * D_MODEL
D_FF = 2816
CONV_WIDTH = 3
NORM_EPS = 1e-6


def rms_norm(x, g):
    xf = x.astype(jnp.float32)
    y = xf * lax.rsqrt(jnp.mean(xf * xf, axis=-1, keepdims=True) + NORM_EPS)
    return (y * g.astype(jnp.float32)).astype(x.dtype)

def alibi_slopes(n_heads):
    return jnp.exp2(-8.0 * jnp.arange(1, n_heads + 1, dtype=jnp.float32) / n_heads)

def lambda_init_for(layer_idx):
    return 0.8 - 0.6 * math.exp(-0.3 * layer_idx)

def diff_attention(q, k, v, lam):
    B, S = q.shape[0], q.shape[1]
    n_blocks = S // Q_BLOCK
    scale = DH_DIFF ** -0.5
    slopes = alibi_slopes(N_DIFF_HEADS)
    kf = k.astype(jnp.float32)
    vf = v.astype(jnp.float32)
    kpos = jnp.arange(S)
    qb = q.astype(jnp.float32).reshape(B, n_blocks, Q_BLOCK, N_DIFF_HEADS, 2, DH_DIFF)
    qb = jnp.moveaxis(qb, 1, 0)

    def one_block(args):
        qblk, i = args
        qpos = i * Q_BLOCK + jnp.arange(Q_BLOCK)
        s = jnp.einsum('bqhcd,bkhcd->bhcqk', qblk, kf) * scale
        dist = qpos[:, None] - kpos[None, :]
        bias = -slopes[:, None, None] * dist.astype(jnp.float32)
        s = s + bias[None, :, None]
        s = jnp.where((dist >= 0)[None, None, None], s, jnp.finfo(jnp.float32).min)
        p = jax.nn.softmax(s, axis=-1)
        a = p[:, :, 0] - lam * p[:, :, 1]
        return jnp.einsum('bhqk,bkhe->bqhe', a, vf)

    out = lax.map(one_block, (qb, jnp.arange(n_blocks)))
    return jnp.moveaxis(out, 0, 1).reshape(B, S, N_DIFF_HEADS, 2 * DH_DIFF)

def multiscale_pool(u, pool_w, pool_scale):
    B, S, _ = u.shape
    uf = u.astype(jnp.float32).reshape(B, S, POOL_GROUPS, POOL_GROUP_WIDTH)
    csum = jnp.cumsum(uf, axis=1)
    cpad = jnp.concatenate([jnp.zeros_like(csum[:, :1]), csum], axis=1)
    t = jnp.arange(S)
    outs = []
    for g, w in enumerate(POOL_WINDOWS):
        lo = jnp.maximum(t + 1 - w, 0)
        window_sum = csum[:, :, g] - cpad[:, lo, g]
        count = jnp.minimum(t + 1, w).astype(jnp.float32)
        outs.append(window_sum / count[None, :, None] - uf[:, :, g])
    p = jnp.stack(outs, axis=2)
    y = jnp.einsum('bsgc,gcd->bsgd', p, pool_w.astype(jnp.float32))
    return (y.reshape(B, S, POOL_WIDTH) * pool_scale.astype(jnp.float32)).astype(u.dtype)

def memory_cross_attention(q, mem_n, w_mem_kv):
    B, S, _ = q.shape
    kv = mem_n @ w_mem_kv
    k_m, v_m = jnp.split(kv, 2, axis=-1)
    qh = q.astype(jnp.float32).reshape(B, S, N_MEM_HEADS, DH_MEM)
    kh = k_m.astype(jnp.float32).reshape(B, -1, N_MEM_HEADS, DH_MEM)
    vh = v_m.astype(jnp.float32).reshape(B, -1, N_MEM_HEADS, DH_MEM)
    s = jnp.einsum('bshd,bmhd->bhsm', qh, kh) * (DH_MEM ** -0.5)
    p = jax.nn.softmax(s, axis=-1)
    o = jnp.einsum('bhsm,bmhd->bshd', p, vh)
    return o.reshape(B, S, MEM_WIDTH).astype(q.dtype)

def causal_depthwise_conv(u, w, b):
    S = u.shape[1]
    up = jnp.pad(u, ((0, 0), (CONV_WIDTH - 1, 0), (0, 0)))
    y = b
    for j in range(CONV_WIDTH):
        y = y + w[j] * up[:, j:j + S]
    return y

def first_inputs(seed: int = 0) -> dict:
    key = jax.random.key(seed)
    ks = jax.random.split(key, 24)

    def nrm(k, shape, scale):
        return jax.random.normal(k, shape, jnp.float32) * scale

    def gain(k, n):
        return 1.0 + nrm(k, (DEPTH, n), 0.05)

    return {
        "x": nrm(ks[0], (BATCH, SEQ, D_MODEL), 1.0),
        "mem": nrm(ks[1], (BATCH, MEM_TOKENS, D_MODEL), 1.0),
        "norm_mix_pre": gain(ks[2], D_MODEL),
        "w_in": nrm(ks[3], (DEPTH, D_MODEL, IN_COLS), D_MODEL ** -0.5),
        "lambda_q1": nrm(ks[4], (DEPTH, DH_DIFF), 0.1),
        "lambda_k1": nrm(ks[5], (DEPTH, DH_DIFF), 0.1),
        "lambda_q2": nrm(ks[6], (DEPTH, DH_DIFF), 0.1),
        "lambda_k2": nrm(ks[7], (DEPTH, DH_DIFF), 0.1),
        "subln_g": gain(ks[8], 2 * DH_DIFF),
        "w_attn_branch": nrm(ks[9], (DEPTH, DIFF_V_WIDTH, D_MODEL), DIFF_V_WIDTH ** -0.5),
        "pool_w": nrm(ks[10], (DEPTH, POOL_GROUPS, POOL_GROUP_WIDTH, POOL_GROUP_WIDTH), POOL_GROUP_WIDTH ** -0.5),
        "pool_scale": gain(ks[11], POOL_WIDTH),
        "w_pool_branch": nrm(ks[12], (DEPTH, POOL_WIDTH, D_MODEL), POOL_WIDTH ** -0.5),
        "norm_mem": gain(ks[13], D_MODEL),
        "w_mem_kv": nrm(ks[14], (DEPTH, D_MODEL, 2 * MEM_WIDTH), D_MODEL ** -0.5),
        "w_mem_branch": nrm(ks[15], (DEPTH, MEM_WIDTH, D_MODEL), MEM_WIDTH ** -0.5),
        "w_out": nrm(ks[16], (DEPTH, D_MODEL, D_MODEL), D_MODEL ** -0.5),
        "norm_mix_post": gain(ks[17], D_MODEL),
        "norm_ffn_pre": gain(ks[18], D_MODEL),
        "w_up": nrm(ks[19], (DEPTH, D_MODEL, 2 * D_FF), D_MODEL ** -0.5),
        "conv_w": nrm(ks[20], (DEPTH, CONV_WIDTH, 2 * D_FF), CONV_WIDTH ** -0.5),
        "conv_b": nrm(ks[21], (DEPTH, 2 * D_FF), 0.02),
        "w_down": nrm(ks[22], (DEPTH, D_FF, D_MODEL), D_FF ** -0.5),
        "norm_ffn_post": gain(ks[23], D_MODEL),
    }

def first_block(x, mem, norm_mix_pre, w_in, lambda_q1, lambda_k1, lambda_q2, lambda_k2, subln_g,
              w_attn_branch, pool_w, pool_scale, w_pool_branch, norm_mem, w_mem_kv, w_mem_branch,
              w_out, norm_mix_post, norm_ffn_pre, w_up, conv_w, conv_b, w_down, norm_ffn_post):
    B, S, D = x.shape
    split_pts = np.cumsum([DIFF_Q_WIDTH, DIFF_Q_WIDTH, DIFF_V_WIDTH, POOL_WIDTH, MEM_WIDTH]).tolist()
    for l in range(DEPTH):
        lam_init = lambda_init_for(l)
        h = rms_norm(x, norm_mix_pre[l])
        proj = h @ w_in[l]
        q_d, k_d, v_d, u_p, q_m, gate_logits = jnp.split(proj, split_pts, axis=-1)

        lam = (jnp.exp(jnp.sum(lambda_q1[l].astype(jnp.float32) * lambda_k1[l].astype(jnp.float32)))
               - jnp.exp(jnp.sum(lambda_q2[l].astype(jnp.float32) * lambda_k2[l].astype(jnp.float32)))
               + lam_init)
        q_d = q_d.reshape(B, S, N_DIFF_HEADS, 2, DH_DIFF)
        k_d = k_d.reshape(B, S, N_DIFF_HEADS, 2, DH_DIFF)
        v_d = v_d.reshape(B, S, N_DIFF_HEADS, 2 * DH_DIFF)
        a = diff_attention(q_d, k_d, v_d, lam)
        a = rms_norm(a, subln_g[l]) * (1.0 - lam_init)
        y_attn = a.reshape(B, S, DIFF_V_WIDTH).astype(x.dtype) @ w_attn_branch[l]

        y_pool = multiscale_pool(u_p, pool_w[l], pool_scale[l]) @ w_pool_branch[l]

        mem_n = rms_norm(mem, norm_mem[l])
        y_mem = memory_cross_attention(q_m, mem_n, w_mem_kv[l]) @ w_mem_branch[l]

        gates = jax.nn.sigmoid(gate_logits.astype(jnp.float32)).reshape(B, S, N_BRANCHES, D).astype(x.dtype)
        mix = gates[:, :, 0] * y_attn + gates[:, :, 1] * y_pool + gates[:, :, 2] * y_mem
        x = x + rms_norm(mix @ w_out[l], norm_mix_post[l])

        h2 = rms_norm(x, norm_ffn_pre[l])
        up = causal_depthwise_conv(h2 @ w_up[l], conv_w[l], conv_b[l])
        g, v = jnp.split(up, 2, axis=-1)
        ff = (jax.nn.gelu(g, approximate=True) * v) @ w_down[l]
        x = x + rms_norm(ff, norm_ffn_post[l])
    return x


DEPTH_2 = 2

GRID_W = 64
CTX_LEN = 256
HEAD_DIM = 64
ROPE_THETA = 10000.0
EPS = 1e-6
NEG_INF = -1e30
ATTN_SCALE = HEAD_DIM ** -0.5

A_HEADS = 8
A_KV_HEADS = 2
B_HEADS = 8
B_KV_HEADS = 2
B_WINDOW = 128
C_WIDTH = 512
C_CONV = 31
D_HEADS = 8
NA_KH = 8
NA_KW = 16

A_Q = A_HEADS * HEAD_DIM
A_KV = A_KV_HEADS * HEAD_DIM
B_Q = B_HEADS * HEAD_DIM
B_KV = B_KV_HEADS * HEAD_DIM
D_W = D_HEADS * HEAD_DIM
EVEN_WIDTHS = (A_Q, A_KV, A_KV, A_Q, B_Q, B_KV, B_KV, B_Q)
ODD_WIDTHS = (C_WIDTH, C_WIDTH, C_WIDTH, D_W, D_W, D_W, D_W)
EVEN_IN = sum(EVEN_WIDTHS)
ODD_IN = sum(ODD_WIDTHS)
EVEN_MIX = A_Q + B_Q
ODD_MIX = C_WIDTH + D_W


def rms_norm_2(x, g):
    xf = x.astype(jnp.float32)
    y = xf * lax.rsqrt(jnp.mean(xf * xf, axis=-1, keepdims=True) + EPS)
    return (y * g.astype(jnp.float32)).astype(x.dtype)

def layer_norm(x, g, b):
    xf = x.astype(jnp.float32)
    mu = jnp.mean(xf, axis=-1, keepdims=True)
    var = jnp.mean(jnp.square(xf - mu), axis=-1, keepdims=True)
    y = (xf - mu) * lax.rsqrt(var + EPS)
    return (y * g.astype(jnp.float32) + b.astype(jnp.float32)).astype(x.dtype)

def split_cols(h, widths):
    offs = [int(o) for o in np.cumsum(widths)[:-1]]
    return jnp.split(h, offs, axis=-1)

def heads(t, n_heads):
    return t.reshape(t.shape[:-1] + (n_heads, HEAD_DIM))

def group(q, kv_heads):
    return q.reshape(q.shape[:-2] + (kv_heads, q.shape[-2] // kv_heads, HEAD_DIM))

def axial_rope_tables(n):
    t = jnp.arange(n)
    row = (t // GRID_W).astype(jnp.float32)
    col = (t % GRID_W).astype(jnp.float32)
    half = HEAD_DIM // 2
    freqs = ROPE_THETA ** (-jnp.arange(0, half, 2, dtype=jnp.float32) / half)
    ang = jnp.concatenate([row[:, None] * freqs, col[:, None] * freqs], axis=-1)
    return jnp.cos(ang), jnp.sin(ang)

def apply_rope(x, cos, sin):
    xf = x.astype(jnp.float32)
    x1, x2 = xf[..., 0::2], xf[..., 1::2]
    c, s = cos[None, :, None, :], sin[None, :, None, :]
    out = jnp.stack([x1 * c - x2 * s, x1 * s + x2 * c], axis=-1).reshape(x.shape)
    return out.astype(x.dtype)

def gqa_attend(q, k, v, bias=None, sink=None):
    s = jnp.einsum("bqhgd,bkhd->bhgqk", q, k, preferred_element_type=jnp.float32) * ATTN_SCALE
    if bias is not None:
        s = s + bias
    if sink is not None:
        sink_col = jnp.broadcast_to(sink.astype(jnp.float32)[None, :, :, None, None], s.shape[:-1] + (1,))
        p = jax.nn.softmax(jnp.concatenate([s, sink_col], axis=-1), axis=-1)[..., :-1]
    else:
        p = jax.nn.softmax(s, axis=-1)
    return jnp.einsum("bhgqk,bkhd->bqhgd", p.astype(v.dtype), v)

def even_mixer(h_lat, h_ctx, w_in, w_out, q_gain, k_gain, sink, cos, sin, update_ctx):
    bsz, n, _ = h_lat.shape
    ctx_len = h_ctx.shape[1]
    n_blk = n // Q_BLOCK
    ga, gb = A_HEADS // A_KV_HEADS, B_HEADS // B_KV_HEADS
    sink = sink.reshape(B_KV_HEADS, gb)

    def project(h):
        aq, ak, av, ag, bq, bk, bv, bg = split_cols(h @ w_in, EVEN_WIDTHS)
        aq = rms_norm_2(heads(aq, A_HEADS), q_gain)
        ak = rms_norm_2(heads(ak, A_KV_HEADS), k_gain)
        return (aq, ak, heads(av, A_KV_HEADS), ag,
                heads(bq, B_HEADS), heads(bk, B_KV_HEADS), heads(bv, B_KV_HEADS), bg)

    aq, ak, av, ag, bq, bk, bv, bg = project(h_lat)
    c_aq, c_ak, c_av, c_ag, c_bq, c_bk, c_bv, c_bg = project(h_ctx)
    aq, ak, bq, bk = (apply_rope(t, cos, sin) for t in (aq, ak, bq, bk))

    ka = jnp.concatenate([c_ak, ak], axis=1)
    va = jnp.concatenate([c_av, av], axis=1)
    qa_blk = jnp.moveaxis(group(aq, A_KV_HEADS).reshape(bsz, n_blk, Q_BLOCK, A_KV_HEADS, ga, HEAD_DIM), 1, 0)
    oa = lax.map(lambda qb: gqa_attend(qb, ka, va), qa_blk)
    oa = jnp.moveaxis(oa, 0, 1).reshape(bsz, n, A_Q)

    band = Q_BLOCK + 2 * B_WINDOW
    kb_pad = jnp.pad(bk, ((0, 0), (B_WINDOW, B_WINDOW), (0, 0), (0, 0)))
    vb_pad = jnp.pad(bv, ((0, 0), (B_WINDOW, B_WINDOW), (0, 0), (0, 0)))
    rel = jnp.arange(band)[None, :] - B_WINDOW - jnp.arange(Q_BLOCK)[:, None]
    in_band = jnp.abs(rel) <= B_WINDOW
    ctx_open = jnp.zeros((Q_BLOCK, ctx_len), jnp.float32)
    qb_blk = jnp.moveaxis(group(bq, B_KV_HEADS).reshape(bsz, n_blk, Q_BLOCK, B_KV_HEADS, gb, HEAD_DIM), 1, 0)

    def b_block(args):
        blk, qb = args
        start = blk * Q_BLOCK
        kpos = start - B_WINDOW + jnp.arange(band)
        valid = in_band & ((kpos >= 0) & (kpos < n))[None, :]
        bias = jnp.concatenate([ctx_open, jnp.where(valid, 0.0, NEG_INF)], axis=-1)
        kk = jnp.concatenate([c_bk, lax.dynamic_slice_in_dim(kb_pad, start, band, axis=1)], axis=1)
        vv = jnp.concatenate([c_bv, lax.dynamic_slice_in_dim(vb_pad, start, band, axis=1)], axis=1)
        return gqa_attend(qb, kk, vv, bias, sink)

    ob = lax.map(b_block, (jnp.arange(n_blk), qb_blk))
    ob = jnp.moveaxis(ob, 0, 1).reshape(bsz, n, B_Q)

    y_lat = jnp.concatenate([oa * jax.nn.silu(ag), ob * jax.nn.silu(bg)], axis=-1) @ w_out
    if not update_ctx:
        return y_lat, None
    oa_c = gqa_attend(group(c_aq, A_KV_HEADS), c_ak, c_av).reshape(bsz, ctx_len, A_Q)
    ob_c = gqa_attend(group(c_bq, B_KV_HEADS), c_bk, c_bv, sink=sink).reshape(bsz, ctx_len, B_Q)
    y_ctx = jnp.concatenate([oa_c * jax.nn.silu(c_ag), ob_c * jax.nn.silu(c_bg)], axis=-1) @ w_out
    return y_lat, y_ctx

def conformer_conv(val, glu_gate, silu_gate, dw_w, dw_b, ln_g, ln_b):
    u = val * jax.nn.sigmoid(glu_gate)
    u = lax.conv_general_dilated(u, dw_w.reshape(C_CONV, 1, C_WIDTH), window_strides=(1,),
                                 padding=[(C_CONV // 2, C_CONV // 2)],
                                 dimension_numbers=("NWC", "WIO", "NWC"),
                                 feature_group_count=C_WIDTH) + dw_b
    u = jax.nn.silu(layer_norm(u, ln_g, ln_b))
    return u * jax.nn.silu(silu_gate)

def odd_mixer(h_lat, h_ctx, w_in, w_out, dw_w, dw_b, ln_g, ln_b, rpb, update_ctx):
    bsz, n, _ = h_lat.shape
    ctx_len = h_ctx.shape[1]
    rows = n // GRID_W
    kh = min(NA_KH, rows)

    cv, cgl, cg, dq, dk, dv, dg = split_cols(h_lat @ w_in, ODD_WIDTHS)
    x_cv, x_cgl, x_cg, x_dq, x_dk, x_dv, x_dg = split_cols(h_ctx @ w_in, ODD_WIDTHS)
    c_dk, c_dv = heads(x_dk, D_HEADS), heads(x_dv, D_HEADS)

    oc = conformer_conv(cv, cgl, cg, dw_w, dw_b, ln_g, ln_b)

    q_rows = jnp.moveaxis(heads(dq, D_HEADS).reshape(bsz, rows, GRID_W, D_HEADS, HEAD_DIM), 1, 0)
    k_grid = heads(dk, D_HEADS).reshape(bsz, rows, GRID_W, D_HEADS, HEAD_DIM)
    v_grid = heads(dv, D_HEADS).reshape(bsz, rows, GRID_W, D_HEADS, HEAD_DIM)
    cols = jnp.arange(GRID_W)
    col_start = jnp.clip(cols - NA_KW // 2, 0, GRID_W - NA_KW)
    col_in = (cols[None, :] >= col_start[:, None]) & (cols[None, :] < col_start[:, None] + NA_KW)
    col_mask = jnp.where(col_in, 0.0, NEG_INF)
    dc_idx = jnp.clip(cols[None, :] - cols[:, None] + NA_KW - 1, 0, 2 * NA_KW - 2)
    rpb = rpb.astype(jnp.float32)
    ctx_open = jnp.zeros((D_HEADS, GRID_W, ctx_len), jnp.float32)

    def d_row(args):
        r, qr = args
        rs = jnp.clip(r - kh // 2, 0, rows - kh)
        kr = lax.dynamic_slice_in_dim(k_grid, rs, kh, axis=1).reshape(bsz, kh * GRID_W, D_HEADS, HEAD_DIM)
        vr = lax.dynamic_slice_in_dim(v_grid, rs, kh, axis=1).reshape(bsz, kh * GRID_W, D_HEADS, HEAD_DIM)
        dr_idx = rs + jnp.arange(kh) - r + NA_KH - 1
        bias = rpb[:, dr_idx][:, :, dc_idx] + col_mask[None, None]
        bias = jnp.transpose(bias, (0, 2, 1, 3)).reshape(D_HEADS, GRID_W, kh * GRID_W)
        bias = jnp.concatenate([ctx_open, bias], axis=-1)[None, :, None]
        kk = jnp.concatenate([c_dk, kr], axis=1)
        vv = jnp.concatenate([c_dv, vr], axis=1)
        return gqa_attend(qr[:, :, :, None, :], kk, vv, bias).reshape(bsz, GRID_W, D_W)

    od = lax.map(d_row, (jnp.arange(rows), q_rows))
    od = jnp.moveaxis(od, 0, 1).reshape(bsz, n, D_W)

    y_lat = jnp.concatenate([oc, od * jax.nn.silu(dg)], axis=-1) @ w_out
    if not update_ctx:
        return y_lat, None
    oc_c = conformer_conv(x_cv, x_cgl, x_cg, dw_w, dw_b, ln_g, ln_b)
    od_c = gqa_attend(heads(x_dq, D_HEADS)[:, :, :, None, :], c_dk, c_dv).reshape(bsz, ctx_len, D_W)
    y_ctx = jnp.concatenate([oc_c, od_c * jax.nn.silu(x_dg)], axis=-1) @ w_out
    return y_lat, y_ctx

def modulation(cond, w, b):
    m = jax.nn.silu(cond) @ w + b
    return jnp.split(m, 3, axis=-1)

def second_inputs(seed: int = 0) -> dict:
    key = jax.random.key(seed)
    ks = jax.random.split(key, 24)
    n_even = (DEPTH_2 + 1) // 2
    n_odd = DEPTH_2 // 2
    f32 = jnp.float32

    def nrm(k, shape, scale):
        return jax.random.normal(k, shape, f32) * scale

    return {
        "x": nrm(ks[0], (BATCH, SEQ, D_MODEL), 1.0),
        "c": nrm(ks[1], (BATCH, D_MODEL), 1.0),
        "ctx": nrm(ks[2], (BATCH, CTX_LEN, D_MODEL), 1.0),
        "c_ctx": nrm(ks[3], (D_MODEL,), 1.0),
        "mod_w": nrm(ks[4], (DEPTH_2, D_MODEL, 3 * D_MODEL), 0.5 * D_MODEL ** -0.5),
        "mod_b": nrm(ks[5], (DEPTH_2, 3 * D_MODEL), 0.02),
        "norm_g": 1.0 + nrm(ks[6], (DEPTH_2, D_MODEL), 0.05),
        "ev_w_in": nrm(ks[7], (n_even, D_MODEL, EVEN_IN), D_MODEL ** -0.5),
        "ev_w_out": nrm(ks[8], (n_even, EVEN_MIX, D_MODEL), EVEN_MIX ** -0.5),
        "a_q_gain": 1.0 + nrm(ks[9], (n_even, HEAD_DIM), 0.05),
        "a_k_gain": 1.0 + nrm(ks[10], (n_even, HEAD_DIM), 0.05),
        "b_sink": nrm(ks[11], (n_even, B_HEADS), 0.5),
        "od_w_in": nrm(ks[12], (n_odd, D_MODEL, ODD_IN), D_MODEL ** -0.5),
        "od_w_out": nrm(ks[13], (n_odd, ODD_MIX, D_MODEL), ODD_MIX ** -0.5),
        "c_dw_w": nrm(ks[14], (n_odd, C_CONV, C_WIDTH), C_CONV ** -0.5),
        "c_dw_b": nrm(ks[15], (n_odd, C_WIDTH), 0.02),
        "c_ln_g": 1.0 + nrm(ks[16], (n_odd, C_WIDTH), 0.05),
        "c_ln_b": nrm(ks[17], (n_odd, C_WIDTH), 0.02),
        "d_rpb": nrm(ks[18], (n_odd, D_HEADS, 2 * NA_KH - 1, 2 * NA_KW - 1), 0.1),
        "final_g": 1.0 + nrm(ks[19], (D_MODEL,), 0.05),
    }

def second_block(x, c, ctx, c_ctx, mod_w, mod_b, norm_g, ev_w_in, ev_w_out, a_q_gain, a_k_gain, b_sink,
              od_w_in, od_w_out, c_dw_w, c_dw_b, c_ln_g, c_ln_b, d_rpb, final_g):
    n = x.shape[1]
    cos, sin = axial_rope_tables(n)
    x_lat, x_ctx = x, ctx
    for i in range(DEPTH_2):
        update_ctx = i < DEPTH_2 - 1
        sh_l, sc_l, g_l = modulation(c, mod_w[i], mod_b[i])
        sh_c, sc_c, g_c = modulation(c_ctx, mod_w[i], mod_b[i])
        h_lat = rms_norm_2(x_lat, norm_g[i]) * (1.0 + sc_l[:, None, :]) + sh_l[:, None, :]
        h_ctx = rms_norm_2(x_ctx, norm_g[i]) * (1.0 + sc_c) + sh_c
        j = i // 2
        if i % 2 == 0:
            y_lat, y_ctx = even_mixer(h_lat, h_ctx, ev_w_in[j], ev_w_out[j], a_q_gain[j], a_k_gain[j],
                                      b_sink[j], cos, sin, update_ctx)
        else:
            y_lat, y_ctx = odd_mixer(h_lat, h_ctx, od_w_in[j], od_w_out[j], c_dw_w[j], c_dw_b[j],
                                     c_ln_g[j], c_ln_b[j], d_rpb[j], update_ctx)
        x_lat = x_lat + g_l[:, None, :] * y_lat
        if update_ctx:
            x_ctx = x_ctx + g_c * y_ctx
    return rms_norm_2(x_lat, final_g)


def setup_inputs(seed=0):
    out = dict(first_inputs(seed))
    for name, value in second_inputs(seed + 1).items():
        if name != "x":
            out[name + "_2"] = value
    return out


def reference(
    x, mem, norm_mix_pre, w_in, lambda_q1, lambda_k1, lambda_q2, lambda_k2, subln_g,
    w_attn_branch, pool_w, pool_scale, w_pool_branch, norm_mem, w_mem_kv, w_mem_branch, w_out,
    norm_mix_post, norm_ffn_pre, w_up, conv_w, conv_b, w_down, norm_ffn_post, c_2, ctx_2,
    c_ctx_2, mod_w_2, mod_b_2, norm_g_2, ev_w_in_2, ev_w_out_2, a_q_gain_2, a_k_gain_2,
    b_sink_2, od_w_in_2, od_w_out_2, c_dw_w_2, c_dw_b_2, c_ln_g_2, c_ln_b_2, d_rpb_2, final_g_2,
):
    x = first_block(
        x, mem, norm_mix_pre, w_in, lambda_q1, lambda_k1, lambda_q2, lambda_k2, subln_g,
        w_attn_branch, pool_w, pool_scale, w_pool_branch, norm_mem, w_mem_kv, w_mem_branch,
        w_out, norm_mix_post, norm_ffn_pre, w_up, conv_w, conv_b, w_down, norm_ffn_post,
    )
    return second_block(
        x, c_2, ctx_2, c_ctx_2, mod_w_2, mod_b_2, norm_g_2, ev_w_in_2, ev_w_out_2, a_q_gain_2,
        a_k_gain_2, b_sink_2, od_w_in_2, od_w_out_2, c_dw_w_2, c_dw_b_2, c_ln_g_2, c_ln_b_2,
        d_rpb_2, final_g_2,
    )


_drawn_inputs = setup_inputs


def setup_inputs(seed=0):
    import zlib

    import numpy as np

    out = dict(_drawn_inputs(seed))
    spreads = {}
    factors = {'lambda_k1': 3.181,
     'lambda_q2': 3.335,
     'norm_mem': 8.0,
     'conv_b': 3.311,
     'ctx_2': 5.928,
     'mod_b_2': 8.0,
     'norm_g_2': 8.0,
     'a_q_gain_2': 8.0,
     'a_k_gain_2': 8.0,
     'b_sink_2': 8.0,
     'c_dw_b_2': 42.828,
     'c_ln_g_2': 22.424,
     'c_ln_b_2': 57.481,
     'd_rpb_2': 8.0}
    for name, (base, spread) in spreads.items():
        noise = np.random.default_rng([zlib.crc32(name.encode()), seed]).standard_normal(out[name].shape)
        drawn = base * np.exp(spread * noise) if base else spread * noise
        out[name] = __import__('jax').numpy.asarray(drawn.astype(out[name].dtype))
    for name, factor in factors.items():
        out[name] = (out[name] * factor).astype(out[name].dtype)
    return out
```

```python
import math
from contextlib import contextmanager

import numpy as np

import concourse.bass as bass
from concourse import mybir
from concourse.alu_op_type import AluOpType as ALU

F32 = mybir.dt.float32
F32R = mybir.dt.float32r
ACT = mybir.ActivationFunctionType
AX = mybir.AxisListType.X
P = 128
EPS = 1e-6

D_MODEL, SEQ, MEM, CTX = 1024, 512, 256, 256
DT = D_MODEL // P
NB = SEQ // P
CB = CTX // P
ALL = CTX + SEQ
DIFF_HEADS, DIFF_DH = 8, 64
MEM_HEADS = 4
POOL_WINDOWS = (2, 4, 8, 16)
POOL_PAD = max(POOL_WINDOWS)
LAM_INIT = 0.8 - 0.6 * math.exp(-0.3 * 0)
D_FF, FT = 2816, 2816 // P
HEAD = 64
GRID_W, NA_KH, NA_KW = 64, 8, 16
CONV_TAPS = 31
CT = 512 // P
MASKED = -1e30
CHUNK_COLS = 256
CHUNK = DT * CHUNK_COLS

ROWS = dict(norm_mix_pre=8, norm_mem=8, norm_mix_post=8, norm_ffn_pre=8, norm_ffn_post=8, pool_scale=4,
            subln_g=1, final_g_2=8, norm_g_2=16, mod_b_2=48, conv_b=44, c_2=8, c_ctx_2=8,
            a_q_gain_2=1, a_k_gain_2=1, c_dw_b_2=4, c_ln_g_2=4, c_ln_b_2=4, conv_w=132, c_dw_w_2=124)


def row_places():
    at, places = 0, {}
    for name, n in ROWS.items():
        places[name] = at
        at += n
    return places, -(-at // P)


def shape_tables():
    f = np.float32
    t = {}
    t["ident"] = np.eye(P, dtype=f)
    q, j = np.arange(P)[:, None], np.arange(SEQ)[None, :]
    rel = j - (SEQ - P) - q
    t["distance"] = np.where(rel <= 0, rel, -1e32).astype(f)
    t["slopes"] = np.tile(np.exp2(-8.0 * np.arange(1, DIFF_HEADS + 1) / DIFF_HEADS).astype(f), (P, 1))
    k = np.arange(P)[None, :]
    t["band_left"] = np.where(k >= q, 0, MASKED).astype(f)
    t["band_right"] = np.where(k <= q, 0, MASKED).astype(f)
    tok = np.arange(SEQ)
    half = HEAD // 2
    freqs = 10000.0 ** (-np.arange(0, half, 2, dtype=f) / half)
    ang = np.concatenate([(tok // GRID_W).astype(f)[:, None] * freqs, (tok % GRID_W).astype(f)[:, None] * freqs], -1)
    pair = (np.arange(P) % HEAD) // 2
    t["rope_cos"] = np.cos(ang).astype(f)[:, pair].T.copy()
    t["rope_sin"] = np.sin(ang).astype(f)[:, pair].T.copy()
    rot = np.zeros((P, P), f)
    e = np.arange(0, P, 2)
    rot[e + 1, e] = -1
    rot[e, e + 1] = 1
    t["rotate"] = rot
    rev = np.zeros((P, P), f)
    i = np.arange(P)
    rev[i, (i // GRID_W) * GRID_W + GRID_W - 1 - i % GRID_W] = 1
    t["reverse"] = rev
    qc, kc = np.arange(GRID_W)[:, None], np.arange(GRID_W)[None, :]
    start = np.clip(qc - NA_KW // 2, 0, GRID_W - NA_KW)
    near = np.where((kc >= start) & (kc < start + NA_KW), 0, MASKED).astype(f)
    t["near_mask"] = np.concatenate([near, near])
    gather = np.zeros((P, 5, 10), f)
    spread = np.zeros((10, 5, P), f)
    for n in range(5):
        for p in range(P):
            gather[p, n, 2 * n + p // HEAD] = 1.0 / HEAD
            spread[2 * n + p // HEAD, n, p] = 1
    t["head_gather"] = gather.reshape(P, 50)
    t["head_spread"] = np.pad(spread.reshape(10, 5 * P), ((0, P - 10), (0, 0)))
    corr = np.zeros((len(POOL_WINDOWS), POOL_PAD), f)
    for g, w in enumerate(POOL_WINDOWS):
        corr[g] = w / np.minimum(np.arange(POOL_PAD) + 1, w)
    t["pool_edge"] = np.tile(corr.reshape(1, -1), (P, 1))
    return t


class Mark:

    def __init__(self, sem, at, step=0, reg=None):
        self.sem, self.at, self.step, self.reg = sem, at, step, reg

    def value(self):
        return self.at + self.step * self.reg if self.reg is not None else self.at

    def before(self, n=1):
        return Mark(self.sem, self.at - n * self.step, self.step, self.reg)

    def minus(self, n):
        return Mark(self.sem, self.at - n, self.step, self.reg)


class Engine:

    def __init__(self, nc, e, name):
        self.e, self.sem, self.n = e, nc.alloc_semaphore(name + "_done"), 0
        self.step, self.reg = 0, None

    def sig(self, ins):
        ins.then_inc(self.sem, 1)
        self.n += 1
        return Mark(self.sem, self.n, self.step, self.reg)

    def now(self):
        return Mark(self.sem, self.n, self.step, self.reg)

    def need(self, *marks):
        for m in marks:
            if m is not None:
                self.e.wait_ge(m.sem, m.value())


def build(nc, a):
    PE, ACTE, DVE, POOL = (Engine(nc, e, n) for e, n in (
        (nc.tensor, "pe"), (nc.scalar, "act"), (nc.vector, "dve"), (nc.gpsimd, "pool")))
    SP = nc.sync

    @contextmanager
    def loop(n, **steps):
        es = {"pe": PE, "act": ACTE, "dve": DVE, "pool": POOL}
        used = {k: es[k] for k in steps}
        start = {k: x.n for k, x in used.items()}
        with nc.Fori(0, n, engines=[x.e.engine for x in used.values()]) as i:
            for k, x in used.items():
                x.step, x.reg = steps[k], i
            yield i
            for k, x in used.items():
                assert x.n - start[k] == steps[k], (k, x.n - start[k], steps[k])
                x.step, x.reg = 0, None
                x.n = start[k] + n * steps[k]

    base = [(nc.sbuf_base + 63) // 64 * 64]

    def sb(name, shape, dt=F32, at=None):
        size = 4 * int(np.prod(shape[1:]))
        if at is None:
            at = base[0]
            base[0] += (size + 63) // 64 * 64
        return nc.alloc_sbuf_tensor_at(name, shape, dt, offset=at)

    raw = [sb(f"w_raw{p}", [P, CHUNK]) for p in range(2)]
    whi = [sb(f"w_hi{p}", [P, CHUNK], F32R) for p in range(2)]
    wlo = [sb(f"w_lo{p}", [P, CHUNK], F32R) for p in range(2)]
    xT = sb("x_T", [P, DT, SEQ])
    hhi, hlo = sb("h_hi", [P, DT, SEQ], F32R), sb("h_lo", [P, DT, SEQ], F32R)
    C0 = base[0]
    chi, clo = sb("c_hi", [P, DT, CTX], F32R), sb("c_lo", [P, DT, CTX], F32R)
    places, n_groups = row_places()
    cols = sb("cols", [P, n_groups * P])
    ident = sb("ident", [P, P])
    ones = sb("ones", [P, P])
    small = sb("small", [P, 256])
    rowvec = sb("rowvec", [1, 16])
    lamrow = sb("lamrow", [1, 4, DIFF_DH])
    modT = sb("mod_T", [P, 2, 24, 2])
    R0 = base[0]
    R_END = nc.sbuf_usable_end

    def region(at):
        pos = [at]

        def put(name, shape, dt=F32):
            size = 4 * int(np.prod(shape[1:]))
            t = nc.alloc_sbuf_tensor_at(name, shape, dt, offset=pos[0])
            pos[0] += (size + 63) // 64 * 64
            put.end = pos[0]
            return t
        return put

    ps = nc.alloc_psum_tensor("ps", [P, 8 * 512], F32)

    def bank(b, n=512, off=0, parts=P):
        return ps[0:parts, b * 512 + off:b * 512 + off + n]

    def col(name, i=0):
        c = places[name] + i
        return cols[:, c:c + 1]

    def dyn_col(name, i):
        return cols[:, bass.ds(places[name] + i, 1)]

    eps = small[:, 0:1]
    nlam = small[:, 1:2]
    sink = small[:, 2:10]
    nsink = small[:, 10:18]
    qgain = small[:, 18:19]
    subg = small[:, 19:20]
    zero1 = small[:, 20:21]
    slopes = small[:, 24:32]
    st = small[:, 32:48]
    sm = small[:, 48:80]

    sem_in = nc.alloc_semaphore("inputs_landed")
    landed = [0]

    def load(eng, dst, src):
        eng.dma_start(dst, src).then_inc(sem_in, 16)
        landed[0] += 16

    def need_inputs(*engines):
        for x in engines:
            x.e.wait_ge(sem_in, landed[0])

    def act(out, in_, func=ACT.Copy, **kw):
        return ACTE.sig(nc.scalar.activation(out, in_, func, **kw))

    def f(ap):
        return ap.bitcast(F32)

    setup = region(R0)
    xin = setup("x_in", [P, NB, D_MODEL])
    min_ = setup("mem_in", [P, CB, D_MODEL])
    memT = setup("mem_T", [P, DT, MEM])
    rows = setup("rows", [P, n_groups, P])
    load(SP, ident[:], a["t_ident"])
    load(SP, xin[:], a["x"][0].rearrange("(b p) d -> p b d", p=P))

    def load_rows(name, src, at=0):
        r, n, done = places[name] + at, src.shape[0], 0
        while done < n:
            g, p = (r + done) // P, (r + done) % P
            k = min(n - done, P - p)
            load(nc.scalar, rows[p:p + k, g, :], src[done:done + k, :])
            done += k

    DVE.sig(nc.vector.memset(rows[:], 0.0))
    ACTE.need(DVE.now())
    for name in ("norm_mix_pre", "norm_mem", "norm_mix_post", "norm_ffn_pre", "norm_ffn_post", "conv_b",
                 "norm_g_2", "c_2", "c_dw_b_2", "c_ln_g_2", "c_ln_b_2", "pool_scale", "mod_b_2"):
        load_rows(name, a[name].rearrange("l (t p) -> (l t) p", p=P))
    load_rows("subln_g", a["subln_g"])
    for name in ("c_ctx_2", "final_g_2"):
        load_rows(name, a[name].rearrange("(t p) -> t p", p=P))
    load_rows("conv_w", a["conv_w"].rearrange("l j (t p) -> (l j t) p", p=P))
    load_rows("c_dw_w_2", a["c_dw_w_2"].rearrange("l j (t p) -> (l j t) p", p=P))
    for name in ("a_q_gain_2", "a_k_gain_2"):
        g, p = places[name] // P, places[name] % P
        for s in range(2):
            load(nc.scalar, rows[p:p + 1, g, s * HEAD:(s + 1) * HEAD], a[name])
    for n, name in enumerate(("lambda_q1", "lambda_k1", "lambda_q2", "lambda_k2")):
        load(nc.scalar, lamrow[:, n, :], a[name])
    load(nc.scalar, rowvec[0:1, 1:9], a["b_sink_2"])
    load(SP, slopes, a["t_slopes"])
    load(SP, min_[:], a["mem"][0].rearrange("(b p) d -> p b d", p=P))
    DVE.sig(nc.vector.memset(ones[:], 1.0))
    DVE.sig(nc.vector.memset(eps, EPS))
    DVE.sig(nc.vector.memset(zero1, 0.0))
    consts_set = DVE.sig(nc.vector.memset(rowvec[0:1, 9:16], 0.0))
    need_inputs(PE, DVE, ACTE)
    PE.need(consts_set)
    ACTE.need(consts_set)

    DVE.sig(nc.vector.tensor_tensor(lamrow[:, 0, :], lamrow[:, 0, :], lamrow[:, 1, :], ALU.mult))
    DVE.need(DVE.sig(nc.vector.tensor_tensor(lamrow[:, 2, :], lamrow[:, 2, :], lamrow[:, 3, :], ALU.mult)))
    m = DVE.sig(nc.vector.tensor_reduce(rowvec[0:1, 10:12], lamrow[:, 0:4:2, :], AX, ALU.add))
    ACTE.need(m)
    nc.scalar.preload_act_table(ACT.Exp)
    m = act(rowvec[0:1, 12:14], rowvec[0:1, 10:12], ACT.Exp)
    DVE.need(m)
    DVE.need(DVE.sig(nc.vector.tensor_tensor(rowvec[0:1, 14:15], rowvec[0:1, 12:13], rowvec[0:1, 13:14], ALU.subtract)))
    m = DVE.sig(nc.vector.tensor_scalar(rowvec[0:1, 0:1], rowvec[0:1, 14:15], LAM_INIT, None, ALU.add))
    PE.need(m)
    m = PE.sig(nc.tensor.matmul(bank(7, 16), ones[0:1, :], rowvec[0:1, :]))
    DVE.need(m)
    DVE.sig(nc.vector.tensor_scalar(nlam, bank(7, 1), -1.0, None, ALU.mult))
    DVE.sig(nc.vector.tensor_copy(sink, bank(7, 8, 1)))
    row_m = DVE.sig(nc.vector.tensor_scalar(nsink, bank(7, 8, 1), -1.0, None, ALU.mult))

    for g in range(n_groups):
        m = PE.sig(nc.tensor.transpose(bank(g), rows[:, g, :], ident[:])) if False else \
            PE.sig(nc.tensor.transpose(bank(g % 6, P), rows[:, g, :], ident[:]))
        ACTE.need(m)
        cols_set = act(cols[:, g * P:(g + 1) * P], bank(g % 6, P))
        assert n_groups <= 6
    DVE.need(cols_set)
    DVE.sig(nc.vector.tensor_scalar(qgain, col("a_q_gain_2"), HEAD ** -0.5, None, ALU.mult))
    DVE.sig(nc.vector.tensor_scalar(subg, col("subln_g"), 1.0 - LAM_INIT, None, ALU.mult))

    def to_feature_major(src, nb, dst, after, banks=(0, 1, 2, 3)):
        PE.need(*after)
        freed = [None] * len(banks)
        for t in range(DT):
            b = banks[t % len(banks)]
            PE.need(freed[t % len(banks)])
            for k in range(nb):
                ins = nc.tensor.transpose(bank(b, P, k * P), src[:, k, t * P:(t + 1) * P], ident[:])
            m = PE.sig(ins)
            if t % 2:
                ACTE.need(m)
                freed[t % len(banks)] = act(dst[:, t, :], bank(b, nb * P))
            else:
                DVE.need(m)
                freed[t % len(banks)] = DVE.sig(nc.vector.tensor_copy(dst[:, t, :], bank(b, nb * P)))
        return ACTE.now(), DVE.now()

    x_ready = to_feature_major(xin, NB, xT, (cols_set, row_m))
    mem_ready = to_feature_major(min_, CB, memT, x_ready)

    landed_w = [nc.alloc_semaphore(f"chunk_landed{p}") for p in range(2)]
    hi_done = nc.alloc_semaphore("chunk_hi_done")
    lo_done = nc.alloc_semaphore("chunk_lo_done")

    cond = region(put_end := setup.end)("cond", [P, DT, 2])
    condt = region(put_end + 64)("cond_t", [P, DT, 2])
    ACTE.need(cols_set)
    for n, name in enumerate(("c_2", "c_ctx_2")):
        c0 = places[name]
        m = act(condt[:, :, n], cols[:, c0:c0 + DT], ACT.Tanh, scale=0.5)
    DVE.need(m)
    for n, name in enumerate(("c_2", "c_ctx_2")):
        c0 = places[name]
        DVE.need(DVE.sig(nc.vector.scalar_tensor_tensor(cond[:, :, n], condt[:, :, n], 1.0, cols[:, c0:c0 + DT],
                                                        ALU.add, ALU.mult)))
    cond_ready = DVE.sig(nc.vector.tensor_scalar(cond[:], cond[:], 0.5, None, ALU.mult))
    PE.need(cond_ready, *mem_ready)
    mod_used = []
    mod_flat = modT[:].rearrange("p l t c -> p (l t) c")
    for layer in range(2):
        n0 = PE.n
        pairs = 3 * D_MODEL // CHUNK_COLS // 2
        with nc.Fori(0, pairs, engines=[SP.engine]) as i:
            for p in range(2):
                SP.wait_ge(PE.sem, n0 + 2 * i + p - 1 if layer or p else n0 + 2 * i - 1)
                src = a["mod_w_2"][layer][:, bass.ds(i * (2 * CHUNK_COLS) + p * CHUNK_COLS, CHUNK_COLS)]
                SP.dma_start(raw[p][:].rearrange("p (k n) -> p k n", k=DT),
                             src.rearrange("(k p) n -> p k n", p=P)).then_inc(landed_w[p], 16)
        with loop(pairs, pe=2, dve=4) as i:
            PE.need(DVE.now())
            for p in range(2):
                PE.e.wait_ge(landed_w[p], 16 * (layer * pairs + 1) + 16 * i)
                w = raw[p][:].rearrange("p (k n) -> p k n", k=DT)
                for o in range(2):
                    for k in range(DT):
                        ins = nc.tensor.matmul(bank(2 * p + o, 2), w[:, k, o * P:(o + 1) * P], cond[:, k, :],
                                               start=k == 0, stop=k == DT - 1)
                m = PE.sig(ins)
                DVE.need(m)
                for o in range(2):
                    t = layer * 24 + 4 * i + 2 * p + o
                    DVE.sig(nc.vector.tensor_scalar(mod_flat[:, bass.ds(t, 1), :].rearrange("p a c -> p (a c)"),
                                                    bank(2 * p + o, 2), dyn_col("mod_b_2", t), None, ALU.add))
    mod_ready = DVE.now()
    mod_done = PE.now()

    chunk = [0]
    sent = [0]

    def sp_load(p, value, src, kt, n):
        if value is not None:
            SP.wait_ge(lo_done, value)
        dst = raw[p][:, 0:kt * n].rearrange("p (k n) -> p k n", k=kt)
        SP.dma_start(dst, src.rearrange("(k p) n -> p k n", p=P)).then_inc(landed_w[p], 16)

    def stream(w, starts, step=0, n=1, rows_=(0, D_MODEL), width=CHUNK_COLS):
        r0, r1 = rows_
        kt = (r1 - r0) // P
        c0 = sent[0]
        assert len(starts) % 2 == 0
        if c0 == 0:
            SP.wait_ge(PE.sem, mod_done.at)
            for i in range(n):
                for q, s in enumerate(starts):
                    c = i * len(starts) + q
                    sp_load(q % 2, c - 1 if c > 1 else None, w[r0:r1, i * step + s:i * step + s + width], kt, width)
            sent[0] += n * len(starts)
            return
        with nc.Fori(0, n, engines=[SP.engine]) as i:
            for q, s in enumerate(starts):
                sp_load(q % 2, (c0 + q - 1) + len(starts) * i,
                        w[r0:r1, bass.ds(i * step + s, width)], kt, width)
        sent[0] += n * len(starts)

    def stream_down(w):
        c0 = sent[0]
        with nc.Fori(0, 2, engines=[SP.engine]) as i:
            for q in range(6):
                g, k = divmod(q, 3)
                k0, k1 = 8 * k, min(8 * k + 8, FT)
                sp_load(q % 2, (c0 + q - 1) + 6 * i, w[k0 * P:k1 * P, bass.ds(i * 512 + g * 256, 256)], k1 - k0, 256)
        sent[0] += 12

    raw_lead = 16 * (2 * 3 * D_MODEL // CHUNK_COLS // 2)

    def round_hi(p, c, i=None, step=0):
        v = raw_lead + 16 * (c // 2 + 1)
        ACTE.e.wait_ge(landed_w[p], v if i is None else v + 8 * step * i)
        nc.scalar.activation(whi[p][:], raw[p][:], ACT.Copy).then_inc(hi_done, 1)

    def mm3(out, whi_, wlo_, xhi_, xlo_, first, last, flip=False):
        for n, (w, x) in enumerate(((wlo_, xhi_), (whi_, xlo_), (whi_, xhi_))):
            l, r = (x, w) if flip else (w, x)
            ins = nc.tensor.matmul(out, l, r, start=first and n == 0, stop=last and n == 2)
        return ins

    class Sources:
        pass

    def gemm(n_pairs, xs, evac, kt=DT, cols_=CHUNK_COLS, flip=0, per=None, after=(), last=False, unroll=False):
        outs = 2 * cols_ // P
        base_chunk = chunk[0]
        for e in after:
            PE.need(e)

        def body(i, peeled=False):
            freed = {}
            for p in range(2):
                c = base_chunk + p
                PE.e.wait_ge(lo_done, c + 1 + 2 * i)
                hi = whi[p][:, 0:kt * cols_].rearrange("p (k n) -> p k n", k=kt)
                lo = wlo[p][:, 0:kt * cols_].rearrange("p (k n) -> p k n", k=kt)
                for o in range(cols_ // P):
                    u = p * (cols_ // P) + o
                    b = u % 4
                    if u >= 4:
                        PE.need(*freed[b])
                    else:
                        PE.need(*before[b])
                    s = slice(o * P, (o + 1) * P)
                    for n, (xh, xl, tok) in enumerate(xs):
                        for k in range(kt):
                            ins = mm3(bank(b + 4 * n, tok), hi[:, k, s], lo[:, k, s], xh[:, k, 0:tok],
                                      xl[:, k, 0:tok], k == 0, k == kt - 1)
                    m = PE.sig(ins)
                    freed[b] = evac(i, u, m)
                if not peeled:
                    ACTE.need(m)
                    round_hi(p, c + 2, None if n_pairs == 1 or unroll else i, 2) if not unroll else \
                        round_hi(p, c + 2 + 2 * i)
            return freed

        before = {b: (ACTE.now(), DVE.now()) for b in range(4)}
        if n_pairs == 1 or unroll:
            for i in range(n_pairs):
                before = body(i, peeled=last and i == n_pairs - 1)
        else:
            n_loop = n_pairs - 1 if last else n_pairs
            before = {b: (ACTE.now(), DVE.now()) for b in range(4)}
            with loop(n_loop, pe=outs, act=per[0], dve=per[1]) as i:
                a0, d0 = ACTE.now(), DVE.now()
                before = {b: (a0, d0) for b in range(4)}
                body(i)
            if last:
                before = {b: (ACTE.now(), DVE.now()) for b in range(4)}
                body_i = n_loop
                body(body_i, peeled=True)
        chunk[0] += 2 * n_pairs

    def gemm_tokens(n_pairs, lhs, dst, col_of, after=(), width=CHUNK_COLS):
        base_chunk = chunk[0]
        for e in after:
            PE.need(e)
        nblk = len(lhs)
        assert nblk * 2 <= 16
        with loop(n_pairs, pe=2 * nblk, act=2 * (nblk // 2), dve=2 * (nblk - nblk // 2)) as i:
            a0, d0 = ACTE.now(), DVE.now()
            freed = {b: (a0, d0) for b in range(8)}
            for p in range(2):
                PE.e.wait_ge(lo_done, base_chunk + p + 1 + 2 * i)
                hi = whi[p][:].rearrange("p (k n) -> p k n", k=DT)
                lo = wlo[p][:].rearrange("p (k n) -> p k n", k=DT)
                for n, (xh, xl, blk) in enumerate(lhs):
                    b = (p * nblk + n) % 8
                    PE.need(*freed[b])
                    ts = slice(blk * P, (blk + 1) * P)
                    for k in range(DT):
                        ins = mm3(bank(b, width), hi[:, k, :], lo[:, k, :], xh[:, k, ts], xl[:, k, ts],
                                  k == 0, k == DT - 1, flip=True)
                    m = PE.sig(ins)
                    out = dst[:, n, bass.ds(col_of(i, p), width)]
                    if n % 2:
                        ACTE.need(m)
                        freed[b] = (act(out, bank(b, width)),)
                    else:
                        DVE.need(m)
                        freed[b] = (DVE.sig(nc.vector.tensor_copy(out, bank(b, width))),)
                ACTE.need(m)
                round_hi(p, base_chunk + p + 2, i, 2)
        chunk[0] += 2 * n_pairs

    w_in = a["w_in"][0]
    stream(a["w_mem_kv"][0], [0, 256], 512, 2)
    stream(w_in, [3584, 3840])
    stream(w_in, [3072, 3328])
    stream(w_in, [6144, 6400], 512, 2)
    stream(a["w_mem_branch"][0], [0, 512], rows_=(0, 512), width=512)
    stream(w_in, [5120, 5376], 512, 2)
    stream(a["w_pool_branch"][0], [0, 512], rows_=(0, 512), width=512)
    stream(w_in, [0, 256], 512, 6)
    stream(w_in, [4096, 4352], 512, 2)
    stream(a["w_attn_branch"][0], [0, 256], 512, 2)
    stream(a["w_out"][0], [0, 256], 512, 2)
    stream(a["w_up"][0], [0, D_FF], 256, D_FF // 256)
    stream_down(a["w_down"][0])
    ev = a["ev_w_in_2"][0]
    stream(ev, [0, 256], 1280, 2)
    stream(ev, [512, 1792])
    stream(ev, [768, 1024])
    stream(ev, [2048, 2304])
    stream(a["ev_w_out_2"][0], [0, 256], 512, 2)
    od = a["od_w_in_2"][0]
    stream(od, [0, 512], 256, 2)
    stream(od, [1536, 1792])
    stream(od, [2048, 2304])
    stream(od, [2560, 2816])
    stream(od, [1024, 1280])
    stream(od, [3072, 3328])
    stream(a["od_w_out_2"][0], [0, 256], 512, 2)

    with nc.Fori(0, sent[0] // 2, engines=[nc.gpsimd.engine]) as i:
        for p in range(2):
            nc.gpsimd.wait_ge(hi_done, 2 * i + p + 1)
            nc.gpsimd.tensor_tensor(wlo[p][:], raw[p][:], f(whi[p][:]), ALU.subtract).then_inc(lo_done, 1)

    for p in range(2):
        round_hi(p, p)

    def col_stats(src_of, n_tiles, tokens, sq, after, bank_=7, dim=D_MODEL):
        nb = tokens // P
        used = [None, None]
        PE.need(*after)
        ACTE.need(*after)
        for t in range(n_tiles):
            ACTE.need(used[t % 2])
            m = act(sq[t % 2][:, 0:tokens], src_of(t), ACT.Square)
            PE.need(m)
            for b in range(nb):
                ins = nc.tensor.matmul(bank(bank_, 1, b), sq[t % 2][:, b * P:(b + 1) * P], ones[:, 0:1],
                                       start=t == 0 and b == 0, stop=t == n_tiles - 1, skip_group_check=True)
            used[t % 2] = PE.sig(ins)
        ACTE.need(used[(n_tiles - 1) % 2])
        m = act(st[:, 0:nb], bank(bank_, nb), ACT.Sqrt, scale=1.0 / dim, bias=eps)
        DVE.need(m)
        nc.scalar.preload_act_table(ACT.Exp)
        return DVE.sig(nc.vector.reciprocal(st[:, 8:8 + nb], st[:, 0:nb]))

    def spread_cols(tokens, dg, m, bank_=6):
        nb = tokens // P
        DVE.need(m)
        for b in range(nb):
            m = DVE.sig(nc.vector.tensor_scalar(dg[:, b * P:(b + 1) * P], ident[:], st[:, 8 + b:9 + b], None, ALU.mult))
        PE.need(m)
        return PE.sig(nc.tensor.matmul(bank(bank_, tokens), ones[:], dg[:, 0:tokens]))

    def norm_split(src, tokens, hi, lo, gain_of, work, after, shift_of=None):
        sq = [work("sq0_" + hi.name, [P, SEQ]), work("sq1_" + hi.name, [P, SEQ])]
        dg = work("dg_" + hi.name, [P, SEQ])
        tmp = [work("nt0_" + hi.name, [P, SEQ]), work("nt1_" + hi.name, [P, SEQ])]
        m = col_stats(lambda t: src[:, t, :], DT, tokens, sq, after)
        m = spread_cols(tokens, dg, m)
        free = [None, None]
        for t in range(DT):
            w = tmp[t % 2][:, 0:tokens]
            DVE.need(m if t == 0 else None, free[t % 2])
            g = DVE.sig(nc.vector.scalar_tensor_tensor(w, src[:, t, :], gain_of(t), bank(6, tokens), ALU.mult, ALU.mult))
            if shift_of is not None:
                DVE.need(g)
                g = DVE.sig(nc.vector.tensor_scalar(w, w, shift_of(t), None, ALU.add))
            ACTE.need(g)
            m2 = act(hi[:, t, 0:tokens], w)
            DVE.need(m2)
            free[t % 2] = DVE.sig(nc.vector.tensor_tensor(lo[:, t, 0:tokens], w, f(hi[:, t, 0:tokens]), ALU.subtract))
        return ACTE.now(), DVE.now()

    def split(hi_ap, lo_ap, src, m, src_is_act=False):
        ACTE.need(m)
        g = act(hi_ap, src)
        DVE.need(g)
        return g, DVE.sig(nc.vector.tensor_tensor(lo_ap, src, f(hi_ap), ALU.subtract))

    nwork = region(put_end + 256)
    h_ready = norm_split(xT, SEQ, hhi, hlo, lambda t: col("norm_mix_pre", t), region(R0), (*x_ready, mod_ready, mod_done))
    m_ready = norm_split(memT, MEM, chi, clo, lambda t: col("norm_mem", t),
                         region(R0 + 5 * 2048), h_ready)

    put = region(R0)
    mixT = put("mix_T", [P, DT, SEQ])
    gate = put("gate", [P, DT, SEQ])
    kmT = put("km_T", [P, MEM_HEADS, MEM])
    vm = put("vm", [P, CB, MEM_HEADS * P])
    qmT = put("qm_T", [P, MEM_HEADS, SEQ])
    upT = put("up_T", [P, 4, POOL_PAD + SEQ])
    om = put("om", [P, NB, MEM_HEADS * P])
    bhi, blo = put("b_hi", [P, 4, SEQ], F32R), put("b_lo", [P, 4, SEQ], F32R)
    pre_end = put.end
    assert pre_end <= R_END, (pre_end, R_END)

    def evac_copy(dst_of, **kw):
        def ev_(i, u, m):
            if u % 2:
                ACTE.need(m)
                return (act(dst_of(i, u), bank(u % 4, dst_of.n), **kw),)
            DVE.need(m)
            s = kw.get("scale")
            if s is None:
                return (DVE.sig(nc.vector.tensor_copy(dst_of(i, u), bank(u % 4, dst_of.n))),)
            return (DVE.sig(nc.vector.tensor_scalar(dst_of(i, u), bank(u % 4, dst_of.n), s, None, ALU.mult)),)
        return ev_

    def dest(t, n, lo_=0):
        def of(i, u):
            j = 4 * i + u
            if isinstance(j, int):
                return t[:, j, lo_:lo_ + n]
            return t[:, bass.ds(j, 1), lo_:lo_ + n].rearrange("p a n -> p (a n)")
        of.n = n
        return of

    X = [(hhi, hlo, SEQ)]
    C = [(chi, clo, CTX)]
    XC = X + C
    gemm(1, C, evac_copy(dest(kmT, MEM)), after=m_ready)
    gemm_tokens(1, [(chi, clo, b) for b in range(CB)], vm, lambda i, p: p * 256)
    gemm(1, X, evac_copy(dest(qmT, SEQ), scale=P ** -0.5), after=h_ready)
    gemm(1, X, evac_copy(dest(upT, SEQ, POOL_PAD)))
    m_proj = (ACTE.now(), DVE.now())

    class Attention:

        def __init__(self, probs, probsT, scale=1.0):
            self.probs, self.probsT, self.scale = probs, probsT, scale
            self.exp, self.out, self.tcopy = {}, {}, {}

        def run(self, units, after=(), tail=()):
            n = len(units)
            PE.need(*after)
            for s in range(n + 2):
                if s < n:
                    self.scores(s, units[s])
                if 0 <= s - 1 < n:
                    self.softmax(s - 1, units[s - 1])
                if 0 <= s - 2 < n:
                    self.values(s - 2, units[s - 2])

        def scores(self, s, u):
            PE.need(self.exp.get(s - 2))
            b = 2 * (s % 2)
            for off, n, q, k in u["scores"]:
                ins = nc.tensor.matmul(ps[:, b * 512 + off:b * 512 + off + n], q, k)
            u["m"] = PE.sig(ins)

        def softmax(self, s, u):
            b, n = 2 * (s % 2), u["n"]
            S = ps[:, b * 512:b * 512 + n]
            mx, sm_, r = (sm[:, 8 * (s % 2) + j:8 * (s % 2) + j + 1] for j in range(3))
            es = sm[:, 8 * (s % 2) + 3:8 * (s % 2) + 4]
            DVE.need(u["m"])
            for off, w, bias in u.get("bias", ()):
                dst = ps[:, b * 512 + off:b * 512 + off + w]
                DVE.need(DVE.sig(nc.vector.tensor_tensor(dst, dst, bias, ALU.add)))
            DVE.need(self.exp.get(s - 2), self.out.get(s - 2))
            m = DVE.sig(nc.vector.tensor_reduce(mx, S, AX, ALU.max, negate=True))
            if self.scale != 1.0:
                DVE.need(m)
                m = DVE.sig(nc.vector.tensor_scalar(mx, mx, self.scale, None, ALU.mult))
            if "sink" in u:
                DVE.need(m)
                m = DVE.sig(nc.vector.tensor_tensor(mx, mx, u["nsink"], ALU.min))
            ACTE.need(m, self.tcopy.get(("pe", s - 2)))
            self.exp[s] = act(self.probs[s % 2][:, 0:n], S, ACT.Exp, bias=mx, scale=self.scale, accum_out=sm_)
            if "sink" in u:
                self.exp[s] = act(es, u["sink"], ACT.Exp, bias=mx)
            DVE.need(self.exp[s])
            if "sink" in u:
                DVE.need(DVE.sig(nc.vector.tensor_tensor(sm_, sm_, es, ALU.add)))
            u["r"] = DVE.sig(nc.vector.reciprocal(r, sm_))

        def values(self, s, u):
            n, nb = u["n"], u["n"] // P
            PE.need(self.exp[s], *self.tcopy.get("copied", ()))
            h = (nb + 1) // 2
            for k in range(nb):
                ins = nc.tensor.transpose(bank(4, P, k * P) if k < h else bank(5, P, (k - h) * P),
                                          self.probs[s % 2][:, k * P:(k + 1) * P], ident[:])
            m = PE.sig(ins)
            self.tcopy[("pe", s)] = m
            T = self.probsT[s % 2]
            half = h * P
            DVE.need(m, self.tcopy.get(("pv", s - 2)))
            d = DVE.sig(nc.vector.tensor_copy(T[:, 0:half], bank(4, half)))
            c = None
            if half < n:
                ACTE.need(m, self.tcopy.get(("pv", s - 2)))
                c = act(T[:, half:n], bank(5, n - half))
            self.tcopy["copied"] = (d, c)
            PE.need(d, c, self.out.get(s - 2))
            w = u["dh"]
            for k in range(nb):
                ins = nc.tensor.matmul(bank(6 + s % 2, w), T[:, k * P:(k + 1) * P], u["values"][k],
                                       start=k == 0, stop=k == nb - 1)
            m = PE.sig(ins)
            self.tcopy[("pv", s)] = m
            DVE.need(m, u["r"])
            r = sm[:, 8 * (s % 2) + 2:8 * (s % 2) + 3]
            self.out[s] = DVE.sig(nc.vector.tensor_scalar(u["out"], bank(6 + s % 2, w), r, None, ALU.mult))

    awork = region(C0)
    probs = [awork(f"probs{n}", [P, ALL]) for n in range(2)]
    probsT = [awork(f"probsT{n}", [P, ALL]) for n in range(2)]
    qs = awork("q_staged", [P, ALL])
    assert awork.end <= C0 + 16384

    def dyn(t, j, sl):
        return t[:, bass.ds(j, 1), sl].rearrange("p a n -> p (a n)")

    c_mem = [PE.n, ACTE.n, DVE.n]
    PE.need(*m_proj)
    DVE.need(*m_proj)
    ACTE.need(*m_proj, PE.now())
    n_u = NB
    with loop(MEM_HEADS, pe=3 * n_u, act=2 * n_u, dve=1 + 4 * n_u) as h:
        DVE.need(PE.now())
        m = DVE.sig(nc.vector.tensor_copy(qs[:, 0:SEQ], dyn(qmT, h, slice(0, SEQ))))
        PE.need(m, ACTE.now())
        att = Attention(probs, probsT)
        att.run([dict(scores=[(0, MEM, qs[:, i * P:(i + 1) * P], dyn(kmT, h, slice(0, MEM)))], n=MEM, dh=P,
                      values=[vm[:, k, bass.ds(h * P, P)] for k in range(CB)],
                      out=om[:, i, bass.ds(h * P, P)]) for i in range(NB)])
    att_done = (ACTE.now(), DVE.now(), PE.now())

    def token_to_split(src, n_tiles, nb, hi, lo, after, gain=None, tile0=0):
        PE.need(*after)
        ACTE.need(*after)
        DVE.need(*after)
        freed = {}
        for t in range(n_tiles):
            b = t % 4
            PE.need(*freed.get(b, ()))
            for k in range(nb):
                ins = nc.tensor.transpose(bank(b, P, k * P), src[:, k, t * P:(t + 1) * P], ident[:])
            m = PE.sig(ins)
            ACTE.need(m)
            g = act(hi[:, t, :], bank(b, nb * P), scale=1.0) if gain is None else \
                act(hi[:, t, :], bank(b, nb * P), ACT.Identity, scale=gain, bias=zero1)
            DVE.need(g)
            if gain is None:
                d = DVE.sig(nc.vector.tensor_tensor(lo[:, t, :], bank(b, nb * P), f(hi[:, t, :]), ALU.subtract))
            else:
                d = DVE.sig(nc.vector.scalar_tensor_tensor(lo[:, t, :], bank(b, nb * P), gain, f(hi[:, t, :]),
                                                           ALU.mult, ALU.subtract))
            freed[b] = (g, d)
        return ACTE.now(), DVE.now()

    def evac_gate(i, u, m):
        ACTE.need(m)
        return (act(dest(gate, SEQ)(i, u), bank(u % 4), ACT.Tanh, scale=0.5),)

    gtmp = [region(C0)("gtmp0", [P, SEQ]), region(C0 + 2048)("gtmp1", [P, SEQ])]

    def evac_branch(first, tiles=4):
        def ev_(i, u, m):
            j = tiles * i + u
            g, x_ = (gate[:, j, :], mixT[:, j, :]) if isinstance(j, int) else \
                (dyn(gate, j, slice(0, SEQ)), dyn(mixT, j, slice(0, SEQ)))
            DVE.need(m)
            m2 = DVE.sig(nc.vector.scalar_tensor_tensor(gtmp[u % 2][:], g, 1.0, bank(u % 4), ALU.add, ALU.mult))
            DVE.need(m2)
            if first:
                DVE.sig(nc.vector.tensor_scalar(x_, gtmp[u % 2][:], 0.5, None, ALU.mult))
            else:
                DVE.sig(nc.vector.scalar_tensor_tensor(x_, gtmp[u % 2][:], 0.5, x_, ALU.mult, ALU.add))
            return (m2,)
        return ev_

    om_ready = token_to_split(om, MEM_HEADS, NB, bhi, blo, att_done)
    gemm(2, X, evac_gate, per=(4, 0), after=om_ready)
    PE.need(*om_ready)
    DVE.need(ACTE.now())
    gemm(1, [(bhi, blo, SEQ)], evac_branch(True), kt=4, cols_=512, after=(ACTE.now(), DVE.now()))
    mem_branch = (PE.now(), DVE.now())

    poolw = region(C0 + 4096)
    pw = poolw("pool_w", [P, 4, P])
    edge = poolw("pool_edge", [P, 4, POOL_PAD])
    s1 = poolw("pool_s1", [P, POOL_PAD + SEQ])
    s2 = poolw("pool_s2", [P, POOL_PAD + SEQ])
    nc.scalar.wait_ge(PE.sem, mem_branch[0].value())
    nc.scalar.wait_ge(DVE.sem, mem_branch[1].value())
    load(nc.scalar, pw[:], a["pool_w"][0].rearrange("g c d -> c g d"))
    load(nc.scalar, edge[:], a["t_pool_edge"].rearrange("p (g n) -> p g n", g=4))
    DVE.need(*mem_branch)
    DVE.sig(nc.vector.memset(upT[:, :, 0:POOL_PAD], 0.0))
    DVE.sig(nc.vector.memset(s1[:, 0:POOL_PAD], 0.0))
    DVE.need(DVE.sig(nc.vector.memset(s2[:, 0:POOL_PAD], 0.0)))
    need_inputs(DVE, PE)
    for g, w in enumerate(POOL_WINDOWS):
        cur, sh, n = upT[:, g, :], 1, 0
        while sh < w:
            nxt = (s1, s2)[n % 2]
            DVE.need(DVE.sig(nc.vector.tensor_tensor(nxt[:, POOL_PAD:], cur[:, POOL_PAD:],
                                                     cur[:, POOL_PAD - sh:POOL_PAD + SEQ - sh], ALU.add)))
            cur, sh, n = nxt, 2 * sh, n + 1
        DVE.need(DVE.sig(nc.vector.tensor_tensor(cur[:, POOL_PAD:2 * POOL_PAD], cur[:, POOL_PAD:2 * POOL_PAD],
                                                 edge[:, g, :], ALU.mult)))
        m = DVE.sig(nc.vector.scalar_tensor_tensor(upT[:, g, POOL_PAD:], cur[:, POOL_PAD:], 1.0 / w,
                                                   upT[:, g, POOL_PAD:], ALU.mult, ALU.subtract))
        DVE.need(m)
        PE.need(m)
        m = PE.sig(nc.tensor.matmul(bank(g), pw[:, g, :], upT[:, g, POOL_PAD:]))
        ACTE.need(m)
        sc = col("pool_scale", g)
        m = act(bhi[:, g, :], bank(g), ACT.Identity, scale=sc, bias=zero1)
        DVE.need(m)
        DVE.sig(nc.vector.scalar_tensor_tensor(blo[:, g, :], bank(g), sc, f(bhi[:, g, :]), ALU.mult, ALU.subtract))
    pool_ready = (ACTE.now(), DVE.now())
    ACTE.need(DVE.now())
    gemm(2, X, evac_gate, per=(4, 0), after=pool_ready)
    DVE.need(ACTE.now())
    gemm(1, [(bhi, blo, SEQ)], evac_branch(False), kt=4, cols_=512, after=(ACTE.now(), DVE.now()))

    put = region(R0 + 16384)
    qT = put("q_T", [P, DIFF_HEADS, SEQ])
    kT = put("k_T", [P, DIFF_HEADS, SEQ])
    vt = put("v_tok", [P, NB, D_MODEL])
    ao = put("attn_tok", [P, NB, D_MODEL])
    work = put
    m = (PE.now(), ACTE.now(), DVE.now())
    ACTE.need(*m)
    DVE.need(*m)
    gemm(2, X, evac_copy(dest(qT, SEQ), scale=DIFF_DH ** -0.5), per=(2, 2), after=m)
    gemm(2, X, evac_copy(dest(kT, SEQ)), per=(2, 2))
    gemm_tokens(2, [(hhi, hlo, b) for b in range(NB)], vt, lambda i, p: i * 512 + p * 256, after=m)
    m = (PE.now(), ACTE.now(), DVE.now())
    for x_ in (PE, ACTE, DVE):
        x_.need(*m)
    awork = region(C0)
    sc2 = [awork(f"diff_s{n}", [P, 2, SEQ]) for n in range(2)]
    aT = [awork(f"diff_aT{n}", [P, SEQ]) for n in range(2)]
    ks = awork("k_staged", [P, SEQ])
    qs2 = awork("q2_staged", [P, SEQ])
    dist = work("distance", [P, SEQ])
    assert work.end <= R_END, work.end
    load(nc.scalar, dist[:], a["t_distance"])
    need_inputs(DVE)

    with loop(DIFF_HEADS, pe=3 * NB, act=3 * NB, dve=2 + 8 * NB) as h:
        DVE.need(PE.now())
        DVE.sig(nc.vector.tensor_copy(qs2[:], dyn(qT, h, slice(0, SEQ))))
        m = DVE.sig(nc.vector.tensor_copy(ks[:], dyn(kT, h, slice(0, SEQ))))
        PE.need(m, ACTE.now())
        biased, expd, comb, tdone, pvd, copied, outd, scored = {}, {}, {}, {}, {}, {}, {}, {}

        def scores(i):
            n, b = (i + 1) * P, 2 * (i % 2)
            PE.need(biased.get(i - 2))
            for c in range(2):
                part = slice(c * DIFF_DH, (c + 1) * DIFF_DH)
                ins = nc.tensor.matmul(bank(b + c, n), qs2[part, i * P:(i + 1) * P], ks[part, 0:n])
            scored[i] = PE.sig(ins)

        def softmax(i):
            n, b, S = (i + 1) * P, 2 * (i % 2), sc2[i % 2]
            st_ = sm[:, 8 * (i % 2):8 * (i % 2) + 8]
            DVE.need(scored[i], tdone.get(i - 2), comb.get(i - 2))
            for c in range(2):
                m = DVE.sig(nc.vector.scalar_tensor_tensor(
                    S[:, c, 0:n], dist[:, SEQ - n:SEQ] if i == NB - 1 else dist[:, (NB - 1 - i) * P:(NB - 1 - i) * P + n],
                    slopes[:, bass.ds(h, 1)], bank(b + c, n), ALU.mult, ALU.add))
            biased[i] = m
            DVE.need(m)
            m = DVE.sig(nc.vector.tensor_reduce(st_[:, 0:2], S[:, :, 0:n], AX, ALU.max, negate=True))
            ACTE.need(m)
            for c in range(2):
                m = act(S[:, c, 0:n], S[:, c, 0:n], ACT.Exp, bias=st_[:, c:c + 1], accum_out=st_[:, 2 + c:3 + c])
            DVE.need(m)
            m = DVE.sig(nc.vector.reciprocal(st_[:, 4:6], st_[:, 2:4]))
            DVE.need(m)
            DVE.sig(nc.vector.tensor_scalar(S[:, 0, 0:n], S[:, 0, 0:n], st_[:, 4:5], None, ALU.mult))
            m = DVE.sig(nc.vector.tensor_scalar(st_[:, 5:6], st_[:, 5:6], nlam, None, ALU.mult))
            DVE.need(m)
            comb[i] = DVE.sig(nc.vector.scalar_tensor_tensor(S[:, 0, 0:n], S[:, 1, 0:n], st_[:, 5:6], S[:, 0, 0:n],
                                                             ALU.mult, ALU.add))

        def values(i):
            n, S = (i + 1) * P, sc2[i % 2]
            PE.need(comb[i], copied.get(i - 1))
            for k in range(i + 1):
                ins = nc.tensor.transpose(bank(4, P, k * P), S[:, 0, k * P:(k + 1) * P], ident[:])
            tdone[i] = PE.sig(ins)
            ACTE.need(tdone[i], pvd.get(i - 2))
            copied[i] = act(aT[i % 2][:, 0:n], bank(4, n))
            PE.need(copied[i], outd.get(i - 2))
            for k in range(i + 1):
                ins = nc.tensor.matmul(bank(6 + i % 2, P), aT[i % 2][:, k * P:(k + 1) * P], vt[:, k, bass.ds(h * P, P)],
                                       start=k == 0, stop=k == i)
            pvd[i] = PE.sig(ins)
            DVE.need(pvd[i])
            outd[i] = DVE.sig(nc.vector.tensor_copy(ao[:, i, bass.ds(h * P, P)], bank(6 + i % 2, P)))

        for s in range(NB + 2):
            if s < NB:
                scores(s)
            if 0 <= s - 1 < NB:
                softmax(s - 1)
            if 0 <= s - 2 < NB:
                values(s - 2)
    m = DVE.now()
    DVE.need(m, PE.now(), ACTE.now())
    sqt = qT[:]
    ao_h = ao[:].rearrange("p b (h d) -> p (b h) d", h=DIFF_HEADS)
    DVE.need(DVE.sig(nc.vector.tensor_tensor(qT[:].rearrange("p h n -> p (h n)"), ao[:].rearrange("p b n -> p (b n)"),
                                             ao[:].rearrange("p b n -> p (b n)"), ALU.mult)))
    hs = small[:, 96:128]
    m = DVE.sig(nc.vector.tensor_reduce(hs, qT[:].rearrange("p h (b d) -> p (h b) d", d=P), AX, ALU.add))
    ACTE.need(m)
    m = act(small[:, 128:160], hs, ACT.Sqrt, scale=1.0 / P, bias=eps)
    nc.scalar.preload_act_table(ACT.Exp)
    DVE.need(m)
    DVE.need(DVE.sig(nc.vector.reciprocal(hs, small[:, 128:160])))
    m = DVE.sig(nc.vector.tensor_tensor(ao_h, ao_h, hs.unsqueeze(2).to_broadcast([P, NB * DIFF_HEADS, P])
                                        if hasattr(hs, "to_broadcast") else
                                        bass.AP(tensor=hs.tensor, offset=hs.offset, ap=[*hs.ap, [0, P]]), ALU.mult))
    put = region(R0 + 16384)
    ahi, alo = put("a_hi", [P, DT, SEQ], F32R), put("a_lo", [P, DT, SEQ], F32R)
    a_ready = token_to_split(ao, DT, NB, ahi, alo, (m, ACTE.now()), gain=subg)
    gate = region(R0 + 16384 + 2 * 16384)("gate_attn", [P, DT, SEQ])
    gemm(2, X, evac_gate, per=(4, 0), after=a_ready)
    DVE.need(ACTE.now())
    gemm(2, [(ahi, alo, SEQ)], evac_branch(False), per=(0, 8), after=(ACTE.now(), DVE.now()))
    m = (PE.now(), ACTE.now(), DVE.now())

    def split_tiles(src, hi, lo, n, after):
        ACTE.need(*after)
        DVE.need(*after)
        for t in range(n):
            split(hi[:, t, :], lo[:, t, :], src[:, t, :], None)
        return ACTE.now(), DVE.now()

    def add_normed(y, gain_name, after, tag):
        w = region(C0)
        sq = [w(f"sq{n}{tag}", [P, SEQ]) for n in range(2)]
        dg = w("dg" + tag, [P, SEQ])
        tmp = [w(f"t{n}{tag}", [P, SEQ]) for n in range(2)]
        m = col_stats(lambda t: y[:, t, :], DT, SEQ, sq, after)
        m = spread_cols(SEQ, dg, m)
        DVE.need(m)
        for t in range(DT):
            DVE.need(DVE.sig(nc.vector.scalar_tensor_tensor(tmp[t % 2][:], y[:, t, :], col(gain_name, t), bank(6),
                                                            ALU.mult, ALU.mult)))
            m = DVE.sig(nc.vector.tensor_tensor(xT[:, t, :], xT[:, t, :], tmp[t % 2][:], ALU.add))
        return m

    mx_ready = split_tiles(mixT, ahi, alo, DT, m)
    yT = region(R0)("y_T", [P, DT, SEQ])
    PE.need(*mx_ready)
    ACTE.need(*mx_ready)
    gemm(2, [(ahi, alo, SEQ)], evac_copy(dest(yT, SEQ)), per=(2, 2), after=mx_ready)
    m = add_normed(yT, "norm_mix_post", (PE.now(), ACTE.now(), DVE.now()), "_mix")

    h2 = norm_split(xT, SEQ, hhi, hlo, lambda t: col("norm_ffn_pre", t), region(R0 + 20480), (m, PE.now(), ACTE.now()))
    put = region(R0)
    fhi, flo = put("f_hi", [P, FT, SEQ], F32R), put("f_lo", [P, FT, SEQ], F32R)
    assert put.end <= R_END, (put.end, R_END)
    cw = region(C0)
    cbuf = [cw(f"conv{n}", [P, SEQ]) for n in range(4)]
    gel = [cw(f"gel{n}", [P, SEQ]) for n in range(2)]
    for x_ in (PE, ACTE, DVE):
        x_.need(*h2)
    nc.scalar.preload_act_table(ACT.Gelu_apprx_tanh)

    conv_marks = {}

    def evac_ffn(i, u, m):
        t = 2 * i + u % 2 + (FT if u >= 2 else 0)
        w = cbuf[u]
        ACTE.need(m, *conv_marks["before"])
        g = act(w[:], bank(u), ACT.Identity, scale=dyn_col("conv_w", t + 2 * 2 * FT), bias=dyn_col("conv_b", t))
        DVE.need(g)
        g = DVE.sig(nc.vector.scalar_tensor_tensor(w[:, 1:], bank(u, SEQ - 1), dyn_col("conv_w", t + 2 * FT), w[:, 1:],
                                                   ALU.mult, ALU.add))
        DVE.need(g)
        g = DVE.sig(nc.vector.scalar_tensor_tensor(w[:, 2:], bank(u, SEQ - 2), dyn_col("conv_w", t), w[:, 2:],
                                                   ALU.mult, ALU.add))
        if u < 2:
            ACTE.need(g)
            conv_marks[u] = act(gel[u][:], w[:], ACT.Gelu_apprx_tanh)
            return (g,)
        DVE.need(g, conv_marks[u - 2])
        p_ = DVE.sig(nc.vector.tensor_tensor(w[:], w[:], gel[u - 2][:], ALU.mult))
        j = 2 * i + (u - 2)
        ACTE.need(p_)
        q_ = act(dyn(fhi, j, slice(0, SEQ)), w[:])
        DVE.need(q_)
        DVE.sig(nc.vector.tensor_tensor(dyn(flo, j, slice(0, SEQ)), w[:], f(dyn(fhi, j, slice(0, SEQ))), ALU.subtract))
        return (g,)

    base_chunk = chunk[0]
    with loop(D_FF // 256, pe=4, act=8, dve=12) as i:
        conv_marks["before"] = (DVE.now(),)
        before = (ACTE.now(), DVE.now())
        for p in range(2):
            PE.e.wait_ge(lo_done, base_chunk + p + 1 + 2 * i)
            hi = whi[p][:].rearrange("p (k n) -> p k n", k=DT)
            lo = wlo[p][:].rearrange("p (k n) -> p k n", k=DT)
            for o in range(2):
                if p == 0 and o == 0:
                    PE.need(*before)
                for k in range(DT):
                    ins = mm3(bank(2 * p + o), hi[:, k, o * P:(o + 1) * P], lo[:, k, o * P:(o + 1) * P],
                              hhi[:, k, :], hlo[:, k, :], k == 0, k == DT - 1)
                m = PE.sig(ins)
                evac_ffn(i, 2 * p + o, m)
            ACTE.need(m)
            round_hi(p, base_chunk + p + 2, i, 2)
    chunk[0] += D_FF // 128
    nc.scalar.preload_act_table(ACT.Exp)

    yT = hlo
    ydn = nc.alloc_sbuf_tensor_at("y_down", [P, DT, SEQ], F32, offset=C0 - 2 * 16384)
    m = (PE.now(), ACTE.now(), DVE.now())
    for x_ in (PE, ACTE, DVE):
        x_.need(*m)
    base_chunk = chunk[0]
    with loop(2, pe=6, act=2, dve=2) as i:
        before = (ACTE.now(), DVE.now())
        PE.need(*before)
        for q in range(6):
            g, kk = divmod(q, 3)
            p = q % 2
            kt = min(8, FT - 8 * kk)
            PE.e.wait_ge(lo_done, base_chunk + q + 1 + 6 * i)
            hi = whi[p][:, 0:kt * 256].rearrange("p (k n) -> p k n", k=kt)
            lo = wlo[p][:, 0:kt * 256].rearrange("p (k n) -> p k n", k=kt)
            for o in range(2):
                for k in range(kt):
                    kf = 8 * kk + k
                    ins = mm3(bank(2 * g + o), hi[:, k, o * P:(o + 1) * P], lo[:, k, o * P:(o + 1) * P],
                              fhi[:, kf, :], flo[:, kf, :], kf == 0, kf == FT - 1)
            m = PE.sig(ins)
            ACTE.need(m)
            round_hi(p, base_chunk + q + 2, i, 6)
            if kk == 2:
                for o in range(2):
                    dst = dyn(ydn, 4 * i + 2 * g + o, slice(0, SEQ))
                    if o:
                        act(dst, bank(2 * g + o))
                    else:
                        DVE.need(m)
                        DVE.sig(nc.vector.tensor_copy(dst, bank(2 * g + o)))
    chunk[0] += 12
    m = add_normed(ydn, "norm_ffn_post", (PE.now(), ACTE.now(), DVE.now()), "_ffn")
    x1_ready = (m, PE.now(), ACTE.now())

    put = region(R0)
    cT = put("ctx_T", [P, DT, CTX])
    k3 = {}
    qT3 = {x_: put(f"q_{x_}", [P, 4, ALL]) for x_ in "AB"}
    kk_ = {x_: put(f"k_{x_}", [P, ALL]) for x_ in "AB"}
    kd = {x_: put(f"kd_{x_}", [P, 2, ALL]) for x_ in "AB"}
    v3 = {x_: put(f"v_{x_}", [P, ALL // P, P]) for x_ in "AB"}
    ao2 = put("attn2_tok", [P, ALL // P, D_MODEL])
    rest = put.end
    assert rest <= R_END, (rest, R_END)
    cin = region(rest - 4 * 6 * D_MODEL)("ctx_in", [P, CB, D_MODEL])
    for x_ in (PE, ACTE, DVE):
        x_.need(*x1_ready)
    nc.scalar.wait_ge(PE.sem, PE.n)
    load(nc.scalar, cin[:], a["ctx_2"][0].rearrange("(b p) d -> p b d", p=P))
    need_inputs(PE)
    c_ready = to_feature_major(cin, CB, cT, x1_ready)

    gs = nc.alloc_sbuf_tensor_at("gain_scale", [P, 4, DT], F32, offset=(small_off := None) or base[0]) if False else None
    gsc = small[:, 160:192].rearrange("p (n t) -> p n t", n=4)

    def mod(layer, part, cond_):
        return modT[:, layer, part * DT:(part + 1) * DT, cond_]

    DVE.need(mod_ready)
    for layer in range(2):
        for cn in range(2):
            g0 = places["norm_g_2"] + layer * DT
            gm = DVE.sig(nc.vector.scalar_tensor_tensor(gsc[:, 2 * layer + cn, :], mod(layer, 1, cn), 1.0,
                                                        cols[:, g0:g0 + DT], ALU.add, ALU.mult))

    def modulated(layer, after, tag):
        hr = norm_split(xT, SEQ, hhi, hlo, lambda t: gsc[:, 2 * layer, t:t + 1], region(rest - 6 * 4096),
                        (*after, gm), lambda t: modT[:, layer, t, 0:1])
        cr = norm_split(cT, CTX, chi, clo, lambda t: gsc[:, 2 * layer + 1, t:t + 1], region(rest - 6 * 4096 + 10240),
                        hr, lambda t: modT[:, layer, t, 1:2])
        return (*hr, *cr, PE.now())

    hh = modulated(0, (*x1_ready, *c_ready), "0")
    for x_ in (PE, ACTE, DVE):
        x_.need(*hh)

    def evac_q2(i, u, m):
        raise NotImplementedError

    def evac_both(dst, scale):
        def ev_(i, u, m):
            ACTE.need(m)
            DVE.need(m)
            return (act(dst[:, u, CTX:], bank(u), scale=scale),
                    DVE.sig(nc.vector.tensor_scalar(dst[:, u, 0:CTX], bank(4 + u, CTX), scale, None, ALU.mult)))
        return ev_

    gemm(1, XC, evac_both(qT3["A"], 1.0), after=hh)
    m = (ACTE.now(), DVE.now())
    gemm(1, XC, evac_both(qT3["B"], HEAD ** -0.5), after=m)
    m = (ACTE.now(), DVE.now())
    PE.need(*m)
    kv_freed = m
    for p, x_ in enumerate("AB"):
        PE.e.wait_ge(lo_done, chunk[0] + p + 1)
        hi = whi[p][:].rearrange("p (k n) -> p k n", k=DT)
        lo = wlo[p][:].rearrange("p (k n) -> p k n", k=DT)
        for n, (xh, xl, tok) in enumerate(XC):
            for k in range(DT):
                ins = mm3(bank(4 * n, tok), hi[:, k, 0:P], lo[:, k, 0:P], xh[:, k, 0:tok], xl[:, k, 0:tok],
                          k == 0, k == DT - 1)
        blocks = [(chi, clo, b) for b in range(CB)] + [(hhi, hlo, b) for b in range(NB)]
        for n, (xh, xl, blk) in enumerate(blocks):
            ts = slice(blk * P, (blk + 1) * P)
            b = (1, 2, 3, 5, 6, 7)[n]
            for k in range(DT):
                ins = mm3(bank(b, P), hi[:, k, P:2 * P], lo[:, k, P:2 * P], xh[:, k, ts], xl[:, k, ts],
                          k == 0, k == DT - 1, flip=True)
        m = PE.sig(ins)
        ACTE.need(m)
        DVE.need(m)
        act(kk_[x_][:, CTX:], bank(0))
        DVE.sig(nc.vector.tensor_copy(kk_[x_][:, 0:CTX], bank(4, CTX)))
        for n in range(6):
            b = (1, 2, 3, 5, 6, 7)[n]
            if n % 2:
                act(v3[x_][:, n, :], bank(b, P))
            else:
                DVE.sig(nc.vector.tensor_copy(v3[x_][:, n, :], bank(b, P)))
        round_hi(p, chunk[0] + p + 2)
        PE.need(ACTE.now(), DVE.now())
    chunk[0] += 2

    t2 = region(rest - 6 * 4096)
    gat = t2("head_gather", [P, 5, 10])
    spr = t2("head_spread", [P, 5, P])
    rms10 = t2("rms10", [P, ALL])
    inv10 = t2("inv10", [P, ALL])
    sqa = [t2(f"sqa{n}", [P, ALL]) for n in range(2)]
    cosT = t2("cos_T", [P, SEQ])
    sinT = t2("sin_T", [P, SEQ])
    rotm = t2("rotate", [P, P])
    assert t2.end <= rest + 0, (t2.end, rest)
    nc.scalar.wait_ge(DVE.sem, DVE.n)
    nc.scalar.wait_ge(PE.sem, PE.n)
    load(nc.scalar, gat[:], a["t_head_gather"].rearrange("p (n c) -> p n c", n=5))
    load(nc.scalar, spr[:], a["t_head_spread"].rearrange("p (n c) -> p n c", n=5))
    load(nc.scalar, cosT[:], a["t_rope_cos"])
    load(nc.scalar, sinT[:], a["t_rope_sin"])
    load(nc.scalar, rotm[:], a["t_rotate"])
    need_inputs(PE, DVE)
    tiles = [qT3["A"][:, n, :] for n in range(4)] + [kk_["A"][:]]
    ACTE.need(DVE.now())
    used = {}
    for n, tl in enumerate(tiles):
        ACTE.need(used.get(n - 2))
        m = act(sqa[n % 2][:], tl, ACT.Square)
        PE.need(m)
        nc.tensor.matmul(bank(4, 512, 0, 10), gat[:, n, :], sqa[n % 2][:, 0:512], start=n == 0, stop=n == 4)
        used[n] = PE.sig(nc.tensor.matmul(bank(5, 256, 0, 10), gat[:, n, :], sqa[n % 2][:, 512:ALL],
                                          start=n == 0, stop=n == 4))
    ACTE.need(used[4])
    m = act(rms10[0:10, :], ps[0:10, 4 * 512:4 * 512 + ALL], ACT.Sqrt, bias=eps[0:10], scale=1.0)
    nc.scalar.preload_act_table(ACT.Exp)
    DVE.need(m)
    m = DVE.sig(nc.vector.reciprocal(inv10[0:10, :], rms10[0:10, :]))
    PE.need(m)
    fr = {}
    for n, tl in enumerate(tiles):
        b = 2 * (n % 2)
        PE.need(fr.get(n - 2))
        nc.tensor.matmul(bank(b), spr[0:10, n, :], inv10[0:10, 0:512])
        m = PE.sig(nc.tensor.matmul(bank(b + 1, 256), spr[0:10, n, :], inv10[0:10, 512:ALL]))
        DVE.need(m)
        gcol = qgain if n < 4 else col("a_k_gain_2")
        fr[n] = DVE.sig(nc.vector.scalar_tensor_tensor(tl, tl, gcol, ps[:, b * 512:b * 512 + ALL], ALU.mult, ALU.mult))
    tiles = tiles + [qT3["B"][:, n, :] for n in range(4)] + [kk_["B"][:]]
    PE.need(DVE.now(), ACTE.now())
    ACTE.need(PE.now())
    DVE.need(ACTE.now())
    fr = {}
    for n, tl in enumerate(tiles):
        b = n % 2
        s = tl[:, CTX:]
        PE.need(fr.get(n - 2))
        m = PE.sig(nc.tensor.matmul(bank(b), rotm[:], s))
        DVE.need(m)
        g = DVE.sig(nc.vector.tensor_tensor(sqa[n % 2][:, 0:SEQ], bank(b), sinT[:], ALU.mult))
        fr[n] = g
        DVE.need(DVE.sig(nc.vector.tensor_tensor(s, s, cosT[:], ALU.mult)), g)
        DVE.sig(nc.vector.tensor_tensor(s, s, sqa[n % 2][:, 0:SEQ], ALU.add))
    DVE.need(DVE.now())
    for x_ in "AB":
        for kv in range(2):
            for half in range(2):
                DVE.sig(nc.vector.tensor_copy(kd[x_][half * HEAD:(half + 1) * HEAD, kv, :],
                                              kk_[x_][kv * HEAD:(kv + 1) * HEAD, :]))
    m = (DVE.now(), ACTE.now(), PE.now())
    for x_ in (PE, ACTE, DVE):
        x_.need(*m)

    free_k = region(R0 + 8192 + 2 * 12288)
    probs2 = [free_k(f"probs2_{n}", [P, ALL]) for n in range(2)]
    tail = region(rest)
    probsT2 = [tail(f"probsT2_{n}", [P, ALL]) for n in range(2)]
    qst = tail("q3_staged", [P, ALL])
    bl, br = tail("band_left", [P, P]), tail("band_right", [P, P])
    assert tail.end <= R_END, tail.end - R_END
    nc.scalar.wait_ge(DVE.sem, DVE.n)
    load(nc.scalar, bl[:], a["t_band_left"])
    load(nc.scalar, br[:], a["t_band_right"])
    need_inputs(DVE)

    def q_units(x_, kv, j, s):
        part = slice(s * HEAD, (s + 1) * HEAD)
        K = kd[x_]
        us = []
        head = 4 * kv + 2 * j + s
        c0 = (0 if x_ == "A" else 512) + (2 * kv + j) * P + s * HEAD
        V = v3[x_]
        vs = slice(kv * HEAD, (kv + 1) * HEAD)
        extra = {} if x_ == "A" else dict(sink=sink[:, bass.ds(head, 1)], nsink=nsink[:, bass.ds(head, 1)])
        for i in range(NB):
            q = qst[part, CTX + i * P:CTX + (i + 1) * P]
            if x_ == "A":
                sc = [(0, 512, q, K[part, kv, 0:512]), (512, 256, q, K[part, kv, 512:ALL])]
                us.append(dict(scores=sc, n=ALL, values=[V[:, k, vs] for k in range(6)]))
            else:
                b0, b1 = max(i - 1, 0), min(i + 2, NB)
                w = (b1 - b0) * P
                k0 = CTX + b0 * P
                w1 = min(w, 256)
                sc = [(0, CTX, q, K[part, kv, 0:CTX]), (CTX, w1, q, K[part, kv, k0:k0 + w1])]
                if w > w1:
                    sc.append((CTX + w1, w - w1, q, K[part, kv, k0 + w1:k0 + w]))
                bias = []
                if i > 0:
                    bias.append((CTX, P, bl[:]))
                if i < NB - 1:
                    bias.append((CTX + w - P, P, br[:]))
                us.append(dict(scores=sc, n=CTX + w, bias=bias,
                               values=[V[:, k, vs] for k in (0, 1, *range(CB + b0, CB + b1))]))
            us[-1]["out"] = ao2[:, CB + i, bass.ds(c0, HEAD)]
        for i in range(CB):
            q = qst[part, i * P:(i + 1) * P]
            us.append(dict(scores=[(0, CTX, q, K[part, kv, 0:CTX])], n=CTX,
                           values=[V[:, k, vs] for k in range(CB)], out=ao2[:, i, bass.ds(c0, HEAD)]))
        for u_ in us:
            u_.update(dh=HEAD, **extra)
        return us

    for x_ in "AB":
        for kv in range(2):
            dummy_counts = dict(A=(36, 24, 1 + 12 * 4), B=(36, 36, 1 + 12 * 6 + 2 * 6))[x_]
            with loop(2, pe=dummy_counts[0], act=dummy_counts[1], dve=dummy_counts[2]) as j:
                DVE.need(PE.now())
                m = DVE.sig(nc.vector.tensor_copy(qst[:], dyn(qT3[x_], 2 * kv + j, slice(0, ALL))))
                PE.need(m, ACTE.now())
                DVE.need(m)
                Attention(probs2, probsT2).run(q_units(x_, kv, j, 0) + q_units(x_, kv, j, 1))
    m = (DVE.now(), ACTE.now(), PE.now())
    for x_ in (PE, ACTE, DVE):
        x_.need(*m)

    put = region(R0 + 8192)
    nmix = 4
    ghi, glo = put("g_hi", [P, DT, ALL], F32R), None
    gw = region(C0 if False else rest)
    silu_t = [gw(f"silu{n}", [P, ALL]) for n in range(2)]
    assert gw.end <= R_END
    glo_at = put.end
    glo = nc.alloc_sbuf_tensor_at("g_lo", [P, DT, ALL], F32R, offset=glo_at) if glo_at + 24576 <= rest - 24576 else None
    if glo is None:
        raise ValueError(f"g_lo: {glo_at + 24576 - (rest - 24576)} over")

    def gated(tile_base, n_blocks, ao_, xs, hi_, lo_, tile_of, silu_, prod_):
        tot = n_blocks * P
        for p in range(2):
            PE.e.wait_ge(lo_done, chunk[0] + p + 1)
            hi = whi[p][:].rearrange("p (k n) -> p k n", k=DT)
            lo = wlo[p][:].rearrange("p (k n) -> p k n", k=DT)
            for o in range(2):
                u = 2 * p + o
                t = tile_base + u
                b = 4 * (u % 2)
                PE.need(gf.get(u % 2))
                pos = 0
                for n, (xh, xl, tok) in enumerate(xs):
                    for k in range(DT):
                        ins = mm3(bank(b + n, tok), hi[:, k, o * P:(o + 1) * P], lo[:, k, o * P:(o + 1) * P],
                                  xh[:, k, 0:tok], xl[:, k, 0:tok], k == 0, k == DT - 1)
                for k in range(n_blocks):
                    c, off = (b + 3, k * P) if n_blocks > NB and k < CB else (b + 2, (k - (n_blocks - NB)) * P)
                    ins = nc.tensor.transpose(bank(c, P, off), ao_[:, k, t * P:(t + 1) * P], ident[:])
                m = PE.sig(ins)
                ACTE.need(m, gf.get(u % 2))
                parts = [(tot - SEQ, SEQ, b, b + 2)] + ([(0, CTX, b + 1, b + 3)] if tot > SEQ else [])
                S_, R_ = silu_[u % 2], prod_[u % 2]
                for off, n, gb, ab in parts:
                    g = act(S_[:, off:off + n], bank(gb, n), ACT.Tanh, scale=0.5)
                DVE.need(g)
                for off, n, gb, ab in parts:
                    g = DVE.sig(nc.vector.scalar_tensor_tensor(S_[:, off:off + n], S_[:, off:off + n], 1.0, bank(gb, n),
                                                               ALU.add, ALU.mult))
                DVE.need(g)
                for off, n, gb, ab in parts:
                    g = DVE.sig(nc.vector.scalar_tensor_tensor(R_[:, off:off + n], S_[:, off:off + n], 0.5, bank(ab, n),
                                                               ALU.mult, ALU.mult))
                _, gf[u % 2] = split(hi_[:, tile_of(u), :], lo_[:, tile_of(u), :], R_[:, 0:tot], g)
            ACTE.need(m)
            round_hi(p, chunk[0] + p + 2)
        chunk[0] += 2

    gf = {}
    gated(0, 6, ao2, XC, ghi, glo, lambda u: u, silu_t, silu_t)
    gated(4, 6, ao2, XC, ghi, glo, lambda u: 4 + u, silu_t, silu_t)
    m = (DVE.now(), ACTE.now(), PE.now())
    ACTE.need(*m)

    def evac_residual(layer, ctx):
        def ev_(i, u, m):
            j = 4 * i + u
            DVE.need(m)
            mf = modT[:].rearrange("p l t c -> p (l t) c")
            gl = mf[:, bass.ds(layer * 24 + 16 + j, 1), 0]
            r = [DVE.sig(nc.vector.scalar_tensor_tensor(dyn(xT, j, slice(0, SEQ)), bank(u), gl,
                                                        dyn(xT, j, slice(0, SEQ)), ALU.mult, ALU.add))]
            if ctx:
                gc = mf[:, bass.ds(layer * 24 + 16 + j, 1), 1]
                r.append(DVE.sig(nc.vector.scalar_tensor_tensor(dyn(cT, j, slice(0, CTX)), bank(4 + u, CTX), gc,
                                                                dyn(cT, j, slice(0, CTX)), ALU.mult, ALU.add)))
            return tuple(r)
        return ev_

    class Tail:

        def __init__(self, t, lo_):
            self.t, self.lo_ = t, lo_

        def __getitem__(self, k):
            a_, b_, c_ = k
            return self.t[a_, b_, self.lo_ + c_.start:self.lo_ + c_.stop]

    gemm(2, [(Tail(ghi, CTX), Tail(glo, CTX), SEQ), (Tail(ghi, 0), Tail(glo, 0), CTX)],
         evac_residual(0, True), per=(0, 8), after=m)
    m = (DVE.now(), ACTE.now(), PE.now())
    for x_ in (PE, ACTE, DVE):
        x_.need(*m)

    hh = modulated(1, m, "1")
    for x_ in (PE, ACTE, DVE):
        x_.need(*hh)
    PADC = CONV_TAPS // 2
    put = region(R0)
    uT = put("u_T", [P, CT, SEQ + 2 * PADC + 2])
    yc = put("conv_y", [P, CT, SEQ])
    dq = put("dq_T", [P, 4, SEQ])
    dk = put("dk_T", [P, 4, ALL])
    dv = put("dv", [P, ALL // P, 512])
    aod = put("attn3_tok", [P, NB, 512])
    oend = put.end
    utmp = [put(f"u_tmp{n}", [P, SEQ]) for n in range(2)]
    for x_ in (PE, ACTE, DVE):
        x_.need(*hh)
    DVE.sig(nc.vector.memset(uT[:, :, 0:PADC], 0.0))
    DVE.sig(nc.vector.memset(uT[:, :, PADC + SEQ:], 0.0))
    u_marks = {}

    def evac_u(i, u, m):
        t = 2 * i + u % 2
        if u < 2:
            DVE.need(m)
            u_marks[u] = DVE.sig(nc.vector.tensor_copy(uT[:, t, PADC:PADC + SEQ], bank(u)))
            return (u_marks[u],)
        ACTE.need(m, u_marks.get("free%d" % u))
        g = act(utmp[u - 2][:], bank(u), ACT.Tanh, scale=0.5)
        DVE.need(g, u_marks[u - 2])
        w = uT[:, t, PADC:PADC + SEQ]
        DVE.need(DVE.sig(nc.vector.scalar_tensor_tensor(w, utmp[u - 2][:], 1.0, w, ALU.add, ALU.mult)))
        u_marks["free%d" % u] = DVE.sig(nc.vector.tensor_scalar(w, w, 0.5, None, ALU.mult))
        return (g,)

    gemm(2, X, evac_u, unroll=True, after=hh)
    u_ready = DVE.now()
    DVE.need(u_ready)
    conv_ready = []
    for n in range(CONV_TAPS):
        for t in range(CT):
            wcol = col("c_dw_w_2", n * CT + t)
            src = uT[:, t, n:n + SEQ]
            if n:
                DVE.need(conv_ready[t])
                g = DVE.sig(nc.vector.scalar_tensor_tensor(yc[:, t, :], src, wcol, yc[:, t, :], ALU.mult, ALU.add))
                conv_ready[t] = g
            else:
                conv_ready.append(DVE.sig(nc.vector.tensor_scalar(yc[:, t, :], src, wcol, col("c_dw_b_2", t),
                                                                  ALU.mult, ALU.add)))
    m = (PE.now(), ACTE.now(), DVE.now())
    gemm(1, X, evac_copy(dest(dq, SEQ), scale=HEAD ** -0.5), after=m)
    m = (ACTE.now(), DVE.now())

    gemm(1, XC, evac_both(dk, 1.0), after=m)
    m = (ACTE.now(), DVE.now())
    blocks = [(chi, clo, b) for b in range(CB)] + [(hhi, hlo, b) for b in range(NB)]
    gemm_tokens(1, blocks, dv, lambda i, p: p * 256, after=m)
    m = (PE.now(), ACTE.now(), DVE.now())
    for x_ in (PE, ACTE, DVE):
        x_.need(*m)

    lw = region(C0)
    sqc = [lw(f"lsq{n}", [P, SEQ]) for n in range(2)]
    mean = lw("mean", [P, SEQ])
    dgl = lw("dg_ln", [P, SEQ])
    for t in range(CT):
        ins = nc.tensor.matmul(bank(0), ones[:], yc[:, t, :], start=t == 0, stop=t == CT - 1)
    m = PE.sig(ins)
    ACTE.need(m)
    m = act(mean[:], bank(0), scale=1.0 / 512)
    DVE.need(m)
    for t in range(CT):
        m = DVE.sig(nc.vector.tensor_tensor(yc[:, t, :], yc[:, t, :], mean[:], ALU.subtract))
    m = col_stats(lambda t: yc[:, t, :], CT, SEQ, sqc, (m,), dim=512)
    m = spread_cols(SEQ, dgl, m)
    DVE.need(m)
    fr = {}
    for t in range(CT):
        y_ = yc[:, t, :]
        DVE.need(DVE.sig(nc.vector.scalar_tensor_tensor(y_, y_, col("c_ln_g_2", t), bank(6), ALU.mult, ALU.mult)))
        m = DVE.sig(nc.vector.tensor_scalar(y_, y_, col("c_ln_b_2", t), None, ALU.add))
        ACTE.need(m, fr.get(t - 2))
        m2 = act(sqc[t % 2][:], y_, ACT.Tanh, scale=0.5)
        DVE.need(m, m2)
        fr[t] = DVE.sig(nc.vector.scalar_tensor_tensor(y_, sqc[t % 2][:], 1.0, y_, ALU.add, ALU.mult))
        DVE.need(fr[t])
        DVE.sig(nc.vector.tensor_scalar(y_, y_, 0.5, None, ALU.mult))
    m = (PE.now(), ACTE.now(), DVE.now())
    for x_ in (PE, ACTE, DVE):
        x_.need(*m)

    SLOTS = 2 * NA_KH - 2
    W2 = SLOTS * GRID_W
    aw = region(C0)
    probs3 = [aw(f"probs3_{n}", [P, ALL]) for n in range(2)]
    qst3 = aw("q4_staged", [P, SEQ])
    kst3 = aw("k4_staged", [P, ALL])
    nmask = aw("near_mask", [P, GRID_W])
    rv = aw("reverse", [P, P])
    assert aw.end <= C0 + 16384, aw.end - C0
    bw = region(oend)
    grev = bw("bias_reversed", [P, W2])
    gbias = [bw(f"bias{n}", [P, W2]) for n in range(2)]
    probsT3 = [bw(f"probsT3_{n}", [P, ALL]) for n in range(2)]
    assert bw.end <= R_END, bw.end - R_END
    nc.scalar.wait_ge(DVE.sem, DVE.n)
    nc.scalar.wait_ge(PE.sem, PE.n)
    load(nc.scalar, nmask[:], a["t_near_mask"])
    load(nc.scalar, rv[:], a["t_reverse"])
    need_inputs(PE, DVE)
    sem_bias = nc.alloc_semaphore("bias_landed")
    LB = 2 * GRID_W - 1
    rp = a["rpb_padded"]
    for j in range(4):
        DVE.need(PE.now())
        DVE.sig(nc.vector.tensor_copy(qst3[:], dq[:, j, :]))
        m0 = DVE.sig(nc.vector.tensor_copy(kst3[:], dk[:, j, :]))
        PE.need(m0)
        for s in range(2):
            head = 2 * j + s
            nc.scalar.wait_ge(PE.sem, PE.n)
            for half in range(2):
                src = bass.AP(tensor=rp.tensor, offset=rp.offset + (head * (2 * NA_KH - 1) + 1 - half) * LB,
                              ap=[[1, GRID_W], [LB, SLOTS], [1, GRID_W]])
                nc.scalar.dma_start(grev[half * 64:(half + 1) * 64, :].rearrange("p (d k) -> p d k", k=GRID_W),
                                    src).then_inc(sem_bias, 16)
            PE.e.wait_ge(sem_bias, 32 * (head + 1))
            PE.need(DVE.now(), ACTE.now())
            nc.tensor.matmul(bank(0, W2 // 2), rv[:], grev[:, 0:W2 // 2])
            m = PE.sig(nc.tensor.matmul(bank(1, W2 // 2), rv[:], grev[:, W2 // 2:W2]))
            DVE.need(m)
            for b in range(2):
                n = W2 // 2
                dst = gbias[s][:, b * n:(b + 1) * n].rearrange("p (d k) -> p d k", k=GRID_W)
                mk = bass.AP(tensor=nmask[:].tensor, offset=nmask[:].offset,
                             ap=[list(nmask[:].ap[0]), [0, n // GRID_W], [1, GRID_W]])
                m = DVE.sig(nc.vector.tensor_tensor(dst, bank(b, n).rearrange("p (d k) -> p d k", k=GRID_W), mk, ALU.add))
        DVE.need(m)
        PE.need(m)
        us = []
        for s in range(2):
            part = slice(s * HEAD, (s + 1) * HEAD)
            c0 = j * P + s * HEAD
            for i in range(NB):
                q = qst3[part, i * P:(i + 1) * P]
                k0 = (NA_KH - 2 - 2 * i) * GRID_W
                bias = gbias[s][:, k0:k0 + SEQ]
                us.append(dict(scores=[(0, 512, q, kst3[part, 0:512]), (512, 256, q, kst3[part, 512:ALL])], n=ALL,
                               bias=[(CTX, SEQ, bias)], dh=HEAD, out=aod[:, i, c0:c0 + HEAD],
                               values=[dv[:, k, c0:c0 + HEAD] for k in range(6)]))
        Attention(probs3, probsT3).run(us)
    m = (PE.now(), ACTE.now(), DVE.now())
    for x_ in (PE, ACTE, DVE):
        x_.need(*m)

    ow = region(R0 + 8 * 2048 + 2304)
    ohi, olo = ow("o_hi", [P, DT, SEQ], F32R), ow("o_lo", [P, DT, SEQ], F32R)
    cg = region(C0)
    sg = [cg(f"sg{n}", [P, SEQ]) for n in range(2)]
    pg = [cg(f"pg{n}", [P, SEQ]) for n in range(2)]
    aod2 = nc.alloc_sbuf_tensor_at("attn3_moved", [P, NB, 512], F32, offset=ow.end + 8192)
    m = DVE.sig(nc.vector.tensor_copy(aod2[:], aod[:]))
    for x_ in (PE, ACTE, DVE):
        x_.need(m)
    fr = {}

    def evac_conv_gate(i, u, m):
        ACTE.need(m, fr.get(u - 2))
        g = act(sg[u % 2][:], bank(u), ACT.Tanh, scale=0.5)
        DVE.need(g)
        g = DVE.sig(nc.vector.scalar_tensor_tensor(sg[u % 2][:], sg[u % 2][:], 1.0, bank(u), ALU.add, ALU.mult))
        DVE.need(g)
        g2 = DVE.sig(nc.vector.scalar_tensor_tensor(pg[u % 2][:], sg[u % 2][:], 0.5, yc[:, u, :], ALU.mult, ALU.mult))
        _, fr[u] = split(ohi[:, u, :], olo[:, u, :], pg[u % 2][:], g2)
        return (g,)

    gemm(1, X, evac_conv_gate)
    m = (PE.now(), ACTE.now(), DVE.now())
    for x_ in (PE, ACTE, DVE):
        x_.need(*m)
    gf = {}

    class Shift:
        def __init__(self, t):
            self.t = t

        def __getitem__(self, k):
            a_, b_, c_ = k
            return self.t[a_, b_, c_]

    gated_base = 0
    gated(0, NB, aod2, X, ohi, olo, lambda u: 4 + u, sg, pg)
    m = (PE.now(), ACTE.now(), DVE.now())
    gemm(2, [(ohi, olo, SEQ)], evac_residual(1, False), per=(0, 4), after=m, last=True)
    m = (PE.now(), ACTE.now(), DVE.now())

    fw = region(R0)
    sq = [fw(f"fsq{n}", [P, SEQ]) for n in range(2)]
    dgf = fw("fdg", [P, SEQ])
    tok = fw("out_tok", [P, NB, D_MODEL])
    m = col_stats(lambda t: xT[:, t, :], DT, SEQ, sq, m)
    m = spread_cols(SEQ, dgf, m)
    DVE.need(m)
    for t in range(DT):
        m = DVE.sig(nc.vector.scalar_tensor_tensor(xT[:, t, :], xT[:, t, :], col("final_g_2", t), bank(6),
                                                   ALU.mult, ALU.mult))
        PE.need(m)
        if t >= 4:
            PE.need(back[t - 4])
        else:
            back = {} if t == 0 else back
        for k in range(NB):
            ins = nc.tensor.transpose(bank(t % 4, P, k * P), xT[:, t, k * P:(k + 1) * P], ident[:])
        m = PE.sig(ins)
        ACTE.need(m)
        back[t] = act(tok[:, :, t * P:(t + 1) * P], bank(t % 4).rearrange("p (b n) -> p b n", b=NB))
    sem_out = nc.alloc_semaphore("output_stored")
    SP.wait_ge(ACTE.sem, ACTE.n)
    SP.dma_start(a["out"][0].rearrange("(b p) d -> p b d", p=P), tok[:]).then_inc(sem_out, 16)
    SP.wait_ge(sem_out, 16)
    assert chunk[0] == sent[0], (chunk, sent)


INPUTS = ["x", "mem", "norm_mix_pre", "w_in", "lambda_q1", "lambda_k1", "lambda_q2", "lambda_k2", "subln_g",
          "w_attn_branch", "pool_w", "pool_scale", "w_pool_branch", "norm_mem", "w_mem_kv", "w_mem_branch", "w_out",
          "norm_mix_post", "norm_ffn_pre", "w_up", "conv_w", "conv_b", "w_down", "norm_ffn_post", "c_2", "ctx_2",
          "c_ctx_2", "mod_w_2", "mod_b_2", "norm_g_2", "ev_w_in_2", "ev_w_out_2", "a_q_gain_2", "a_k_gain_2",
          "b_sink_2", "od_w_in_2", "od_w_out_2", "c_dw_w_2", "c_dw_b_2", "c_ln_g_2", "c_ln_b_2", "final_g_2"]


def kernel(**inputs):
    import concourse.bacc as bacc
    from concourse.bass_utils import run_bass_kernel_spmd

    arrays = {n: np.ascontiguousarray(inputs[n]) for n in INPUTS}
    rpb = np.asarray(inputs["d_rpb_2"])[0]
    padded = np.zeros((rpb.shape[0], rpb.shape[1], 2 * GRID_W - 1), rpb.dtype)
    padded[:, :, GRID_W - NA_KW:GRID_W + NA_KW - 1] = rpb
    arrays["rpb_padded"] = padded
    for n, v in shape_tables().items():
        arrays["t_" + n] = np.ascontiguousarray(v)
    nc = bacc.Bacc("TRN2", target_bir_lowering=False, num_devices=1)
    aps = {n: nc.dram_tensor("in_" + n, v.shape, mybir.dt.from_np(v.dtype), kind="ExternalInput").ap()
           for n, v in arrays.items()}
    aps["out"] = nc.dram_tensor("out_0", (1, SEQ, D_MODEL), F32, kind="ExternalOutput").ap()
    build(nc, aps)
    r = run_bass_kernel_spmd(nc, [{"in_" + n: v for n, v in arrays.items()}], core_ids=[0])
    return r.results[0]["out_0"]
```

```python
import math
from contextlib import contextmanager

import numpy as np

import concourse.bass as bass
from concourse import mybir
from concourse.alu_op_type import AluOpType as ALU

F32 = mybir.dt.float32
F32R = mybir.dt.float32r
ACT = mybir.ActivationFunctionType
AX = mybir.AxisListType.X
P = 128
EPS = 1e-6

D_MODEL, SEQ, MEM, CTX = 1024, 512, 256, 256
DT = D_MODEL // P
NB = SEQ // P
CB = CTX // P
ALL = CTX + SEQ
DIFF_HEADS, DIFF_DH = 8, 64
MEM_HEADS = 4
POOL_WINDOWS = (2, 4, 8, 16)
POOL_PAD = max(POOL_WINDOWS)
LAM_INIT = 0.8 - 0.6 * math.exp(-0.3 * 0)
D_FF, FT = 2816, 2816 // P
HEAD = 64
GRID_W, NA_KH, NA_KW = 64, 8, 16
CONV_TAPS = 31
CT = 512 // P
MASKED = -1e30
CHUNK_COLS = 256
CHUNK = DT * CHUNK_COLS

ROWS = dict(norm_mix_pre=8, norm_mem=8, norm_mix_post=8, norm_ffn_pre=8, norm_ffn_post=8, pool_scale=4,
            subln_g=1, final_g_2=8, norm_g_2=16, mod_b_2=48, conv_b=44, c_2=8, c_ctx_2=8,
            a_q_gain_2=1, a_k_gain_2=1, c_dw_b_2=4, c_ln_g_2=4, c_ln_b_2=4, conv_w=132, c_dw_w_2=124)


def row_places():
    at, places = 0, {}
    for name, n in ROWS.items():
        places[name] = at
        at += n
    return places, -(-at // P)


def shape_tables():
    f = np.float32
    t = {}
    t["ident"] = np.eye(P, dtype=f)
    q, j = np.arange(P)[:, None], np.arange(SEQ)[None, :]
    rel = j - (SEQ - P) - q
    t["distance"] = np.where(rel <= 0, rel, -1e32).astype(f)
    t["slopes"] = np.tile(np.exp2(-8.0 * np.arange(1, DIFF_HEADS + 1) / DIFF_HEADS).astype(f), (P, 1))
    k = np.arange(P)[None, :]
    t["band_left"] = np.where(k >= q, 0, MASKED).astype(f)
    t["band_right"] = np.where(k <= q, 0, MASKED).astype(f)
    tok = np.arange(SEQ)
    half = HEAD // 2
    freqs = 10000.0 ** (-np.arange(0, half, 2, dtype=f) / half)
    ang = np.concatenate([(tok // GRID_W).astype(f)[:, None] * freqs, (tok % GRID_W).astype(f)[:, None] * freqs], -1)
    pair = (np.arange(P) % HEAD) // 2
    t["rope_cos"] = np.cos(ang).astype(f)[:, pair].T.copy()
    t["rope_sin"] = np.sin(ang).astype(f)[:, pair].T.copy()
    rot = np.zeros((P, P), f)
    e = np.arange(0, P, 2)
    rot[e + 1, e] = -1
    rot[e, e + 1] = 1
    t["rotate"] = rot
    rev = np.zeros((P, P), f)
    i = np.arange(P)
    rev[i, (i // GRID_W) * GRID_W + GRID_W - 1 - i % GRID_W] = 1
    t["reverse"] = rev
    qc, kc = np.arange(GRID_W)[:, None], np.arange(GRID_W)[None, :]
    start = np.clip(qc - NA_KW // 2, 0, GRID_W - NA_KW)
    near = np.where((kc >= start) & (kc < start + NA_KW), 0, MASKED).astype(f)
    t["near_mask"] = np.concatenate([near, near])
    gather = np.zeros((P, 5, 10), f)
    spread = np.zeros((10, 5, P), f)
    for n in range(5):
        for p in range(P):
            gather[p, n, 2 * n + p // HEAD] = 1.0 / HEAD
            spread[2 * n + p // HEAD, n, p] = 1
    t["head_gather"] = gather.reshape(P, 50)
    t["head_spread"] = np.pad(spread.reshape(10, 5 * P), ((0, P - 10), (0, 0)))
    corr = np.zeros((len(POOL_WINDOWS), POOL_PAD), f)
    for g, w in enumerate(POOL_WINDOWS):
        corr[g] = w / np.minimum(np.arange(POOL_PAD) + 1, w)
    t["pool_edge"] = np.tile(corr.reshape(1, -1), (P, 1))
    return t


class Mark:

    def __init__(self, sem, at, step=0, reg=None):
        self.sem, self.at, self.step, self.reg = sem, at, step, reg

    def value(self):
        return self.at + self.step * self.reg if self.reg is not None else self.at

    def before(self, n=1):
        return Mark(self.sem, self.at - n * self.step, self.step, self.reg)

    def minus(self, n):
        return Mark(self.sem, self.at - n, self.step, self.reg)


class Engine:

    def __init__(self, nc, e, name):
        self.e, self.sem, self.n = e, nc.alloc_semaphore(name + "_done"), 0
        self.step, self.reg = 0, None

    def sig(self, ins):
        ins.then_inc(self.sem, 1)
        self.n += 1
        return Mark(self.sem, self.n, self.step, self.reg)

    def now(self):
        return Mark(self.sem, self.n, self.step, self.reg)

    def need(self, *marks):
        for m in marks:
            if m is not None:
                self.e.wait_ge(m.sem, m.value())


def build(nc, a):
    PE, ACTE, DVE, POOL = (Engine(nc, e, n) for e, n in (
        (nc.tensor, "pe"), (nc.scalar, "act"), (nc.vector, "dve"), (nc.gpsimd, "pool")))
    SP = nc.sync

    @contextmanager
    def loop(n, **steps):
        es = {"pe": PE, "act": ACTE, "dve": DVE, "pool": POOL}
        used = {k: es[k] for k in steps}
        start = {k: x.n for k, x in used.items()}
        with nc.Fori(0, n, engines=[x.e.engine for x in used.values()]) as i:
            for k, x in used.items():
                x.step, x.reg = steps[k], i
            yield i
            for k, x in used.items():
                assert x.n - start[k] == steps[k], (k, x.n - start[k], steps[k])
                x.step, x.reg = 0, None
                x.n = start[k] + n * steps[k]

    base = [(nc.sbuf_base + 63) // 64 * 64]

    def sb(name, shape, dt=F32, at=None):
        size = 4 * int(np.prod(shape[1:]))
        if at is None:
            at = base[0]
            base[0] += (size + 63) // 64 * 64
        return nc.alloc_sbuf_tensor_at(name, shape, dt, offset=at)

    raw = [sb(f"w_raw{p}", [P, CHUNK]) for p in range(2)]
    whi = [sb(f"w_hi{p}", [P, CHUNK], F32R) for p in range(2)]
    wlo = [sb(f"w_lo{p}", [P, CHUNK], F32R) for p in range(2)]
    xT = sb("x_T", [P, DT, SEQ])
    hhi, hlo = sb("h_hi", [P, DT, SEQ], F32R), sb("h_lo", [P, DT, SEQ], F32R)
    C0 = base[0]
    chi, clo = sb("c_hi", [P, DT, CTX], F32R), sb("c_lo", [P, DT, CTX], F32R)
    places, n_groups = row_places()
    cols = sb("cols", [P, n_groups * P])
    ident = sb("ident", [P, P])
    ones = sb("ones", [P, P])
    small = sb("small", [P, 256])
    rowvec = sb("rowvec", [1, 16])
    lamrow = sb("lamrow", [1, 4, DIFF_DH])
    modT = sb("mod_T", [P, 2, 24, 2])
    R0 = base[0]
    R_END = nc.sbuf_usable_end

    def region(at):
        pos = [at]

        def put(name, shape, dt=F32):
            size = 4 * int(np.prod(shape[1:]))
            t = nc.alloc_sbuf_tensor_at(name, shape, dt, offset=pos[0])
            pos[0] += (size + 63) // 64 * 64
            put.end = pos[0]
            return t
        return put

    ps = nc.alloc_psum_tensor("ps", [P, 8 * 512], F32)

    def bank(b, n=512, off=0, parts=P):
        return ps[0:parts, b * 512 + off:b * 512 + off + n]

    def col(name, i=0):
        c = places[name] + i
        return cols[:, c:c + 1]

    def dyn_col(name, i):
        return cols[:, bass.ds(places[name] + i, 1)]

    eps = small[:, 0:1]
    nlam = small[:, 1:2]
    sink = small[:, 2:10]
    nsink = small[:, 10:18]
    qgain = small[:, 18:19]
    subg = small[:, 19:20]
    zero1 = small[:, 20:21]
    slopes = small[:, 24:32]
    st = small[:, 32:48]
    sm = small[:, 48:80]

    sem_in = nc.alloc_semaphore("inputs_landed")
    landed = [0]

    def load(eng, dst, src):
        eng.dma_start(dst, src).then_inc(sem_in, 16)
        landed[0] += 16

    def need_inputs(*engines):
        for x in engines:
            x.e.wait_ge(sem_in, landed[0])

    def act(out, in_, func=ACT.Copy, **kw):
        return ACTE.sig(nc.scalar.activation(out, in_, func, **kw))

    def f(ap):
        return ap.bitcast(F32)

    setup = region(R0)
    xin = setup("x_in", [P, NB, D_MODEL])
    min_ = setup("mem_in", [P, CB, D_MODEL])
    memT = setup("mem_T", [P, DT, MEM])
    rows = setup("rows", [P, n_groups, P])
    load(SP, ident[:], a["t_ident"])
    load(SP, xin[:], a["x"][0].rearrange("(b p) d -> p b d", p=P))

    def load_rows(name, src, at=0):
        r, n, done = places[name] + at, src.shape[0], 0
        while done < n:
            g, p = (r + done) // P, (r + done) % P
            k = min(n - done, P - p)
            load(nc.scalar, rows[p:p + k, g, :], src[done:done + k, :])
            done += k

    DVE.sig(nc.vector.memset(rows[:], 0.0))
    ACTE.need(DVE.now())
    for name in ("norm_mix_pre", "norm_mem", "norm_mix_post", "norm_ffn_pre", "norm_ffn_post", "conv_b",
                 "norm_g_2", "c_2", "c_dw_b_2", "c_ln_g_2", "c_ln_b_2", "pool_scale", "mod_b_2"):
        load_rows(name, a[name].rearrange("l (t p) -> (l t) p", p=P))
    load_rows("subln_g", a["subln_g"])
    for name in ("c_ctx_2", "final_g_2"):
        load_rows(name, a[name].rearrange("(t p) -> t p", p=P))
    load_rows("conv_w", a["conv_w"].rearrange("l j (t p) -> (l j t) p", p=P))
    load_rows("c_dw_w_2", a["c_dw_w_2"].rearrange("l j (t p) -> (l j t) p", p=P))
    for name in ("a_q_gain_2", "a_k_gain_2"):
        g, p = places[name] // P, places[name] % P
        for s in range(2):
            load(nc.scalar, rows[p:p + 1, g, s * HEAD:(s + 1) * HEAD], a[name])
    for n, name in enumerate(("lambda_q1", "lambda_k1", "lambda_q2", "lambda_k2")):
        load(nc.scalar, lamrow[:, n, :], a[name])
    load(nc.scalar, rowvec[0:1, 1:9], a["b_sink_2"])
    load(SP, slopes, a["t_slopes"])
    load(SP, min_[:], a["mem"][0].rearrange("(b p) d -> p b d", p=P))
    DVE.sig(nc.vector.memset(ones[:], 1.0))
    DVE.sig(nc.vector.memset(eps, EPS))
    DVE.sig(nc.vector.memset(zero1, 0.0))
    consts_set = DVE.sig(nc.vector.memset(rowvec[0:1, 9:16], 0.0))
    need_inputs(PE, DVE, ACTE)
    PE.need(consts_set)
    ACTE.need(consts_set)

    DVE.sig(nc.vector.tensor_tensor(lamrow[:, 0, :], lamrow[:, 0, :], lamrow[:, 1, :], ALU.mult))
    DVE.need(DVE.sig(nc.vector.tensor_tensor(lamrow[:, 2, :], lamrow[:, 2, :], lamrow[:, 3, :], ALU.mult)))
    m = DVE.sig(nc.vector.tensor_reduce(rowvec[0:1, 10:12], lamrow[:, 0:4:2, :], AX, ALU.add))
    ACTE.need(m)
    nc.scalar.preload_act_table(ACT.Exp)
    m = act(rowvec[0:1, 12:14], rowvec[0:1, 10:12], ACT.Exp)
    DVE.need(m)
    DVE.need(DVE.sig(nc.vector.tensor_tensor(rowvec[0:1, 14:15], rowvec[0:1, 12:13], rowvec[0:1, 13:14], ALU.subtract)))
    m = DVE.sig(nc.vector.tensor_scalar(rowvec[0:1, 0:1], rowvec[0:1, 14:15], LAM_INIT, None, ALU.add))
    PE.need(m)
    m = PE.sig(nc.tensor.matmul(bank(7, 16), ones[0:1, :], rowvec[0:1, :]))
    DVE.need(m)
    DVE.sig(nc.vector.tensor_scalar(nlam, bank(7, 1), -1.0, None, ALU.mult))
    DVE.sig(nc.vector.tensor_copy(sink, bank(7, 8, 1)))
    row_m = DVE.sig(nc.vector.tensor_scalar(nsink, bank(7, 8, 1), -1.0, None, ALU.mult))

    for g in range(n_groups):
        m = PE.sig(nc.tensor.transpose(bank(g), rows[:, g, :], ident[:])) if False else \
            PE.sig(nc.tensor.transpose(bank(g % 6, P), rows[:, g, :], ident[:]))
        ACTE.need(m)
        cols_set = act(cols[:, g * P:(g + 1) * P], bank(g % 6, P))
        assert n_groups <= 6
    DVE.need(cols_set)
    DVE.sig(nc.vector.tensor_scalar(qgain, col("a_q_gain_2"), HEAD ** -0.5, None, ALU.mult))
    DVE.sig(nc.vector.tensor_scalar(subg, col("subln_g"), 1.0 - LAM_INIT, None, ALU.mult))

    def to_feature_major(src, nb, dst, after, banks=(0, 1, 2, 3)):
        PE.need(*after)
        freed = [None] * len(banks)
        for t in range(DT):
            b = banks[t % len(banks)]
            PE.need(freed[t % len(banks)])
            for k in range(nb):
                ins = nc.tensor.transpose(bank(b, P, k * P), src[:, k, t * P:(t + 1) * P], ident[:])
            m = PE.sig(ins)
            if t % 2:
                ACTE.need(m)
                freed[t % len(banks)] = act(dst[:, t, :], bank(b, nb * P))
            else:
                DVE.need(m)
                freed[t % len(banks)] = DVE.sig(nc.vector.tensor_copy(dst[:, t, :], bank(b, nb * P)))
        return ACTE.now(), DVE.now()

    x_ready = to_feature_major(xin, NB, xT, (cols_set, row_m))
    mem_ready = to_feature_major(min_, CB, memT, x_ready)

    landed_w = [nc.alloc_semaphore(f"chunk_landed{p}") for p in range(2)]
    hi_done = nc.alloc_semaphore("chunk_hi_done")
    lo_done = nc.alloc_semaphore("chunk_lo_done")

    MOD_CHUNKS = 3 * D_MODEL // CHUNK_COLS
    cond = small[:, 192:208].rearrange("p (t n) -> p t n", n=2)
    condt = small[:, 208:224].rearrange("p (t n) -> p t n", n=2)
    ACTE.need(cols_set)
    for n, name in enumerate(("c_2", "c_ctx_2")):
        c0 = places[name]
        m = act(condt[:, :, n], cols[:, c0:c0 + DT], ACT.Tanh, scale=0.5)
    DVE.need(m)
    for n, name in enumerate(("c_2", "c_ctx_2")):
        c0 = places[name]
        DVE.need(DVE.sig(nc.vector.scalar_tensor_tensor(cond[:, :, n], condt[:, :, n], 1.0, cols[:, c0:c0 + DT],
                                                        ALU.add, ALU.mult)))
    cond_ready = DVE.sig(nc.vector.tensor_scalar(cond, cond, 0.5, None, ALU.mult))
    PE.need(cond_ready, *mem_ready)
    mod_raw = [nc.alloc_sbuf_tensor_at(f"mod_raw{p}", [P, CHUNK], F32, offset=C0 + p * 4 * CHUNK) for p in range(2)]
    mod_landed = [nc.alloc_semaphore(f"mod_landed{p}") for p in range(2)]
    mod_slots = nc.alloc_semaphore("mod_slots")
    mod_flat = modT[:].rearrange("p l t c -> p (l t) c")

    def mod_load(layer, p, m, i, step):
        SP.wait_ge(mod_slots, layer * (MOD_CHUNKS + 2) + m + 1 + step * i)
        src = a["mod_w_2"][layer][:, bass.ds(i * (step * CHUNK_COLS) + m * CHUNK_COLS, CHUNK_COLS)]
        SP.dma_start(mod_raw[p][:].rearrange("p (k n) -> p k n", k=DT),
                     src.rearrange("(k p) n -> p k n", p=P)).then_inc(mod_landed[p], 16)

    def mod_open(*marks):
        DVE.need(*marks)
        nc.vector.memset(zero1, 0.0).then_inc(mod_slots, 2)

    def mod_product(layer, m, i, step, bank_free):
        p = m % 2
        PE.e.wait_ge(mod_landed[p], 16 * (layer * MOD_CHUNKS // 2 + m // 2 + 1) + 8 * step * i)
        PE.need(bank_free)
        w = mod_raw[p][:].rearrange("p (k n) -> p k n", k=DT)
        for o in range(2):
            for k in range(DT):
                ins = nc.tensor.matmul(bank(4 + p, 2, 2 * o), w[:, k, o * P:(o + 1) * P], cond[:, k, :],
                                       start=k == 0, stop=k == DT - 1)
        ins.then_inc(mod_slots, 1)
        DVE.e.wait_ge(mod_slots, layer * (MOD_CHUNKS + 2) + 2 + m + 1 + step * i)
        for o in range(2):
            t = layer * 3 * DT + 2 * m + o + 2 * step * i
            d = DVE.sig(nc.vector.tensor_scalar(mod_flat[:, bass.ds(t, 1), :].rearrange("p a c -> p (a c)"),
                                                bank(4 + p, 2, 2 * o), dyn_col("mod_b_2", t), None, ALU.add))
        return d

    chunk = [0]
    sent = [0]

    def sp_load(p, value, src, kt, n):
        if value is not None:
            SP.wait_ge(lo_done, value)
        dst = raw[p][:, 0:kt * n].rearrange("p (k n) -> p k n", k=kt)
        SP.dma_start(dst, src.rearrange("(k p) n -> p k n", p=P)).then_inc(landed_w[p], 16)

    def stream(w, starts, step=0, n=1, rows_=(0, D_MODEL), width=CHUNK_COLS, mod=None):
        r0, r1 = rows_
        kt = (r1 - r0) // P
        c0 = sent[0]
        assert len(starts) % 2 == 0
        if c0 == 0:
            for i in range(n):
                for q, s in enumerate(starts):
                    c = i * len(starts) + q
                    sp_load(q % 2, c - 1 if c > 1 else None, w[r0:r1, i * step + s:i * step + s + width], kt, width)
            sent[0] += n * len(starts)
            return
        with nc.Fori(0, n, engines=[SP.engine]) as i:
            for q, s in enumerate(starts):
                sp_load(q % 2, (c0 + q - 1) + len(starts) * i,
                        w[r0:r1, bass.ds(i * step + s, width)], kt, width)
                if mod is not None:
                    mod_load(mod[0], q % 2, mod[1] + q, i, len(starts))
        sent[0] += n * len(starts)

    def stream_down(w):
        c0 = sent[0]
        with nc.Fori(0, 2, engines=[SP.engine]) as i:
            for q in range(6):
                g, k = divmod(q, 3)
                k0, k1 = 8 * k, min(8 * k + 8, FT)
                sp_load(q % 2, (c0 + q - 1) + 6 * i, w[k0 * P:k1 * P, bass.ds(i * 512 + g * 256, 256)], k1 - k0, 256)
                mod_load(1, q % 2, q, i, 6)
        sent[0] += 12

    def round_hi(p, c, i=None, step=0):
        v = 16 * (c // 2 + 1)
        ACTE.e.wait_ge(landed_w[p], v if i is None else v + 8 * step * i)
        nc.scalar.activation(whi[p][:], raw[p][:], ACT.Copy).then_inc(hi_done, 1)

    def mm3(out, whi_, wlo_, xhi_, xlo_, first, last, flip=False):
        for n, (w, x) in enumerate(((wlo_, xhi_), (whi_, xlo_), (whi_, xhi_))):
            l, r = (x, w) if flip else (w, x)
            ins = nc.tensor.matmul(out, l, r, start=first and n == 0, stop=last and n == 2)
        return ins

    class Sources:
        pass

    def gemm(n_pairs, xs, evac, kt=DT, cols_=CHUNK_COLS, per=None, after=(), last=False, unroll=False, ready=None, mod=None):
        outs = 2 * cols_ // P
        base_chunk = chunk[0]
        for e in after:
            PE.need(e)

        in_loop, mod_start = False, [None]

        def body(i, peeled=False):
            freed = {}
            for p in range(2):
                c = base_chunk + p
                PE.e.wait_ge(lo_done, c + 1 + 2 * i)
                hi = whi[p][:, 0:kt * cols_].rearrange("p (k n) -> p k n", k=kt)
                lo = wlo[p][:, 0:kt * cols_].rearrange("p (k n) -> p k n", k=kt)
                for o in range(cols_ // P):
                    u = p * (cols_ // P) + o
                    b = u % 4
                    if u >= 4:
                        PE.need(*freed[b])
                    elif in_loop:
                        na, nd = evac.own(u)
                        PE.need(ACTE.now().minus(per[0] - na) if na else None, DVE.now().minus(per[1] - nd) if nd else None)
                    else:
                        PE.need(*before[b])
                    s = slice(o * P, (o + 1) * P)
                    for n, (xh, xl, tok) in enumerate(xs):
                        for k in range(kt):
                            if ready and u == 0:
                                PE.need(ready[n][k])
                            ins = mm3(bank(b + 4 * n, tok), hi[:, k, s], lo[:, k, s], xh[:, k, 0:tok],
                                      xl[:, k, 0:tok], k == 0, k == kt - 1)
                    m = PE.sig(ins)
                    freed[b] = evac(i, u, m)
                if mod is not None:
                    mod_product(mod[0], mod[1] + p, i, 2, mod_start[0])
                if not peeled:
                    ACTE.need(m)
                    round_hi(p, c + 2, None if n_pairs == 1 or unroll else i, 2) if not unroll else \
                        round_hi(p, c + 2 + 2 * i)
            return freed

        before = {b: (ACTE.now(), DVE.now()) for b in range(4)}
        if n_pairs == 1 or unroll:
            for i in range(n_pairs):
                before = body(i, peeled=last and i == n_pairs - 1)
        else:
            n_loop = n_pairs - 1 if last else n_pairs
            PE.need(ACTE.now(), DVE.now())
            in_loop = True
            with loop(n_loop, pe=outs, act=per[0], dve=per[1]) as i:
                mod_start[0] = DVE.now()
                body(i)
            in_loop = False
            if last:
                before = {b: (ACTE.now(), DVE.now()) for b in range(4)}
                body_i = n_loop
                body(body_i, peeled=True)
        chunk[0] += 2 * n_pairs

    def gemm_tokens(n_pairs, lhs, dst, col_of, after=(), width=CHUNK_COLS, mod=None, only_act=False):
        base_chunk = chunk[0]
        for e in after:
            PE.need(e)
        nblk = len(lhs)
        assert nblk * 2 <= 16
        banks = 4 if mod is not None else 8
        n_act = nblk if only_act else nblk // 2
        with loop(n_pairs, pe=2 * nblk, act=2 * n_act, dve=2 * (nblk - n_act) + (4 if mod is not None else 0)) as i:
            a0, d0 = ACTE.now(), DVE.now()
            freed = {b: (a0, d0) for b in range(8)}
            for p in range(2):
                PE.e.wait_ge(lo_done, base_chunk + p + 1 + 2 * i)
                hi = whi[p][:].rearrange("p (k n) -> p k n", k=DT)
                lo = wlo[p][:].rearrange("p (k n) -> p k n", k=DT)
                for n, (xh, xl, blk) in enumerate(lhs):
                    b = (p * nblk + n) % banks
                    PE.need(*freed[b])
                    ts = slice(blk * P, (blk + 1) * P)
                    for k in range(DT):
                        ins = mm3(bank(b, width), hi[:, k, :], lo[:, k, :], xh[:, k, ts], xl[:, k, ts],
                                  k == 0, k == DT - 1, flip=True)
                    m = PE.sig(ins)
                    out = dst[:, n, bass.ds(col_of(i, p), width)]
                    if n % 2 or only_act:
                        ACTE.need(m)
                        freed[b] = (act(out, bank(b, width)),)
                    else:
                        DVE.need(m)
                        freed[b] = (DVE.sig(nc.vector.tensor_copy(out, bank(b, width))),)
                if mod is not None:
                    mod_product(mod[0], mod[1] + p, i, 2, d0)
                ACTE.need(m)
                round_hi(p, base_chunk + p + 2, i, 2)
        chunk[0] += 2 * n_pairs

    w_in = a["w_in"][0]
    stream(a["w_mem_kv"][0], [0, 256], 512, 2)
    stream(w_in, [3584, 3840])
    stream(w_in, [3072, 3328])
    stream(w_in, [6144, 6400], 512, 2)
    stream(a["w_mem_branch"][0], [0, 512], rows_=(0, 512), width=512)
    stream(w_in, [5120, 5376], 512, 2)
    stream(a["w_pool_branch"][0], [0, 512], rows_=(0, 512), width=512)
    stream(w_in, [0, 256], 512, 2, mod=(0, 0))
    stream(w_in, [1024, 1280], 512, 2, mod=(0, 4))
    stream(w_in, [2048, 2304], 512, 2, mod=(0, 8))
    stream(w_in, [4096, 4352], 512, 2)
    stream(a["w_attn_branch"][0], [0, 256], 512, 2)
    stream(a["w_out"][0], [0, 256], 512, 2)
    stream(a["w_up"][0], [0, D_FF], 256, D_FF // 256)
    stream_down(a["w_down"][0])
    ev = a["ev_w_in_2"][0]
    stream(ev, [0, 256], 1280, 2)
    stream(ev, [512, 1792])
    stream(ev, [768, 1024])
    stream(ev, [2048, 2304])
    stream(a["ev_w_out_2"][0], [0, 256], 512, 2)
    od = a["od_w_in_2"][0]
    stream(od, [0, 512], 256, 2)
    stream(od, [1536, 1792])
    stream(od, [2048, 2304])
    stream(od, [2560, 2816])
    stream(od, [1024, 1280])
    stream(od, [3072, 3328])
    stream(a["od_w_out_2"][0], [0, 256], 512, 2)

    with nc.Fori(0, sent[0] // 2, engines=[nc.gpsimd.engine]) as i:
        for p in range(2):
            nc.gpsimd.wait_ge(hi_done, 2 * i + p + 1)
            nc.gpsimd.tensor_tensor(wlo[p][:], raw[p][:], f(whi[p][:]), ALU.subtract).then_inc(lo_done, 1)

    for p in range(2):
        round_hi(p, p)

    norm_count = []

    def col_stats(src_of, n_tiles, tokens, sq, after=(), ready=None, bank_=7, dim=D_MODEL, both=True):
        nb = tokens // P
        used = {}
        nc.scalar.preload_act_table(ACT.Sqrt)
        for x_ in (PE, ACTE, DVE) if both else (PE, ACTE):
            x_.need(*after)
        for t in range(n_tiles):
            w, s_ = sq[t % 2][:, 0:tokens], src_of(t)
            e = DVE if both and t % 2 else ACTE
            e.need(used.get(t - 2), ready[t] if ready else None)
            m = DVE.sig(nc.vector.tensor_tensor(w, s_, s_, ALU.mult)) if e is DVE else act(w, s_, ACT.Square)
            PE.need(m)
            for b in range(nb):
                ins = nc.tensor.matmul(bank(bank_, 1, b), sq[t % 2][:, b * P:(b + 1) * P], ones[:, 0:1],
                                       start=t == 0 and b == 0, stop=t == n_tiles - 1, skip_group_check=True)
            used[t] = PE.sig(ins)
        ACTE.need(used[n_tiles - 1])
        m = act(st[:, 0:nb], bank(bank_, nb), ACT.Sqrt, scale=1.0 / dim, bias=eps)
        DVE.need(m)
        nc.scalar.preload_act_table(ACT.Exp)
        return DVE.sig(nc.vector.reciprocal(st[:, 8:8 + nb], st[:, 0:nb]))

    def spread_cols(tokens, dg, m, bank_=6):
        nb = tokens // P
        DVE.need(m)
        for b in range(nb):
            m = DVE.sig(nc.vector.tensor_scalar(dg[:, b * P:(b + 1) * P], ident[:], st[:, 8 + b:9 + b], None, ALU.mult))
        PE.need(m)
        return PE.sig(nc.tensor.matmul(bank(bank_, tokens), ones[:], dg[:, 0:tokens]))

    def norm_split(src, tokens, hi, lo, gain_of, work, after, shift_of=None, ready=None, bank_=6):
        tag = str(len(norm_count))
        norm_count.append(0)
        sq = [work(f"sq{n}_{tag}", [P, SEQ]) for n in range(2)]
        dg = work("dg_" + tag, [P, SEQ])
        tmp = [work(f"nt{n}_{tag}", [P, SEQ]) for n in range(3)]
        m = col_stats(lambda t: src[:, t, :], DT, tokens, sq, after, ready, both=ready is None)
        spread = spread_cols(tokens, dg, m, bank_)
        rounded, done = {}, {}

        def low(t):
            DVE.need(rounded[t])
            w, h = tmp[t % 3][:, 0:tokens], f(hi[:, t, 0:tokens])
            done[t] = DVE.sig(nc.vector.tensor_tensor(lo[:, t, 0:tokens], w, h, ALU.subtract) if shift_of is None else
                              nc.vector.scalar_tensor_tensor(lo[:, t, 0:tokens], w, shift_of(t), h, ALU.add, ALU.subtract))

        DVE.need(spread)
        for t in range(DT):
            w = tmp[t % 3][:, 0:tokens]
            DVE.need(done.get(t - 3))
            g = DVE.sig(nc.vector.scalar_tensor_tensor(w, src[:, t, :], gain_of(t), bank(bank_, tokens), ALU.mult, ALU.mult))
            ACTE.need(g)
            rounded[t] = act(hi[:, t, 0:tokens], w) if shift_of is None else \
                act(hi[:, t, 0:tokens], w, ACT.Identity, bias=shift_of(t))
            if t:
                low(t - 1)
        low(DT - 1)
        return [done[t] for t in range(DT)]

    def split(hi_ap, lo_ap, src, m, src_is_act=False):
        ACTE.need(m)
        g = act(hi_ap, src)
        DVE.need(g)
        return g, DVE.sig(nc.vector.tensor_tensor(lo_ap, src, f(hi_ap), ALU.subtract))

    h_ready = norm_split(xT, SEQ, hhi, hlo, lambda t: col("norm_mix_pre", t), region(R0), (*x_ready, cond_ready))
    m_ready = norm_split(memT, MEM, chi, clo, lambda t: col("norm_mem", t),
                         region(R0 + 6 * 2048), h_ready[-1:])

    put = region(R0)
    mixT = put("mix_T", [P, DT, SEQ])
    gate = put("gate", [P, DT, SEQ])
    kmT = put("km_T", [P, MEM_HEADS, MEM])
    vm = put("vm", [P, CB, MEM_HEADS * P])
    qmT = put("qm_T", [P, MEM_HEADS, SEQ])
    upT = put("up_T", [P, 4, POOL_PAD + SEQ])
    om = put("om", [P, NB, MEM_HEADS * P])
    bhi, blo = put("b_hi", [P, 4, SEQ], F32R), put("b_lo", [P, 4, SEQ], F32R)
    pre_end = put.end
    assert pre_end <= R_END, (pre_end, R_END)

    def owns(*signals):
        def mark(ev_):
            ev_.own = lambda u: signals[u % 2]
            return ev_
        return mark

    def evac_copy(dst_of, **kw):
        @owns((0, 1), (1, 0))
        def ev_(i, u, m):
            if u % 2:
                ACTE.need(m)
                return (act(dst_of(i, u), bank(u % 4, dst_of.n), **kw),)
            DVE.need(m)
            s = kw.get("scale")
            if s is None:
                return (DVE.sig(nc.vector.tensor_copy(dst_of(i, u), bank(u % 4, dst_of.n))),)
            return (DVE.sig(nc.vector.tensor_scalar(dst_of(i, u), bank(u % 4, dst_of.n), s, None, ALU.mult)),)
        return ev_

    def dest(t, n, lo_=0):
        def of(i, u):
            j = 4 * i + u
            if isinstance(j, int):
                return t[:, j, lo_:lo_ + n]
            return t[:, bass.ds(j, 1), lo_:lo_ + n].rearrange("p a n -> p (a n)")
        of.n = n
        return of

    X = [(hhi, hlo, SEQ)]
    C = [(chi, clo, CTX)]
    XC = X + C
    gemm(1, C, evac_copy(dest(kmT, MEM)), ready=[m_ready])
    gemm_tokens(1, [(chi, clo, b) for b in range(CB)], vm, lambda i, p: p * 256)
    gemm(1, X, evac_copy(dest(qmT, SEQ), scale=P ** -0.5))
    gemm(1, X, evac_copy(dest(upT, SEQ, POOL_PAD)))
    m_proj = (ACTE.now(), DVE.now())

    class Attention:

        def __init__(self, probs, probsT, scale=1.0):
            self.probs, self.probsT, self.scale = probs, probsT, scale
            self.exp, self.turned, self.copied, self.weighted, self.out, self.inv = {}, {}, {}, {}, {}, {}

        def run(self, units):
            n = len(units)
            for s in range(n + 3):
                if 0 <= s - 2 < n:
                    self.turn(s - 2, units[s - 2])
                if s < n:
                    self.scores(s, units[s])
                if 0 <= s - 1 < n:
                    self.softmax(s - 1, units[s - 1])
                if 0 <= s - 2 < n:
                    self.copy(s - 2, units[s - 2])
                if 0 <= s - 3 < n:
                    self.values(s - 3, units[s - 3])

        @staticmethod
        def stats(s):
            return (sm[:, 8 * (s % 2) + j:8 * (s % 2) + j + 1] for j in range(4))

        def scores(self, s, u):
            PE.need(self.exp.get(s - 2))
            b = 2 * (s % 2)
            for off, n, q, k in u["scores"]:
                ins = nc.tensor.matmul(ps[:, b * 512 + off:b * 512 + off + n], q, k)
            u["scored"] = PE.sig(ins)

        def softmax(self, s, u):
            b, n = 2 * (s % 2), u["n"]
            S = ps[:, b * 512:b * 512 + n]
            neg_max, total, _, esink = self.stats(s)
            DVE.need(u["scored"])
            for off, w, bias in u.get("bias", ()):
                dst = ps[:, b * 512 + off:b * 512 + off + w]
                m = DVE.sig(nc.vector.tensor_tensor(dst, dst, bias, ALU.add))
            if u.get("bias"):
                DVE.need(m)
            DVE.need(self.exp.get(s - 2))
            m = DVE.sig(nc.vector.tensor_reduce(neg_max, S, AX, ALU.max, negate=True))
            if self.scale != 1.0:
                DVE.need(m)
                m = DVE.sig(nc.vector.tensor_scalar(neg_max, neg_max, self.scale, None, ALU.mult))
            if "sink" in u:
                DVE.need(m)
                m = DVE.sig(nc.vector.tensor_tensor(neg_max, neg_max, u["nsink"], ALU.min))
            ACTE.need(m, self.turned.get(s - 2), self.inv.get(s - 2))
            self.exp[s] = act(self.probs[s % 2][:, 0:n], S, ACT.Exp, bias=neg_max, scale=self.scale, accum_out=total)
            if "sink" in u:
                self.exp[s] = act(esink, u["sink"], ACT.Exp, bias=neg_max)

        def turn(self, s, u):
            nb = u["n"] // P
            h = (nb + 1) // 2
            PE.need(self.exp[s], *self.copied.get(s - 1, ()))
            for k in range(nb):
                ins = nc.tensor.transpose(bank(4, P, k * P) if k < h else bank(5, P, (k - h) * P),
                                          self.probs[s % 2][:, k * P:(k + 1) * P], ident[:])
            self.turned[s] = PE.sig(ins)

        def copy(self, s, u):
            n, half = u["n"], (u["n"] // P + 1) // 2 * P
            T = self.probsT[s % 2]
            _, total, inv, esink = self.stats(s)
            DVE.need(self.exp[s], self.out.get(s - 2))
            if "sink" in u:
                DVE.need(DVE.sig(nc.vector.tensor_tensor(total, total, esink, ALU.add)))
            self.inv[s] = DVE.sig(nc.vector.reciprocal(inv, total))
            DVE.need(self.turned[s], self.weighted.get(s - 2))
            c = [DVE.sig(nc.vector.tensor_copy(T[:, 0:half], bank(4, half)))]
            if half < n:
                ACTE.need(self.turned[s], self.weighted.get(s - 2))
                c.append(act(T[:, half:n], bank(5, n - half)))
            self.copied[s] = c

        def values(self, s, u):
            T, w, nb = self.probsT[s % 2], u["dh"], u["n"] // P
            PE.need(*self.copied[s], self.out.get(s - 2))
            for k in range(nb):
                ins = nc.tensor.matmul(bank(6 + s % 2, w), T[:, k * P:(k + 1) * P], u["values"][k],
                                       start=k == 0, stop=k == nb - 1)
            self.weighted[s] = PE.sig(ins)
            _, _, inv, _ = self.stats(s)
            DVE.need(self.weighted[s], self.inv[s])
            self.out[s] = DVE.sig(nc.vector.tensor_scalar(u["out"], bank(6 + s % 2, w), inv, None, ALU.mult))

    awork = region(C0)
    probs = [awork(f"probs{n}", [P, ALL]) for n in range(2)]
    probsT = [awork(f"probsT{n}", [P, ALL]) for n in range(2)]
    qs = awork("q_staged", [P, ALL])
    assert awork.end <= C0 + 16384

    def dyn(t, j, sl):
        return t[:, bass.ds(j, 1), sl].rearrange("p a n -> p (a n)")

    c_mem = [PE.n, ACTE.n, DVE.n]
    PE.need(*m_proj)
    DVE.need(*m_proj)
    ACTE.need(*m_proj, PE.now())
    n_u = NB
    with loop(MEM_HEADS, pe=3 * n_u, act=2 * n_u, dve=1 + 4 * n_u) as h:
        DVE.need(PE.now(), DVE.now())
        m = DVE.sig(nc.vector.tensor_copy(qs[:, 0:SEQ], dyn(qmT, h, slice(0, SEQ))))
        PE.need(m, ACTE.now())
        att = Attention(probs, probsT)
        att.run([dict(scores=[(0, MEM, qs[:, i * P:(i + 1) * P], dyn(kmT, h, slice(0, MEM)))], n=MEM, dh=P,
                      values=[vm[:, k, bass.ds(h * P, P)] for k in range(CB)],
                      out=om[:, i, bass.ds(h * P, P)]) for i in range(NB)])
    att_done = (ACTE.now(), DVE.now(), PE.now())

    def token_to_split(src, n_tiles, nb, hi, lo, after, gain=None, tile0=0):
        PE.need(*after)
        ACTE.need(*after)
        DVE.need(*after)
        freed = {}
        for t in range(n_tiles):
            b = t % 4
            PE.need(*freed.get(b, ()))
            for k in range(nb):
                ins = nc.tensor.transpose(bank(b, P, k * P), src[:, k, t * P:(t + 1) * P], ident[:])
            m = PE.sig(ins)
            ACTE.need(m)
            g = act(hi[:, t, :], bank(b, nb * P), scale=1.0) if gain is None else \
                act(hi[:, t, :], bank(b, nb * P), ACT.Identity, scale=gain, bias=zero1)
            DVE.need(g)
            if gain is None:
                d = DVE.sig(nc.vector.tensor_tensor(lo[:, t, :], bank(b, nb * P), f(hi[:, t, :]), ALU.subtract))
            else:
                d = DVE.sig(nc.vector.scalar_tensor_tensor(lo[:, t, :], bank(b, nb * P), gain, f(hi[:, t, :]),
                                                           ALU.mult, ALU.subtract))
            freed[b] = (g, d)
        return ACTE.now(), DVE.now()

    @owns((1, 0), (1, 0))
    def evac_gate(i, u, m):
        ACTE.need(m)
        return (act(dest(gate, SEQ)(i, u), bank(u % 4), ACT.Tanh, scale=0.5),)

    gtmp = [region(C0)("gtmp0", [P, SEQ]), region(C0 + 2048)("gtmp1", [P, SEQ])]

    def evac_branch(first, tiles=4):
        @owns((0, 2), (0, 2))
        def ev_(i, u, m):
            j = tiles * i + u
            g, x_ = (gate[:, j, :], mixT[:, j, :]) if isinstance(j, int) else \
                (dyn(gate, j, slice(0, SEQ)), dyn(mixT, j, slice(0, SEQ)))
            DVE.need(m)
            m2 = DVE.sig(nc.vector.scalar_tensor_tensor(gtmp[u % 2][:], g, 1.0, bank(u % 4), ALU.add, ALU.mult))
            DVE.need(m2)
            if first:
                DVE.sig(nc.vector.tensor_scalar(x_, gtmp[u % 2][:], 0.5, None, ALU.mult))
            else:
                DVE.sig(nc.vector.scalar_tensor_tensor(x_, gtmp[u % 2][:], 0.5, x_, ALU.mult, ALU.add))
            return (m2,)
        return ev_

    om_ready = token_to_split(om, MEM_HEADS, NB, bhi, blo, att_done)
    gemm(2, X, evac_gate, per=(4, 0), after=om_ready)
    PE.need(*om_ready)
    DVE.need(ACTE.now())
    gemm(1, [(bhi, blo, SEQ)], evac_branch(True), kt=4, cols_=512, after=(ACTE.now(), DVE.now()))
    mem_branch = (PE.now(), DVE.now())

    poolw = region(C0 + 4096)
    pw = poolw("pool_w", [P, 4, P])
    edge = poolw("pool_edge", [P, 4, POOL_PAD])
    s1 = poolw("pool_s1", [P, POOL_PAD + SEQ])
    s2 = poolw("pool_s2", [P, POOL_PAD + SEQ])
    nc.scalar.wait_ge(PE.sem, mem_branch[0].value())
    nc.scalar.wait_ge(DVE.sem, mem_branch[1].value())
    load(nc.scalar, pw[:], a["pool_w"][0].rearrange("g c d -> c g d"))
    load(nc.scalar, edge[:], a["t_pool_edge"].rearrange("p (g n) -> p g n", g=4))
    DVE.need(*mem_branch)
    DVE.sig(nc.vector.memset(upT[:, :, 0:POOL_PAD], 0.0))
    DVE.sig(nc.vector.memset(s1[:, 0:POOL_PAD], 0.0))
    DVE.need(DVE.sig(nc.vector.memset(s2[:, 0:POOL_PAD], 0.0)))
    need_inputs(DVE, PE)
    for g, w in enumerate(POOL_WINDOWS):
        cur, sh, n = upT[:, g, :], 1, 0
        while sh < w:
            nxt = (s1, s2)[n % 2]
            DVE.need(DVE.sig(nc.vector.tensor_tensor(nxt[:, POOL_PAD:], cur[:, POOL_PAD:],
                                                     cur[:, POOL_PAD - sh:POOL_PAD + SEQ - sh], ALU.add)))
            cur, sh, n = nxt, 2 * sh, n + 1
        DVE.need(DVE.sig(nc.vector.tensor_tensor(cur[:, POOL_PAD:2 * POOL_PAD], cur[:, POOL_PAD:2 * POOL_PAD],
                                                 edge[:, g, :], ALU.mult)))
        m = DVE.sig(nc.vector.scalar_tensor_tensor(upT[:, g, POOL_PAD:], cur[:, POOL_PAD:], 1.0 / w,
                                                   upT[:, g, POOL_PAD:], ALU.mult, ALU.subtract))
        DVE.need(m)
        PE.need(m)
        m = PE.sig(nc.tensor.matmul(bank(g), pw[:, g, :], upT[:, g, POOL_PAD:]))
        ACTE.need(m)
        sc = col("pool_scale", g)
        m = act(bhi[:, g, :], bank(g), ACT.Identity, scale=sc, bias=zero1)
        DVE.need(m)
        DVE.sig(nc.vector.scalar_tensor_tensor(blo[:, g, :], bank(g), sc, f(bhi[:, g, :]), ALU.mult, ALU.subtract))
    pool_ready = (ACTE.now(), DVE.now())
    ACTE.need(DVE.now())
    gemm(2, X, evac_gate, per=(4, 0), after=pool_ready)
    DVE.need(ACTE.now())
    gemm(1, [(bhi, blo, SEQ)], evac_branch(False), kt=4, cols_=512, after=(ACTE.now(), DVE.now()))

    put = region(R0 + 16384)
    qT = put("q_T", [P, DIFF_HEADS, SEQ])
    kT = put("k_T", [P, DIFF_HEADS, SEQ])
    vt = put("v_tok", [P, NB, D_MODEL])
    ao = put("attn_tok", [P, NB, D_MODEL])
    work = put
    m = (PE.now(), ACTE.now(), DVE.now())
    ACTE.need(*m)
    DVE.need(*m)
    mod_open(*m)
    gemm(2, X, evac_copy(dest(qT, SEQ), scale=DIFF_DH ** -0.5), per=(2, 6), after=m, mod=(0, 0))
    gemm(2, X, evac_copy(dest(kT, SEQ)), per=(2, 6), mod=(0, 4))
    gemm_tokens(2, [(hhi, hlo, b) for b in range(NB)], vt, lambda i, p: i * 512 + p * 256, after=m, mod=(0, 8))
    m = (PE.now(), ACTE.now(), DVE.now())
    for x_ in (PE, ACTE, DVE):
        x_.need(*m)
    awork = region(C0)
    sc2 = [awork(f"diff_s{n}", [P, 2, SEQ]) for n in range(3)]
    aT = [awork(f"diff_aT{n}", [P, SEQ]) for n in range(2)]
    qs2 = work("q2_staged", [P, 2, 2, SEQ])
    assert awork.end <= C0 + 16384
    dist = work("distance", [P, SEQ])
    assert work.end <= R_END, work.end
    load(nc.scalar, dist[:], a["t_distance"])
    need_inputs(DVE)

    DVE.sig(nc.vector.memset(qs2[:], 0.0))
    HPI = 2
    with loop(DIFF_HEADS // HPI, pe=3 * HPI * NB, act=3 * HPI * NB, dve=2 * HPI + 8 * HPI * NB) as it:
        DVE.need(PE.now(), DVE.now())
        for e in range(HPI):
            for c in range(2):
                part = slice(c * DIFF_DH, (c + 1) * DIFF_DH)
                m = DVE.sig(nc.vector.tensor_copy(qs2[part, e, c, :], qT[part, bass.ds(HPI * it + e, 1), :]
                                                  .rearrange("p a n -> p (a n)")))
        PE.need(m, ACTE.now())
        biased, expd, comb, tdone, pvd, copied, outd, scored = {}, {}, {}, {}, {}, {}, {}, {}

        def where(u):
            return u % NB, u // NB, (u % NB + 1) * P

        def scores(u):
            (i, e, n), b = where(u), 2 * (u % 2)
            PE.need(biased.get(u - 2))
            for c in range(2):
                ins = nc.tensor.matmul(bank(b + c, n), qs2[:, e, c, i * P:(i + 1) * P],
                                       dyn(kT, HPI * it + e, slice(0, n)))
            scored[u] = PE.sig(ins)

        def stats(u):
            return sm[:, 8 * (u % 3):8 * (u % 3) + 8]

        def softmax(u):
            (i, e, n), b, S, st_ = where(u), 2 * (u % 2), sc2[u % 3], stats(u)
            DVE.need(scored[u], tdone.get(u - 3), comb.get(u - 3))
            for c in range(2):
                m = DVE.sig(nc.vector.scalar_tensor_tensor(
                    S[:, c, 0:n], dist[:, (NB - 1 - i) * P:(NB - 1 - i) * P + n],
                    slopes[:, bass.ds(HPI * it + e, 1)], bank(b + c, n), ALU.mult, ALU.add))
            biased[u] = m
            DVE.need(m)
            m = DVE.sig(nc.vector.tensor_reduce(st_[:, 0:2], S[:, :, 0:n], AX, ALU.max, negate=True))
            ACTE.need(m)
            for c in range(2):
                expd[u] = act(S[:, c, 0:n], S[:, c, 0:n], ACT.Exp, bias=st_[:, c:c + 1], accum_out=st_[:, 2 + c:3 + c])

        def combine(u):
            (i, e, n), S, st_ = where(u), sc2[u % 3], stats(u)
            DVE.need(expd[u])
            m = DVE.sig(nc.vector.reciprocal(st_[:, 4:6], st_[:, 2:4]))
            DVE.need(m)
            DVE.sig(nc.vector.tensor_scalar(S[:, 0, 0:n], S[:, 0, 0:n], st_[:, 4:5], None, ALU.mult))
            m = DVE.sig(nc.vector.tensor_scalar(st_[:, 5:6], st_[:, 5:6], nlam, None, ALU.mult))
            DVE.need(m)
            comb[u] = DVE.sig(nc.vector.scalar_tensor_tensor(S[:, 0, 0:n], S[:, 1, 0:n], st_[:, 5:6], S[:, 0, 0:n],
                                                             ALU.mult, ALU.add))

        def turn(u):
            (i, e, n), S = where(u), sc2[u % 3]
            PE.need(comb[u], copied.get(u - 1))
            for k in range(i + 1):
                ins = nc.tensor.transpose(bank(4, P, k * P), S[:, 0, k * P:(k + 1) * P], ident[:])
            tdone[u] = PE.sig(ins)
            ACTE.need(tdone[u], pvd.get(u - 2))
            copied[u] = act(aT[u % 2][:, 0:n], bank(4, n))

        def values(u):
            i, e, n = where(u)
            head = HPI * it + e
            PE.need(copied[u], outd.get(u - 2))
            for k in range(i + 1):
                ins = nc.tensor.matmul(bank(6 + u % 2, P), aT[u % 2][:, k * P:(k + 1) * P],
                                       vt[:, k, bass.ds(head * P, P)], start=k == 0, stop=k == i)
            pvd[u] = PE.sig(ins)
            DVE.need(pvd[u])
            outd[u] = DVE.sig(nc.vector.tensor_copy(ao[:, i, bass.ds(head * P, P)], bank(6 + u % 2, P)))

        N_U = HPI * NB
        for s in range(N_U + 4):
            if s < N_U:
                scores(s)
            if 0 <= s - 1 < N_U:
                softmax(s - 1)
            if 0 <= s - 2 < N_U:
                combine(s - 2)
            if 0 <= s - 3 < N_U:
                turn(s - 3)
            if 0 <= s - 4 < N_U:
                values(s - 4)
    m = DVE.now()
    DVE.need(m, PE.now(), ACTE.now())
    sqt = qT[:]
    ao_h = ao[:].rearrange("p b (h d) -> p (b h) d", h=DIFF_HEADS)
    DVE.need(DVE.sig(nc.vector.tensor_tensor(qT[:].rearrange("p h n -> p (h n)"), ao[:].rearrange("p b n -> p (b n)"),
                                             ao[:].rearrange("p b n -> p (b n)"), ALU.mult)))
    hs = small[:, 96:128]
    m = DVE.sig(nc.vector.tensor_reduce(hs, qT[:].rearrange("p h (b d) -> p (h b) d", d=P), AX, ALU.add))
    ACTE.need(m)
    m = act(small[:, 128:160], hs, ACT.Sqrt, scale=1.0 / P, bias=eps)
    nc.scalar.preload_act_table(ACT.Exp)
    DVE.need(m)
    DVE.need(DVE.sig(nc.vector.reciprocal(hs, small[:, 128:160])))
    m = DVE.sig(nc.vector.tensor_tensor(ao_h, ao_h, hs.unsqueeze(2).to_broadcast([P, NB * DIFF_HEADS, P])
                                        if hasattr(hs, "to_broadcast") else
                                        bass.AP(tensor=hs.tensor, offset=hs.offset, ap=[*hs.ap, [0, P]]), ALU.mult))
    put = region(R0 + 16384)
    ahi, alo = put("a_hi", [P, DT, SEQ], F32R), put("a_lo", [P, DT, SEQ], F32R)
    a_ready = token_to_split(ao, DT, NB, ahi, alo, (m, ACTE.now()), gain=subg)
    gate = region(R0 + 16384 + 2 * 16384)("gate_attn", [P, DT, SEQ])
    gemm(2, X, evac_gate, per=(4, 0), after=a_ready)
    DVE.need(ACTE.now())
    gemm(2, [(ahi, alo, SEQ)], evac_branch(False), per=(0, 8), after=(ACTE.now(), DVE.now()))
    m = (PE.now(), ACTE.now(), DVE.now())

    def split_tiles(src, hi, lo, n, after):
        ACTE.need(*after)
        DVE.need(*after)
        for t in range(n):
            split(hi[:, t, :], lo[:, t, :], src[:, t, :], None)
        return ACTE.now(), DVE.now()

    def add_normed(y, gain_name, after, tag):
        w = region(C0)
        sq = [w(f"sq{n}{tag}", [P, SEQ]) for n in range(2)]
        dg = w("dg" + tag, [P, SEQ])
        tmp = [w(f"t{n}{tag}", [P, SEQ]) for n in range(2)]
        m = col_stats(lambda t: y[:, t, :], DT, SEQ, sq, after)
        m = spread_cols(SEQ, dg, m)
        DVE.need(m)
        scaled, ready = {}, []
        for t in range(DT + 1):
            if t < DT:
                DVE.need(ready[t - 2] if t >= 2 else None)
                scaled[t] = DVE.sig(nc.vector.scalar_tensor_tensor(tmp[t % 2][:], y[:, t, :], col(gain_name, t), bank(6),
                                                                   ALU.mult, ALU.mult))
            if t:
                DVE.need(scaled[t - 1])
                ready.append(DVE.sig(nc.vector.tensor_tensor(xT[:, t - 1, :], xT[:, t - 1, :], tmp[(t - 1) % 2][:],
                                                             ALU.add)))
        return ready

    mx_ready = split_tiles(mixT, ahi, alo, DT, m)
    yT = region(R0)("y_T", [P, DT, SEQ])
    PE.need(*mx_ready)
    ACTE.need(*mx_ready)
    gemm(2, [(ahi, alo, SEQ)], evac_copy(dest(yT, SEQ)), per=(2, 2), after=mx_ready)
    x_tiles = add_normed(yT, "norm_mix_post", (PE.now(), ACTE.now(), DVE.now()), "_mix")

    h2 = norm_split(xT, SEQ, hhi, hlo, lambda t: col("norm_ffn_pre", t), region(R0 + 20480), (),
                    ready=x_tiles, bank_=5)
    put = region(R0)
    fhi, flo = put("f_hi", [P, FT, SEQ], F32R), put("f_lo", [P, FT, SEQ], F32R)
    assert put.end <= R_END, (put.end, R_END)
    cw = region(C0)
    cbuf = [cw(f"conv{n}", [P, SEQ]) for n in range(4)]
    gel = [cw(f"gel{n}", [P, SEQ]) for n in range(2)]
    ACTE.need(h2[-1])
    nc.scalar.preload_act_table(ACT.Gelu_apprx_tanh)

    conv_marks = {}

    def evac_ffn(i, u, m):
        t = 2 * i + u % 2 + (FT if u >= 2 else 0)
        w = cbuf[u]
        ACTE.need(m, DVE.now().minus(12 - (4 if u >= 2 else 2)), ACTE.now().minus(8 - 2))
        g = act(w[:], bank(u), ACT.Identity, scale=dyn_col("conv_w", t + 2 * 2 * FT), bias=dyn_col("conv_b", t))
        DVE.need(g)
        g = DVE.sig(nc.vector.scalar_tensor_tensor(w[:, 1:], bank(u, SEQ - 1), dyn_col("conv_w", t + 2 * FT), w[:, 1:],
                                                   ALU.mult, ALU.add))
        DVE.need(g)
        g = DVE.sig(nc.vector.scalar_tensor_tensor(w[:, 2:], bank(u, SEQ - 2), dyn_col("conv_w", t), w[:, 2:],
                                                   ALU.mult, ALU.add))
        if u < 2:
            ACTE.need(g, conv_marks["start"].minus(12 - (7 if u == 0 else 11)))
            conv_marks[u] = act(gel[u][:], w[:], ACT.Gelu_apprx_tanh)
            return (g,)
        DVE.need(g, conv_marks[u - 2])
        p_ = DVE.sig(nc.vector.tensor_tensor(w[:], w[:], gel[u - 2][:], ALU.mult))
        j = 2 * i + (u - 2)
        ACTE.need(p_)
        q_ = act(dyn(fhi, j, slice(0, SEQ)), w[:])
        DVE.need(q_)
        DVE.sig(nc.vector.tensor_tensor(dyn(flo, j, slice(0, SEQ)), w[:], f(dyn(fhi, j, slice(0, SEQ))), ALU.subtract))
        return (g,)

    base_chunk = chunk[0]
    with loop(D_FF // 256, pe=4, act=8, dve=12) as i:
        conv_marks["start"] = DVE.now()
        for p in range(2):
            PE.e.wait_ge(lo_done, base_chunk + p + 1 + 2 * i)
            hi = whi[p][:].rearrange("p (k n) -> p k n", k=DT)
            lo = wlo[p][:].rearrange("p (k n) -> p k n", k=DT)
            for o in range(2):
                PE.need(DVE.now().minus(12 - 2))
                for k in range(DT):
                    if p == 0 and o == 0:
                        PE.need(h2[k])
                    ins = mm3(bank(2 * p + o), hi[:, k, o * P:(o + 1) * P], lo[:, k, o * P:(o + 1) * P],
                              hhi[:, k, :], hlo[:, k, :], k == 0, k == DT - 1)
                m = PE.sig(ins)
                evac_ffn(i, 2 * p + o, m)
            ACTE.need(m)
            round_hi(p, base_chunk + p + 2, i, 2)
    chunk[0] += D_FF // 128
    nc.scalar.preload_act_table(ACT.Exp)

    ydn = nc.alloc_sbuf_tensor_at("y_down", [P, DT, SEQ], F32, offset=C0 - 2 * 16384)
    cin = nc.alloc_sbuf_tensor_at("ctx_in", [P, CB, D_MODEL], F32, offset=C0 - 16384)
    m = (PE.now(), ACTE.now(), DVE.now())
    nc.scalar.wait_ge(PE.sem, PE.n)
    load(nc.scalar, cin[:], a["ctx_2"][0].rearrange("(b p) d -> p b d", p=P))
    c_landed = landed[0]
    for x_ in (PE, ACTE, DVE):
        x_.need(*m)
    mod_open(*m)
    base_chunk = chunk[0]
    with loop(2, pe=6, act=2, dve=2 + 12) as i:
        before = (ACTE.now(), DVE.now())
        mod_free = [DVE.now()] * 2
        PE.need(*before)
        for q in range(6):
            g, kk = divmod(q, 3)
            p = q % 2
            kt = min(8, FT - 8 * kk)
            PE.e.wait_ge(lo_done, base_chunk + q + 1 + 6 * i)
            hi = whi[p][:, 0:kt * 256].rearrange("p (k n) -> p k n", k=kt)
            lo = wlo[p][:, 0:kt * 256].rearrange("p (k n) -> p k n", k=kt)
            for o in range(2):
                for k in range(kt):
                    kf = 8 * kk + k
                    ins = mm3(bank(2 * g + o), hi[:, k, o * P:(o + 1) * P], lo[:, k, o * P:(o + 1) * P],
                              fhi[:, kf, :], flo[:, kf, :], kf == 0, kf == FT - 1)
            m = PE.sig(ins)
            mod_free[q % 2] = mod_product(1, q, i, 6, mod_free[q % 2])
            ACTE.need(m)
            round_hi(p, base_chunk + q + 2, i, 6)
            if kk == 2:
                for o in range(2):
                    dst = dyn(ydn, 4 * i + 2 * g + o, slice(0, SEQ))
                    if o:
                        act(dst, bank(2 * g + o))
                    else:
                        DVE.need(m)
                        DVE.sig(nc.vector.tensor_copy(dst, bank(2 * g + o)))
    chunk[0] += 12
    m = (PE.now(), ACTE.now(), DVE.now())
    cT = nc.alloc_sbuf_tensor_at("ctx_T", [P, DT, CTX], F32, offset=R0)
    for x_ in (ACTE, DVE):
        x_.need(*m)
    PE.e.wait_ge(sem_in, c_landed)
    c_ready = to_feature_major(cin, CB, cT, m, banks=(4, 5))
    x_tiles = add_normed(ydn, "norm_ffn_post", m, "_ffn")

    put = region(R0 + 4 * DT * CTX)
    k3 = {}
    qT3 = {x_: put(f"q_{x_}", [P, 4, ALL]) for x_ in "AB"}
    kk_ = {x_: put(f"k_{x_}", [P, ALL]) for x_ in "AB"}
    v3 = {x_: put(f"v_{x_}", [P, ALL // P, P]) for x_ in "AB"}
    probs2 = [put(f"probs2_{n}", [P, ALL]) for n in range(2)]
    probsT2 = [put(f"probsT2_{n}", [P, ALL]) for n in range(2)]
    ao2 = put("attn2_tok", [P, ALL // P, D_MODEL])
    rest = put.end
    assert rest <= R_END, (rest, R_END)
    gs = nc.alloc_sbuf_tensor_at("gain_scale", [P, 4, DT], F32, offset=(small_off := None) or base[0]) if False else None
    gsc = small[:, 160:192].rearrange("p (n t) -> p n t", n=4)

    def mod(layer, part, cond_):
        return modT[:, layer, part * DT:(part + 1) * DT, cond_]

    DVE.need(DVE.now())
    for layer in range(2):
        for cn in range(2):
            g0 = places["norm_g_2"] + layer * DT
            gm = DVE.sig(nc.vector.scalar_tensor_tensor(gsc[:, 2 * layer + cn, :], mod(layer, 1, cn), 1.0,
                                                        cols[:, g0:g0 + DT], ALU.add, ALU.mult))

    def modulated(layer, after, ready):
        hr = norm_split(xT, SEQ, hhi, hlo, lambda t: gsc[:, 2 * layer, t:t + 1], region(rest - 6 * 4096),
                        (*after, gm), lambda t: modT[:, layer, t, 0:1], ready=ready, bank_=5)
        cr = norm_split(cT, CTX, chi, clo, lambda t: gsc[:, 2 * layer + 1, t:t + 1], region(rest - 6 * 4096 + 12288),
                        (), lambda t: modT[:, layer, t, 1:2])
        return hr, cr

    hx, hc = modulated(0, c_ready, x_tiles)

    def evac_q2(i, u, m):
        raise NotImplementedError

    def evac_both(dst, scale):
        def ev_(i, u, m):
            ACTE.need(m)
            DVE.need(m)
            return (act(dst[:, u, CTX:], bank(u), scale=scale),
                    DVE.sig(nc.vector.tensor_scalar(dst[:, u, 0:CTX], bank(4 + u, CTX), scale, None, ALU.mult)))
        return ev_

    gemm(1, XC, evac_both(qT3["A"], 1.0), ready=[hx, hc])
    m = (ACTE.now(), DVE.now())
    gemm(1, XC, evac_both(qT3["B"], HEAD ** -0.5), after=m)
    m = (ACTE.now(), DVE.now())
    PE.need(*m)
    kv_freed = m
    for p, x_ in enumerate("AB"):
        PE.e.wait_ge(lo_done, chunk[0] + p + 1)
        hi = whi[p][:].rearrange("p (k n) -> p k n", k=DT)
        lo = wlo[p][:].rearrange("p (k n) -> p k n", k=DT)
        for n, (xh, xl, tok) in enumerate(XC):
            for k in range(DT):
                ins = mm3(bank(4 * n, tok), hi[:, k, 0:P], lo[:, k, 0:P], xh[:, k, 0:tok], xl[:, k, 0:tok],
                          k == 0, k == DT - 1)
        blocks = [(chi, clo, b) for b in range(CB)] + [(hhi, hlo, b) for b in range(NB)]
        for n, (xh, xl, blk) in enumerate(blocks):
            ts = slice(blk * P, (blk + 1) * P)
            b = (1, 2, 3, 5, 6, 7)[n]
            for k in range(DT):
                ins = mm3(bank(b, P), hi[:, k, P:2 * P], lo[:, k, P:2 * P], xh[:, k, ts], xl[:, k, ts],
                          k == 0, k == DT - 1, flip=True)
        m = PE.sig(ins)
        ACTE.need(m)
        DVE.need(m)
        act(kk_[x_][:, CTX:], bank(0))
        DVE.sig(nc.vector.tensor_copy(kk_[x_][:, 0:CTX], bank(4, CTX)))
        for n in range(6):
            b = (1, 2, 3, 5, 6, 7)[n]
            if n % 2:
                act(v3[x_][:, n, :], bank(b, P))
            else:
                DVE.sig(nc.vector.tensor_copy(v3[x_][:, n, :], bank(b, P)))
        round_hi(p, chunk[0] + p + 2)
        PE.need(ACTE.now(), DVE.now())
    chunk[0] += 2

    t2 = region(rest - 6 * 4096)
    gat = t2("head_gather", [P, 5, 10])
    spr = t2("head_spread", [P, 5, P])
    rms10 = t2("rms10", [P, ALL])
    inv10 = t2("inv10", [P, ALL])
    sqa = [t2(f"sqa{n}", [P, ALL]) for n in range(2)]
    cosT = t2("cos_T", [P, SEQ])
    sinT = t2("sin_T", [P, SEQ])
    rotm = t2("rotate", [P, P])
    assert t2.end <= rest + 0, (t2.end, rest)
    nc.scalar.wait_ge(DVE.sem, DVE.n)
    nc.scalar.wait_ge(PE.sem, PE.n)
    load(nc.scalar, gat[:], a["t_head_gather"].rearrange("p (n c) -> p n c", n=5))
    load(nc.scalar, spr[:], a["t_head_spread"].rearrange("p (n c) -> p n c", n=5))
    load(nc.scalar, cosT[:], a["t_rope_cos"])
    load(nc.scalar, sinT[:], a["t_rope_sin"])
    load(nc.scalar, rotm[:], a["t_rotate"])
    need_inputs(PE, DVE)
    tiles = [qT3["A"][:, n, :] for n in range(4)] + [kk_["A"][:]]
    ACTE.need(DVE.now())
    used = {}
    for n, tl in enumerate(tiles):
        ACTE.need(used.get(n - 2))
        m = act(sqa[n % 2][:], tl, ACT.Square)
        PE.need(m)
        nc.tensor.matmul(bank(4, 512, 0, 10), gat[:, n, :], sqa[n % 2][:, 0:512], start=n == 0, stop=n == 4)
        used[n] = PE.sig(nc.tensor.matmul(bank(5, 256, 0, 10), gat[:, n, :], sqa[n % 2][:, 512:ALL],
                                          start=n == 0, stop=n == 4))
    ACTE.need(used[4])
    m = act(rms10[0:10, :], ps[0:10, 4 * 512:4 * 512 + ALL], ACT.Sqrt, bias=eps[0:10], scale=1.0)
    nc.scalar.preload_act_table(ACT.Exp)
    DVE.need(m)
    m = DVE.sig(nc.vector.reciprocal(inv10[0:10, :], rms10[0:10, :]))
    PE.need(m)
    fr = {}
    for n, tl in enumerate(tiles):
        b = 2 * (n % 2)
        PE.need(fr.get(n - 2))
        nc.tensor.matmul(bank(b), spr[0:10, n, :], inv10[0:10, 0:512])
        m = PE.sig(nc.tensor.matmul(bank(b + 1, 256), spr[0:10, n, :], inv10[0:10, 512:ALL]))
        DVE.need(m)
        gcol = qgain if n < 4 else col("a_k_gain_2")
        fr[n] = DVE.sig(nc.vector.scalar_tensor_tensor(tl, tl, gcol, ps[:, b * 512:b * 512 + ALL], ALU.mult, ALU.mult))
    tiles = tiles + [qT3["B"][:, n, :] for n in range(4)] + [kk_["B"][:]]
    PE.need(DVE.now(), ACTE.now())
    ACTE.need(PE.now())
    DVE.need(ACTE.now())
    fr = {}
    for n, tl in enumerate(tiles):
        b = n % 2
        s = tl[:, CTX:]
        PE.need(fr.get(n - 2))
        m = PE.sig(nc.tensor.matmul(bank(b), rotm[:], s))
        DVE.need(m)
        g = DVE.sig(nc.vector.tensor_tensor(sqa[n % 2][:, 0:SEQ], bank(b), sinT[:], ALU.mult))
        fr[n] = g
        DVE.need(DVE.sig(nc.vector.tensor_tensor(s, s, cosT[:], ALU.mult)), g)
        DVE.sig(nc.vector.tensor_tensor(s, s, sqa[n % 2][:, 0:SEQ], ALU.add))
    m = (DVE.now(), ACTE.now(), PE.now())
    for x_ in (PE, ACTE, DVE):
        x_.need(*m)

    tail = region(rest)
    qst = [tail(f"q3_staged{n}", [P, ALL]) for n in range(2)]
    bl, br = tail("band_left", [P, P]), tail("band_right", [P, P])
    assert tail.end <= R_END, tail.end - R_END
    nc.scalar.wait_ge(DVE.sem, DVE.n)
    load(nc.scalar, bl[:], a["t_band_left"])
    load(nc.scalar, br[:], a["t_band_right"])
    need_inputs(DVE)

    def q_units(x_, kv, j, s):
        K = kk_[x_]
        us = []
        head = 4 * kv + 2 * j + s
        c0 = (0 if x_ == "A" else 512) + (2 * kv + j) * P + s * HEAD
        V = v3[x_]
        vs = slice(kv * HEAD, (kv + 1) * HEAD)
        extra = {} if x_ == "A" else dict(sink=sink[:, bass.ds(head, 1)], nsink=nsink[:, bass.ds(head, 1)])
        for i in range(NB):
            q = qst[s][:, CTX + i * P:CTX + (i + 1) * P]
            if x_ == "A":
                sc = [(0, 512, q, K[:, 0:512]), (512, 256, q, K[:, 512:ALL])]
                us.append(dict(scores=sc, n=ALL, values=[V[:, k, vs] for k in range(6)]))
            else:
                b0, b1 = max(i - 1, 0), min(i + 2, NB)
                w = (b1 - b0) * P
                k0 = CTX + b0 * P
                w1 = min(w, 256)
                sc = [(0, CTX, q, K[:, 0:CTX]), (CTX, w1, q, K[:, k0:k0 + w1])]
                if w > w1:
                    sc.append((CTX + w1, w - w1, q, K[:, k0 + w1:k0 + w]))
                bias = []
                if i > 0:
                    bias.append((CTX, P, bl[:]))
                if i < NB - 1:
                    bias.append((CTX + w - P, P, br[:]))
                us.append(dict(scores=sc, n=CTX + w, bias=bias,
                               values=[V[:, k, vs] for k in (0, 1, *range(CB + b0, CB + b1))]))
            us[-1]["out"] = ao2[:, CB + i, bass.ds(c0, HEAD)]
        for i in range(CB):
            q = qst[s][:, i * P:(i + 1) * P]
            us.append(dict(scores=[(0, CTX, q, K[:, 0:CTX])], n=CTX,
                           values=[V[:, k, vs] for k in range(CB)], out=ao2[:, i, bass.ds(c0, HEAD)]))
        for u_ in us:
            u_.update(dh=HEAD, **extra)
        return us

    for x_ in "AB":
        for kv in range(2):
            dummy_counts = dict(A=(36, 24, 2 + 12 * 4), B=(36, 36, 2 + 12 * 6 + 2 * 6))[x_]
            DVE.need(PE.now(), DVE.now())
            DVE.sig(nc.vector.memset(qst[0][(1 - kv) * HEAD:(2 - kv) * HEAD, :], 0.0))
            DVE.sig(nc.vector.memset(qst[1][(1 - kv) * HEAD:(2 - kv) * HEAD, :], 0.0))
            with loop(2, pe=dummy_counts[0], act=dummy_counts[1], dve=dummy_counts[2]) as j:
                DVE.need(PE.now(), DVE.now())
                for s in range(2):
                    m = DVE.sig(nc.vector.tensor_copy(
                        qst[s][kv * HEAD:(kv + 1) * HEAD, :],
                        qT3[x_][s * HEAD:(s + 1) * HEAD, bass.ds(2 * kv + j, 1), :].rearrange("p a n -> p (a n)")))
                PE.need(m, ACTE.now())
                DVE.need(m)
                Attention(probs2, probsT2).run(q_units(x_, kv, j, 0) + q_units(x_, kv, j, 1))
    m = (DVE.now(), ACTE.now(), PE.now())
    for x_ in (PE, ACTE, DVE):
        x_.need(*m)

    put = region(R0 + 8192)
    nmix = 4
    ghi, glo = put("g_hi", [P, DT, ALL], F32R), None
    gw = region(C0 if False else rest)
    silu_t = [gw(f"silu{n}", [P, ALL]) for n in range(2)]
    assert gw.end <= R_END
    glo_at = put.end
    assert glo_at + 4 * DT * ALL <= rest - 4 * 6 * D_MODEL
    glo = nc.alloc_sbuf_tensor_at("g_lo", [P, DT, ALL], F32R, offset=glo_at) 

    def gated(tile_base, n_blocks, ao_, xs, hi_, lo_, tile_of, silu_, prod_):
        tot = n_blocks * P
        for p in range(2):
            PE.e.wait_ge(lo_done, chunk[0] + p + 1)
            hi = whi[p][:].rearrange("p (k n) -> p k n", k=DT)
            lo = wlo[p][:].rearrange("p (k n) -> p k n", k=DT)
            for o in range(2):
                u = 2 * p + o
                t = tile_base + u
                b = 4 * (u % 2)
                PE.need(gf.get(u % 2))
                pos = 0
                for n, (xh, xl, tok) in enumerate(xs):
                    for k in range(DT):
                        ins = mm3(bank(b + n, tok), hi[:, k, o * P:(o + 1) * P], lo[:, k, o * P:(o + 1) * P],
                                  xh[:, k, 0:tok], xl[:, k, 0:tok], k == 0, k == DT - 1)
                for k in range(n_blocks):
                    c, off = (b + 3, k * P) if n_blocks > NB and k < CB else (b + 2, (k - (n_blocks - NB)) * P)
                    ins = nc.tensor.transpose(bank(c, P, off), ao_[:, k, t * P:(t + 1) * P], ident[:])
                m = PE.sig(ins)
                ACTE.need(m, gf.get(u % 2))
                parts = [(tot - SEQ, SEQ, b, b + 2)] + ([(0, CTX, b + 1, b + 3)] if tot > SEQ else [])
                S_, R_ = silu_[u % 2], prod_[u % 2]
                for off, n, gb, ab in parts:
                    g = act(S_[:, off:off + n], bank(gb, n), ACT.Tanh, scale=0.5)
                DVE.need(g)
                for off, n, gb, ab in parts:
                    g = DVE.sig(nc.vector.scalar_tensor_tensor(S_[:, off:off + n], S_[:, off:off + n], 1.0, bank(gb, n),
                                                               ALU.add, ALU.mult))
                DVE.need(g)
                for off, n, gb, ab in parts:
                    g = DVE.sig(nc.vector.scalar_tensor_tensor(R_[:, off:off + n], S_[:, off:off + n], 0.5, bank(ab, n),
                                                               ALU.mult, ALU.mult))
                _, gf[u % 2] = split(hi_[:, tile_of(u), :], lo_[:, tile_of(u), :], R_[:, 0:tot], g)
            ACTE.need(m)
            round_hi(p, chunk[0] + p + 2)
        chunk[0] += 2

    gf = {}
    gated(0, 6, ao2, XC, ghi, glo, lambda u: u, silu_t, silu_t)
    gated(4, 6, ao2, XC, ghi, glo, lambda u: 4 + u, silu_t, silu_t)
    m = (DVE.now(), ACTE.now(), PE.now())
    ACTE.need(*m)

    def evac_residual(layer, ctx):
        @owns(*[(0, 1 + ctx)] * 2)
        def ev_(i, u, m):
            j = 4 * i + u
            DVE.need(m)
            mf = modT[:].rearrange("p l t c -> p (l t) c")
            gl = mf[:, bass.ds(layer * 24 + 16 + j, 1), 0]
            r = [DVE.sig(nc.vector.scalar_tensor_tensor(dyn(xT, j, slice(0, SEQ)), bank(u), gl,
                                                        dyn(xT, j, slice(0, SEQ)), ALU.mult, ALU.add))]
            if ctx:
                gc = mf[:, bass.ds(layer * 24 + 16 + j, 1), 1]
                r.append(DVE.sig(nc.vector.scalar_tensor_tensor(dyn(cT, j, slice(0, CTX)), bank(4 + u, CTX), gc,
                                                                dyn(cT, j, slice(0, CTX)), ALU.mult, ALU.add)))
            return tuple(r)
        return ev_

    class Tail:

        def __init__(self, t, lo_):
            self.t, self.lo_ = t, lo_

        def __getitem__(self, k):
            a_, b_, c_ = k
            return self.t[a_, b_, self.lo_ + c_.start:self.lo_ + c_.stop]

    gemm(2, [(Tail(ghi, CTX), Tail(glo, CTX), SEQ), (Tail(ghi, 0), Tail(glo, 0), CTX)],
         evac_residual(0, True), per=(0, 8), after=m)
    m = (DVE.now(), ACTE.now(), PE.now())
    for x_ in (PE, ACTE, DVE):
        x_.need(*m)

    hx, hc = modulated(1, m, None)
    PADC = CONV_TAPS // 2
    put = region(R0)
    uT = put("u_T", [P, CT, SEQ + 2 * PADC + 2])
    yc = put("conv_y", [P, CT, SEQ])
    dq = put("dq_T", [P, 4, SEQ])
    dk = put("dk_T", [P, 4, ALL])
    dv = put("dv", [P, ALL // P, 512])
    aod = put("attn3_tok", [P, NB, 512])
    oend = put.end
    utmp = [put(f"u_tmp{n}", [P, SEQ]) for n in range(2)]
    DVE.sig(nc.vector.memset(uT[:, :, 0:PADC], 0.0))
    DVE.sig(nc.vector.memset(uT[:, :, PADC + SEQ:], 0.0))
    u_marks = {}

    def evac_u(i, u, m):
        t = 2 * i + u % 2
        if u < 2:
            DVE.need(m)
            u_marks[u] = DVE.sig(nc.vector.tensor_copy(uT[:, t, PADC:PADC + SEQ], bank(u)))
            return (u_marks[u],)
        ACTE.need(m, u_marks.get("free%d" % u))
        g = act(utmp[u - 2][:], bank(u), ACT.Tanh, scale=0.5)
        DVE.need(g, u_marks[u - 2])
        w = uT[:, t, PADC:PADC + SEQ]
        DVE.need(DVE.sig(nc.vector.scalar_tensor_tensor(w, utmp[u - 2][:], 1.0, w, ALU.add, ALU.mult)))
        u_marks["free%d" % u] = DVE.sig(nc.vector.tensor_scalar(w, w, 0.5, None, ALU.mult))
        return (g,)

    gemm(2, X, evac_u, unroll=True, ready=[hx])
    u_ready = DVE.now()
    def evac_act(dst_of, scale=1.0):
        def ev_(i, u, m):
            ACTE.need(m)
            return (act(dst_of(i, u), bank(u % 4, dst_of.n), scale=scale),)
        return ev_

    def evac_both_act(dst):
        def ev_(i, u, m):
            ACTE.need(m)
            act(dst[:, u, CTX:], bank(u))
            return (act(dst[:, u, 0:CTX], bank(4 + u, CTX)),)
        return ev_

    gemm(1, X, evac_act(dest(dq, SEQ), HEAD ** -0.5), after=(ACTE.now(), u_ready))
    gemm(1, XC, evac_both_act(dk), ready=[hx, hc])
    blocks = [(chi, clo, b) for b in range(CB)] + [(hhi, hlo, b) for b in range(NB)]
    gemm_tokens(1, blocks, dv, lambda i, p: p * 256, after=(ACTE.now(),), only_act=True)
    DVE.need(u_ready)
    conv_ready = []
    for n in range(CONV_TAPS):
        for t in range(CT):
            wcol = col("c_dw_w_2", n * CT + t)
            src = uT[:, t, n:n + SEQ]
            if n:
                DVE.need(conv_ready[t])
                g = DVE.sig(nc.vector.scalar_tensor_tensor(yc[:, t, :], src, wcol, yc[:, t, :], ALU.mult, ALU.add))
                conv_ready[t] = g
            else:
                conv_ready.append(DVE.sig(nc.vector.tensor_scalar(yc[:, t, :], src, wcol, col("c_dw_b_2", t),
                                                                  ALU.mult, ALU.add)))
    m = (PE.now(), ACTE.now(), DVE.now())
    for x_ in (PE, ACTE, DVE):
        x_.need(*m)

    lw = region(C0)
    sqc = [lw(f"lsq{n}", [P, SEQ]) for n in range(2)]
    mean = lw("mean", [P, SEQ])
    dgl = lw("dg_ln", [P, SEQ])
    for t in range(CT):
        ins = nc.tensor.matmul(bank(0), ones[:], yc[:, t, :], start=t == 0, stop=t == CT - 1)
    m = PE.sig(ins)
    ACTE.need(m)
    m = act(mean[:], bank(0), scale=1.0 / 512)
    DVE.need(m)
    for t in range(CT):
        m = DVE.sig(nc.vector.tensor_tensor(yc[:, t, :], yc[:, t, :], mean[:], ALU.subtract))
    m = col_stats(lambda t: yc[:, t, :], CT, SEQ, sqc, (m,), dim=512)
    m = spread_cols(SEQ, dgl, m)
    DVE.need(m)
    fr = {}
    for t in range(CT):
        y_ = yc[:, t, :]
        DVE.need(DVE.sig(nc.vector.scalar_tensor_tensor(y_, y_, col("c_ln_g_2", t), bank(6), ALU.mult, ALU.mult)))
        m = DVE.sig(nc.vector.tensor_scalar(y_, y_, col("c_ln_b_2", t), None, ALU.add))
        ACTE.need(m, fr.get(t - 2))
        m2 = act(sqc[t % 2][:], y_, ACT.Tanh, scale=0.5)
        DVE.need(m, m2)
        fr[t] = DVE.sig(nc.vector.scalar_tensor_tensor(y_, sqc[t % 2][:], 1.0, y_, ALU.add, ALU.mult))
        DVE.need(fr[t])
        DVE.sig(nc.vector.tensor_scalar(y_, y_, 0.5, None, ALU.mult))
    m = (PE.now(), ACTE.now(), DVE.now())
    for x_ in (PE, ACTE, DVE):
        x_.need(*m)

    SLOTS = 2 * NA_KH - 2
    W2 = SLOTS * GRID_W
    aw = region(C0)
    probs3 = [aw(f"probs3_{n}", [P, ALL]) for n in range(2)]
    qst3 = [aw(f"q4_staged{n}", [P, SEQ]) for n in range(2)]
    nmask = aw("near_mask", [P, GRID_W])
    rv = aw("reverse", [P, P])
    assert aw.end <= C0 + 16384, aw.end - C0
    bw = region(oend)
    grev = [bw(f"bias_reversed{n}", [P, W2]) for n in range(2)]
    gbias = [bw(f"bias{n}", [P, W2]) for n in range(2)]
    probsT3 = [bw(f"probsT3_{n}", [P, ALL]) for n in range(2)]
    assert bw.end <= R_END, bw.end - R_END
    nc.scalar.wait_ge(DVE.sem, DVE.n)
    nc.scalar.wait_ge(PE.sem, PE.n)
    load(nc.scalar, nmask[:], a["t_near_mask"])
    load(nc.scalar, rv[:], a["t_reverse"])
    need_inputs(PE, DVE)
    sem_bias = [nc.alloc_semaphore(f"bias_landed{n}") for n in range(2)]
    LB = 2 * GRID_W - 1
    rp = a["rpb_padded"]
    for s in range(2):
        DVE.sig(nc.vector.memset(qst3[s][:], 0.0))
    read_bias = {}

    def load_bias(j):
        for s in range(2):
            head = 2 * j + s
            if head >= 2:
                nc.scalar.wait_ge(PE.sem, read_bias[head - 2].at)
            for half in range(2):
                src = bass.AP(tensor=rp.tensor, offset=rp.offset + (head * (2 * NA_KH - 1) + 1 - half) * LB,
                              ap=[[1, GRID_W], [LB, SLOTS], [1, GRID_W]])
                nc.scalar.dma_start(grev[s][half * 64:(half + 1) * 64, :].rearrange("p (d k) -> p d k", k=GRID_W),
                                    src).then_inc(sem_bias[s], 16)

    def turn_bias(j):
        for s in range(2):
            head = 2 * j + s
            PE.e.wait_ge(sem_bias[s], 32 * (j + 1))
            PE.need(DVE.now(), ACTE.now())
            n = W2 // 2
            nc.tensor.matmul(bank(2 * s, n), rv[:], grev[s][:, 0:n])
            read_bias[head] = PE.sig(nc.tensor.matmul(bank(2 * s + 1, n), rv[:], grev[s][:, n:W2]))
            DVE.need(read_bias[head])
            for b in range(2):
                dst = gbias[s][:, b * n:(b + 1) * n].rearrange("p (d k) -> p d k", k=GRID_W)
                mk = bass.AP(tensor=nmask[:].tensor, offset=nmask[:].offset,
                             ap=[list(nmask[:].ap[0]), [0, n // GRID_W], [1, GRID_W]])
                m = DVE.sig(nc.vector.tensor_tensor(dst, bank(2 * s + b, n).rearrange("p (d k) -> p d k", k=GRID_W),
                                                    mk, ALU.add))
        return m

    load_bias(0)
    for j in range(4):
        m = turn_bias(j)
        if j < 3:
            load_bias(j + 1)
        DVE.need(PE.now(), DVE.now())
        for s in range(2):
            part = slice(s * HEAD, (s + 1) * HEAD)
            m0 = DVE.sig(nc.vector.tensor_copy(qst3[s][part, :], dq[part, j, :]))
        DVE.need(m)
        PE.need(m, m0)
        us = []
        for s in range(2):
            c0 = j * P + s * HEAD
            for i in range(NB):
                q = qst3[s][:, i * P:(i + 1) * P]
                k0 = (NA_KH - 2 - 2 * i) * GRID_W
                bias = gbias[s][:, k0:k0 + SEQ]
                us.append(dict(scores=[(0, 512, q, dk[:, j, 0:512]), (512, 256, q, dk[:, j, 512:ALL])], n=ALL,
                               bias=[(CTX, SEQ, bias)], dh=HEAD, out=aod[:, i, c0:c0 + HEAD],
                               values=[dv[:, k, c0:c0 + HEAD] for k in range(6)]))
        Attention(probs3, probsT3).run(us)
    m = (PE.now(), ACTE.now(), DVE.now())
    for x_ in (PE, ACTE, DVE):
        x_.need(*m)

    ow = region(R0 + 8 * 2048 + 2304)
    ohi, olo = ow("o_hi", [P, DT, SEQ], F32R), ow("o_lo", [P, DT, SEQ], F32R)
    cg = region(C0)
    sg = [cg(f"sg{n}", [P, SEQ]) for n in range(2)]
    pg = [cg(f"pg{n}", [P, SEQ]) for n in range(2)]
    aod2 = nc.alloc_sbuf_tensor_at("attn3_moved", [P, NB, 512], F32, offset=ow.end + 8192)
    m = DVE.sig(nc.vector.tensor_copy(aod2[:], aod[:]))
    for x_ in (PE, ACTE, DVE):
        x_.need(m)
    fr = {}

    def evac_conv_gate(i, u, m):
        ACTE.need(m, fr.get(u - 2))
        g = act(sg[u % 2][:], bank(u), ACT.Tanh, scale=0.5)
        DVE.need(g)
        g = DVE.sig(nc.vector.scalar_tensor_tensor(sg[u % 2][:], sg[u % 2][:], 1.0, bank(u), ALU.add, ALU.mult))
        DVE.need(g)
        g2 = DVE.sig(nc.vector.scalar_tensor_tensor(pg[u % 2][:], sg[u % 2][:], 0.5, yc[:, u, :], ALU.mult, ALU.mult))
        _, fr[u] = split(ohi[:, u, :], olo[:, u, :], pg[u % 2][:], g2)
        return (g,)

    gemm(1, X, evac_conv_gate)
    m = (PE.now(), ACTE.now(), DVE.now())
    for x_ in (PE, ACTE, DVE):
        x_.need(*m)
    gf = {}

    class Shift:
        def __init__(self, t):
            self.t = t

        def __getitem__(self, k):
            a_, b_, c_ = k
            return self.t[a_, b_, c_]

    gated_base = 0
    gated(0, NB, aod2, X, ohi, olo, lambda u: 4 + u, sg, pg)
    m = (PE.now(), ACTE.now(), DVE.now())
    gemm(2, [(ohi, olo, SEQ)], evac_residual(1, False), per=(0, 4), after=m, last=True)
    m = (PE.now(), ACTE.now(), DVE.now())

    fw = region(R0)
    sq = [fw(f"fsq{n}", [P, SEQ]) for n in range(2)]
    dgf = fw("fdg", [P, SEQ])
    tok = fw("out_tok", [P, NB, D_MODEL])
    m = col_stats(lambda t: xT[:, t, :], DT, SEQ, sq, m)
    m = spread_cols(SEQ, dgf, m)
    DVE.need(m)
    for t in range(DT):
        m = DVE.sig(nc.vector.scalar_tensor_tensor(xT[:, t, :], xT[:, t, :], col("final_g_2", t), bank(6),
                                                   ALU.mult, ALU.mult))
        PE.need(m)
        if t >= 4:
            PE.need(back[t - 4])
        else:
            back = {} if t == 0 else back
        for k in range(NB):
            ins = nc.tensor.transpose(bank(t % 4, P, k * P), xT[:, t, k * P:(k + 1) * P], ident[:])
        m = PE.sig(ins)
        ACTE.need(m)
        back[t] = act(tok[:, :, t * P:(t + 1) * P], bank(t % 4).rearrange("p (b n) -> p b n", b=NB))
    sem_out = nc.alloc_semaphore("output_stored")
    SP.wait_ge(ACTE.sem, ACTE.n)
    SP.dma_start(a["out"][0].rearrange("(b p) d -> p b d", p=P), tok[:]).then_inc(sem_out, 16)
    SP.wait_ge(sem_out, 16)
    assert chunk[0] == sent[0], (chunk, sent)


INPUTS = ["x", "mem", "norm_mix_pre", "w_in", "lambda_q1", "lambda_k1", "lambda_q2", "lambda_k2", "subln_g",
          "w_attn_branch", "pool_w", "pool_scale", "w_pool_branch", "norm_mem", "w_mem_kv", "w_mem_branch", "w_out",
          "norm_mix_post", "norm_ffn_pre", "w_up", "conv_w", "conv_b", "w_down", "norm_ffn_post", "c_2", "ctx_2",
          "c_ctx_2", "mod_w_2", "mod_b_2", "norm_g_2", "ev_w_in_2", "ev_w_out_2", "a_q_gain_2", "a_k_gain_2",
          "b_sink_2", "od_w_in_2", "od_w_out_2", "c_dw_w_2", "c_dw_b_2", "c_ln_g_2", "c_ln_b_2", "final_g_2"]


def kernel(**inputs):
    import concourse.bacc as bacc
    from concourse.bass_utils import run_bass_kernel_spmd

    arrays = {n: np.ascontiguousarray(inputs[n]) for n in INPUTS}
    rpb = np.asarray(inputs["d_rpb_2"])[0]
    padded = np.zeros((rpb.shape[0], rpb.shape[1], 2 * GRID_W - 1), rpb.dtype)
    padded[:, :, GRID_W - NA_KW:GRID_W + NA_KW - 1] = rpb
    arrays["rpb_padded"] = padded
    for n, v in shape_tables().items():
        arrays["t_" + n] = np.ascontiguousarray(v)
    nc = bacc.Bacc("TRN2", target_bir_lowering=False, num_devices=1)
    aps = {n: nc.dram_tensor("in_" + n, v.shape, mybir.dt.from_np(v.dtype), kind="ExternalInput").ap()
           for n, v in arrays.items()}
    aps["out"] = nc.dram_tensor("out_0", (1, SEQ, D_MODEL), F32, kind="ExternalOutput").ap()
    build(nc, aps)
    r = run_bass_kernel_spmd(nc, [{"in_" + n: v for n, v in arrays.items()}], core_ids=[0])
    return r.results[0]["out_0"]
```

```python
import math
from contextlib import contextmanager

import numpy as np

import concourse.bass as bass
from concourse import mybir
from concourse.alu_op_type import AluOpType as ALU

F32 = mybir.dt.float32
F32R = mybir.dt.float32r
ACT = mybir.ActivationFunctionType
AX = mybir.AxisListType.X
P = 128
EPS = 1e-6

D_MODEL, SEQ, MEM, CTX = 1024, 512, 256, 256
DT = D_MODEL // P
NB = SEQ // P
CB = CTX // P
ALL = CTX + SEQ
DIFF_HEADS, DIFF_DH = 8, 64
MEM_HEADS = 4
POOL_WINDOWS = (2, 4, 8, 16)
POOL_PAD = max(POOL_WINDOWS)
LAM_INIT = 0.8 - 0.6 * math.exp(-0.3 * 0)
D_FF, FT = 2816, 2816 // P
HEAD = 64
GRID_W, NA_KH, NA_KW = 64, 8, 16
CONV_TAPS = 31
CT = 512 // P
MASKED = -1e30
CHUNK_COLS = 256
CHUNK = DT * CHUNK_COLS

ROWS = dict(norm_mix_pre=8, norm_mem=8, norm_mix_post=8, norm_ffn_pre=8, norm_ffn_post=8, pool_scale=4,
            subln_g=1, final_g_2=8, norm_g_2=16, mod_b_2=48, conv_b=44, c_2=8, c_ctx_2=8,
            a_q_gain_2=1, a_k_gain_2=1, c_dw_b_2=4, c_ln_g_2=4, c_ln_b_2=4, conv_w=132, c_dw_w_2=124)


def row_places():
    at, places = 0, {}
    for name, n in ROWS.items():
        places[name] = at
        at += n
    return places, -(-at // P)


def shape_tables():
    f = np.float32
    t = {}
    t["ident"] = np.eye(P, dtype=f)
    q, j = np.arange(P)[:, None], np.arange(SEQ)[None, :]
    rel = j - (SEQ - P) - q
    t["distance"] = np.where(rel <= 0, rel, -1e32).astype(f)
    t["slopes"] = np.tile(np.exp2(-8.0 * np.arange(1, DIFF_HEADS + 1) / DIFF_HEADS).astype(f), (P, 1))
    k = np.arange(P)[None, :]
    t["band_left"] = np.where(k >= q, 0, MASKED).astype(f)
    t["band_right"] = np.where(k <= q, 0, MASKED).astype(f)
    tok = np.arange(SEQ)
    half = HEAD // 2
    freqs = 10000.0 ** (-np.arange(0, half, 2, dtype=f) / half)
    ang = np.concatenate([(tok // GRID_W).astype(f)[:, None] * freqs, (tok % GRID_W).astype(f)[:, None] * freqs], -1)
    pair = (np.arange(P) % HEAD) // 2
    t["rope_cos"] = np.cos(ang).astype(f)[:, pair].T.copy()
    t["rope_sin"] = np.sin(ang).astype(f)[:, pair].T.copy()
    rot = np.zeros((P, P), f)
    e = np.arange(0, P, 2)
    rot[e + 1, e] = -1
    rot[e, e + 1] = 1
    t["rotate"] = rot
    rev = np.zeros((P, P), f)
    i = np.arange(P)
    rev[i, (i // GRID_W) * GRID_W + GRID_W - 1 - i % GRID_W] = 1
    t["reverse"] = rev
    qc, kc = np.arange(GRID_W)[:, None], np.arange(GRID_W)[None, :]
    start = np.clip(qc - NA_KW // 2, 0, GRID_W - NA_KW)
    near = np.where((kc >= start) & (kc < start + NA_KW), 0, MASKED).astype(f)
    t["near_mask"] = np.concatenate([near[::-1], near[::-1]])
    gather = np.zeros((P, 5, 10), f)
    spread = np.zeros((10, 5, P), f)
    for n in range(5):
        for p in range(P):
            gather[p, n, 2 * n + p // HEAD] = 1.0 / HEAD
            spread[2 * n + p // HEAD, n, p] = 1
    t["head_gather"] = gather.reshape(P, 50)
    t["head_spread"] = np.pad(spread.reshape(10, 5 * P), ((0, P - 10), (0, 0)))
    corr = np.zeros((len(POOL_WINDOWS), POOL_PAD), f)
    for g, w in enumerate(POOL_WINDOWS):
        corr[g] = w / np.minimum(np.arange(POOL_PAD) + 1, w)
    t["pool_edge"] = np.tile(corr.reshape(1, -1), (P, 1))
    return t


class Mark:

    def __init__(self, sem, at, step=0, reg=None):
        self.sem, self.at, self.step, self.reg = sem, at, step, reg

    def value(self):
        return self.at + self.step * self.reg if self.reg is not None else self.at

    def before(self, n=1):
        return Mark(self.sem, self.at - n * self.step, self.step, self.reg)

    def minus(self, n):
        return Mark(self.sem, self.at - n, self.step, self.reg)


class Engine:

    def __init__(self, nc, e, name):
        self.e, self.sem, self.n = e, nc.alloc_semaphore(name + "_done"), 0
        self.step, self.reg = 0, None

    def sig(self, ins):
        ins.then_inc(self.sem, 1)
        self.n += 1
        return Mark(self.sem, self.n, self.step, self.reg)

    def now(self):
        return Mark(self.sem, self.n, self.step, self.reg)

    def need(self, *marks):
        for m in marks:
            if m is not None:
                self.e.wait_ge(m.sem, m.value())


def build(nc, a):
    PE, ACTE, DVE, POOL = (Engine(nc, e, n) for e, n in (
        (nc.tensor, "pe"), (nc.scalar, "act"), (nc.vector, "dve"), (nc.gpsimd, "pool")))
    SP = nc.sync

    @contextmanager
    def loop(n, **steps):
        es = {"pe": PE, "act": ACTE, "dve": DVE, "pool": POOL}
        used = {k: es[k] for k in steps}
        start = {k: x.n for k, x in used.items()}
        with nc.Fori(0, n, engines=[x.e.engine for x in used.values()]) as i:
            for k, x in used.items():
                x.step, x.reg = steps[k], i
            yield i
            for k, x in used.items():
                assert x.n - start[k] == steps[k], (k, x.n - start[k], steps[k])
                x.step, x.reg = 0, None
                x.n = start[k] + n * steps[k]

    base = [(nc.sbuf_base + 63) // 64 * 64]

    def sb(name, shape, dt=F32, at=None):
        size = 4 * int(np.prod(shape[1:]))
        if at is None:
            at = base[0]
            base[0] += (size + 63) // 64 * 64
        return nc.alloc_sbuf_tensor_at(name, shape, dt, offset=at)

    raw = [sb(f"w_raw{p}", [P, CHUNK]) for p in range(2)]
    whi = [sb(f"w_hi{p}", [P, CHUNK], F32R) for p in range(2)]
    wlo = [sb(f"w_lo{p}", [P, CHUNK], F32R) for p in range(2)]
    xT = sb("x_T", [P, DT, SEQ])
    hhi, hlo = sb("h_hi", [P, DT, SEQ], F32R), sb("h_lo", [P, DT, SEQ], F32R)
    C0 = base[0]
    chi, clo = sb("c_hi", [P, DT, CTX], F32R), sb("c_lo", [P, DT, CTX], F32R)
    places, n_groups = row_places()
    cols = sb("cols", [P, n_groups * P])
    ident = sb("ident", [P, P])
    ones = sb("ones", [P, P])
    small = sb("small", [P, 256])
    rowvec = sb("rowvec", [1, 16])
    lamrow = sb("lamrow", [1, 4, DIFF_DH])
    modT = sb("mod_T", [P, 2, 24, 2])
    R0 = base[0]
    R_END = nc.sbuf_usable_end

    def region(at):
        pos = [at]

        def put(name, shape, dt=F32):
            size = 4 * int(np.prod(shape[1:]))
            t = nc.alloc_sbuf_tensor_at(name, shape, dt, offset=pos[0])
            pos[0] += (size + 63) // 64 * 64
            put.end = pos[0]
            return t
        return put

    ps = nc.alloc_psum_tensor("ps", [P, 8 * 512], F32)

    def bank(b, n=512, off=0, parts=P):
        return ps[0:parts, b * 512 + off:b * 512 + off + n]

    def col(name, i=0):
        c = places[name] + i
        return cols[:, c:c + 1]

    def dyn_col(name, i):
        return cols[:, bass.ds(places[name] + i, 1)]

    eps = small[:, 0:1]
    nlam = small[:, 1:2]
    sink = small[:, 2:10]
    nsink = small[:, 10:18]
    qgain = small[:, 18:19]
    subg = small[:, 19:20]
    zero1 = small[:, 20:21]
    slopes = small[:, 24:32]
    st = small[:, 32:48]
    sm = small[:, 48:80]

    sem_in = nc.alloc_semaphore("inputs_landed")
    landed = [0]

    def load(eng, dst, src):
        eng.dma_start(dst, src).then_inc(sem_in, 16)
        landed[0] += 16

    def need_inputs(*engines):
        for x in engines:
            x.e.wait_ge(sem_in, landed[0])

    def meet():
        marks = (PE.now(), ACTE.now(), DVE.now())
        for x_ in (PE, ACTE, DVE):
            x_.need(*marks)
        return marks

    def act(out, in_, func=ACT.Copy, **kw):
        return ACTE.sig(nc.scalar.activation(out, in_, func, **kw))

    def f(ap):
        return ap.bitcast(F32)

    setup = region(R0)
    xin = setup("x_in", [P, NB, D_MODEL])
    min_ = setup("mem_in", [P, CB, D_MODEL])
    memT = setup("mem_T", [P, DT, MEM])
    rows = setup("rows", [P, n_groups, P])
    x_landed = nc.alloc_semaphore("x_landed")
    SP.dma_start(ident[:], a["t_ident"]).then_inc(x_landed, 16)
    for b in range(NB):
        SP.dma_start(xin[:, b, :], a["x"][0][b * P:(b + 1) * P, :]).then_inc(x_landed, 16)

    def load_rows(name, src, at=0):
        r, n, done = places[name] + at, src.shape[0], 0
        while done < n:
            g, p = (r + done) // P, (r + done) % P
            k = min(n - done, P - p)
            load(SP, rows[p:p + k, g, :], src[done:done + k, :])
            done += k

    rows_clear = DVE.sig(nc.vector.memset(rows[:], 0.0))
    SP.wait_ge(rows_clear.sem, rows_clear.at)
    for name in ("norm_mix_pre", "norm_mem", "norm_mix_post", "norm_ffn_pre", "norm_ffn_post", "conv_b",
                 "norm_g_2", "c_2", "c_dw_b_2", "c_ln_g_2", "c_ln_b_2", "pool_scale", "mod_b_2"):
        load_rows(name, a[name].rearrange("l (t p) -> (l t) p", p=P))
    load_rows("subln_g", a["subln_g"])
    for name in ("c_ctx_2", "final_g_2"):
        load_rows(name, a[name].rearrange("(t p) -> t p", p=P))
    load_rows("conv_w", a["conv_w"].rearrange("l j (t p) -> (l j t) p", p=P))
    load_rows("c_dw_w_2", a["c_dw_w_2"].rearrange("l j (t p) -> (l j t) p", p=P))
    for name in ("a_q_gain_2", "a_k_gain_2"):
        g, p = places[name] // P, places[name] % P
        for s in range(2):
            load(SP, rows[p:p + 1, g, s * HEAD:(s + 1) * HEAD], a[name])
    for n, name in enumerate(("lambda_q1", "lambda_k1", "lambda_q2", "lambda_k2")):
        load(SP, lamrow[:, n, :], a[name])
    load(SP, rowvec[0:1, 1:9], a["b_sink_2"])
    load(SP, slopes, a["t_slopes"])
    load(SP, min_[:], a["mem"][0].rearrange("(b p) d -> p b d", p=P))
    DVE.sig(nc.vector.memset(ones[:], 1.0))
    DVE.sig(nc.vector.memset(eps, EPS))
    DVE.sig(nc.vector.memset(zero1, 0.0))
    consts_set = DVE.sig(nc.vector.memset(rowvec[0:1, 9:16], 0.0))
    PE.need(consts_set)
    ACTE.need(consts_set)

    def to_feature_major(src, nb, dst, after, banks=(0, 1, 2, 3), only_act=False):
        PE.need(*after)
        freed = [None] * len(banks)
        for t in range(DT):
            b = banks[t % len(banks)]
            PE.need(freed[t % len(banks)])
            for k in range(nb):
                ins = nc.tensor.transpose(bank(b, P, k * P), src[:, k, t * P:(t + 1) * P], ident[:])
            m = PE.sig(ins)
            if t % 2 or only_act:
                ACTE.need(m)
                freed[t % len(banks)] = act(dst[:, t, :], bank(b, nb * P))
            else:
                DVE.need(m)
                freed[t % len(banks)] = DVE.sig(nc.vector.tensor_copy(dst[:, t, :], bank(b, nb * P)))
        return ACTE.now(), DVE.now()

    PE.e.wait_ge(x_landed, 16 * (NB + 1))
    x_ready = to_feature_major(xin, NB, xT, ())

    landed_w = [nc.alloc_semaphore(f"chunk_landed{p}") for p in range(2)]
    hi_done = nc.alloc_semaphore("chunk_hi_done")
    lo_done = nc.alloc_semaphore("chunk_lo_done")

    MOD_CHUNKS = 3 * D_MODEL // CHUNK_COLS
    cond = small[:, 192:208].rearrange("p (t n) -> p t n", n=2)
    cond_tanh = small[:, 208:224].rearrange("p (t n) -> p t n", n=2)
    mod_raw = [nc.alloc_sbuf_tensor_at(f"mod_raw{p}", [P, CHUNK], F32, offset=C0 + p * 4 * CHUNK) for p in range(2)]
    mod_landed = [nc.alloc_semaphore(f"mod_landed{p}") for p in range(2)]
    mod_slots = nc.alloc_semaphore("mod_slots")
    mod_flat = modT[:].rearrange("p l t c -> p (l t) c")

    def mod_load(layer, p, m, i, step):
        SP.wait_ge(mod_slots, layer * (MOD_CHUNKS + 2) + m + 1 + step * i)
        src = a["mod_w_2"][layer][:, bass.ds(i * (step * CHUNK_COLS) + m * CHUNK_COLS, CHUNK_COLS)]
        SP.dma_start(mod_raw[p][:].rearrange("p (k n) -> p k n", k=DT),
                     src.rearrange("(k p) n -> p k n", p=P)).then_inc(mod_landed[p], 16)

    MOD_SIGNALS = 2 * DT + 2
    mod_sum = [None]

    def mod_open(sums_at, *marks):
        mod_sum[0] = nc.alloc_sbuf_tensor_at(f"mod_sums_{sums_at}", [P, 2, CHUNK_COLS], F32, offset=sums_at)
        DVE.need(*marks)
        nc.vector.memset(zero1, 0.0).then_inc(mod_slots, 2)

    def mod_weigh(layer, m, i, step):
        p = m % 2
        DVE.e.wait_ge(mod_landed[p], 16 * (layer * MOD_CHUNKS // 2 + m // 2 + 1) + 8 * step * i)
        w = mod_raw[p][:].rearrange("p (k n) -> p k n", k=DT)
        last = [None, None]
        for k in range(DT):
            for n in range(2):
                out, c = mod_sum[0][:, n, :], cond[:, k, n:n + 1]
                DVE.need(last[n])
                last[n] = DVE.sig(nc.vector.tensor_scalar(out, w[:, k, :], c, None, ALU.mult) if k == 0 else
                                  nc.vector.scalar_tensor_tensor(out, w[:, k, :], c, out, ALU.mult, ALU.add))
        return last

    def mod_product(layer, m, i, step, weighed, bank_free):
        p = m % 2
        PE.need(bank_free, *weighed)
        for o in range(2):
            for n in range(2):
                ins = nc.tensor.matmul(bank(4 + p, 1, 2 * o + n), mod_sum[0][:, n, o * P:(o + 1) * P], ones[:, 0:1])
        ins.then_inc(mod_slots, 1)
        DVE.e.wait_ge(mod_slots, layer * (MOD_CHUNKS + 2) + 2 + m + 1 + step * i)
        for o in range(2):
            t = layer * 3 * DT + 2 * m + o + 2 * step * i
            d = DVE.sig(nc.vector.tensor_scalar(mod_flat[:, bass.ds(t, 1), :].rearrange("p a c -> p (a c)"),
                                                bank(4 + p, 2, 2 * o), dyn_col("mod_b_2", t), None, ALU.add))
        return d

    chunk = [0]
    sent = [0]

    def sp_load(p, value, src, kt, n):
        if value is not None:
            SP.wait_ge(lo_done, value)
        dst = raw[p][:, 0:kt * n].rearrange("p (k n) -> p k n", k=kt)
        SP.dma_start(dst, src.rearrange("(k p) n -> p k n", p=P)).then_inc(landed_w[p], 16)

    def stream(w, starts, step=0, n=1, rows_=(0, D_MODEL), width=CHUNK_COLS, mod=None):
        r0, r1 = rows_
        kt = (r1 - r0) // P
        c0 = sent[0]
        assert len(starts) % 2 == 0
        if c0 == 0:
            for i in range(n):
                for q, s in enumerate(starts):
                    c = i * len(starts) + q
                    sp_load(q % 2, c - 1 if c > 1 else None, w[r0:r1, i * step + s:i * step + s + width], kt, width)
            sent[0] += n * len(starts)
            return
        with nc.Fori(0, n, engines=[SP.engine]) as i:
            for q, s in enumerate(starts):
                sp_load(q % 2, (c0 + q - 1) + len(starts) * i,
                        w[r0:r1, bass.ds(i * step + s, width)], kt, width)
                if mod is not None:
                    mod_load(mod[0], q % 2, mod[1] + q, i, len(starts))
        sent[0] += n * len(starts)

    def stream_down(w):
        c0 = sent[0]
        with nc.Fori(0, 2, engines=[SP.engine]) as i:
            for q in range(6):
                g, k = divmod(q, 3)
                k0, k1 = 8 * k, min(8 * k + 8, FT)
                sp_load(q % 2, (c0 + q - 1) + 6 * i, w[k0 * P:k1 * P, bass.ds(i * 512 + g * 256, 256)], k1 - k0, 256)
                mod_load(1, q % 2, q, i, 6)
        sent[0] += 12

    def round_hi(p, c, i=None, step=0):
        v = 16 * (c // 2 + 1)
        ACTE.e.wait_ge(landed_w[p], v if i is None else v + 8 * step * i)
        nc.scalar.activation(whi[p][:], raw[p][:], ACT.Copy).then_inc(hi_done, 1)

    def mm3(out, whi_, wlo_, xhi_, xlo_, first, last, flip=False):
        for n, (w, x) in enumerate(((wlo_, xhi_), (whi_, xlo_), (whi_, xhi_))):
            l, r = (x, w) if flip else (w, x)
            ins = nc.tensor.matmul(out, l, r, start=first and n == 0, stop=last and n == 2)
        return ins

    freed_banks = [None]

    def gemm(n_pairs, xs, evac, kt=DT, cols_=CHUNK_COLS, per=None, after=(), last=False, ready=None, mod=None,
             middle=None, before=None, entry=None):
        outs = 2 * cols_ // P
        base_chunk = chunk[0]
        PE.need(*after)
        entry = entry or (ACTE.now(), DVE.now())
        before = before or {b: entry for b in range(4)}

        def x_first():
            for n, (xh, xl, tok) in enumerate(xs):
                if n == 1:
                    ready[1] = middle()
                for p in range(2):
                    PE.e.wait_ge(lo_done, base_chunk + p + 1)
                    hi, lo = (w_[p][:].rearrange("p (k n) -> p k n", k=DT) for w_ in (whi, wlo))
                    for o in range(2):
                        if n == 0:
                            PE.need(*before[2 * p + o])
                        for k in range(DT):
                            if p == o == 0:
                                PE.need(ready[n][k])
                            ins = mm3(bank(2 * p + o + 4 * n, tok), hi[:, k, o * P:(o + 1) * P],
                                      lo[:, k, o * P:(o + 1) * P], xh[:, k, 0:tok], xl[:, k, 0:tok],
                                      k == 0, k == DT - 1)
                    if n == 1:
                        m = PE.sig(ins)
                        for o in range(2):
                            evac(0, 2 * p + o, m)
                        ACTE.need(m)
                        round_hi(p, base_chunk + p + 2)

        def body(i, before=None, mod_free=None, rounds=True):
            freed = {}
            for p in range(2):
                PE.e.wait_ge(lo_done, base_chunk + p + 1 + 2 * i)
                hi = whi[p][:, 0:kt * cols_].rearrange("p (k n) -> p k n", k=kt)
                lo = wlo[p][:, 0:kt * cols_].rearrange("p (k n) -> p k n", k=kt)
                if mod is not None:
                    weighed = mod_weigh(mod[0], mod[1] + p, i, 2)
                for o in range(cols_ // P):
                    u = p * (cols_ // P) + o
                    b = u % 4
                    if u >= 4:
                        PE.need(*freed[b])
                    elif before is None:
                        na, nd = evac.own(u)
                        PE.need(ACTE.now().minus(per[0] - na) if na else None,
                                DVE.now().minus(per[1] - nd) if nd else None)
                    else:
                        PE.need(*before[b])
                    s = slice(o * P, (o + 1) * P)
                    for n, (xh, xl, tok) in enumerate(xs):
                        for k in range(kt):
                            if ready and u == 0:
                                PE.need(ready[n][k])
                            ins = mm3(bank(b + 4 * n, tok), hi[:, k, s], lo[:, k, s], xh[:, k, 0:tok],
                                      xl[:, k, 0:tok], k == 0, k == kt - 1)
                    m = PE.sig(ins)
                    freed[b] = evac(i, u, m)
                if mod is not None:
                    mod_product(mod[0], mod[1] + p, i, 2, weighed, mod_free)
                if rounds:
                    ACTE.need(m)
                    round_hi(p, base_chunk + p + 2, None if n_pairs == 1 else i, 2)
            return freed

        if middle:
            x_first()
        elif n_pairs == 1:
            freed_banks[0] = body(0, before)
        else:
            PE.need(*entry)
            with loop(n_pairs - last, pe=outs, act=per[0], dve=per[1]) as i:
                body(i, mod_free=DVE.now())
            if last:
                body(n_pairs - 1, {b: (ACTE.now(), DVE.now()) for b in range(4)}, rounds=False)
        chunk[0] += 2 * n_pairs

    def gemm_tokens(n_pairs, lhs, dst, col_of, after=(), width=CHUNK_COLS, mod=None, only_act=False):
        base_chunk = chunk[0]
        PE.need(*after)
        nblk = len(lhs)
        banks = 4 if mod is not None else 8
        n_act = nblk if only_act else nblk // 2
        mod_dve = 2 * MOD_SIGNALS if mod is not None else 0
        with loop(n_pairs, pe=2 * nblk, act=2 * n_act, dve=2 * (nblk - n_act) + mod_dve) as i:
            a0, d0 = ACTE.now(), DVE.now()
            freed = {b: (a0, d0) for b in range(8)}
            for p in range(2):
                PE.e.wait_ge(lo_done, base_chunk + p + 1 + 2 * i)
                hi = whi[p][:].rearrange("p (k n) -> p k n", k=DT)
                lo = wlo[p][:].rearrange("p (k n) -> p k n", k=DT)
                if mod is not None:
                    weighed = mod_weigh(mod[0], mod[1] + p, i, 2)
                for n, (xh, xl, blk) in enumerate(lhs):
                    b = (p * nblk + n) % banks
                    PE.need(*freed[b])
                    ts = slice(blk * P, (blk + 1) * P)
                    for k in range(DT):
                        ins = mm3(bank(b, width), hi[:, k, :], lo[:, k, :], xh[:, k, ts], xl[:, k, ts],
                                  k == 0, k == DT - 1, flip=True)
                    m = PE.sig(ins)
                    out = dst[:, n, bass.ds(col_of(i, p), width)]
                    if n % 2 or only_act:
                        ACTE.need(m)
                        freed[b] = (act(out, bank(b, width)),)
                    else:
                        DVE.need(m)
                        freed[b] = (DVE.sig(nc.vector.tensor_copy(out, bank(b, width))),)
                if mod is not None:
                    mod_product(mod[0], mod[1] + p, i, 2, weighed, d0)
                ACTE.need(m)
                round_hi(p, base_chunk + p + 2, i, 2)
        chunk[0] += 2 * n_pairs

    w_in = a["w_in"][0]
    stream(w_in, [3584, 3840])
    stream(w_in, [3072, 3328])
    stream(a["w_mem_kv"][0], [0, 256], 512, 2)
    stream(w_in, [6144, 6400], 512, 2)
    stream(a["w_mem_branch"][0], [0, 512], rows_=(0, 512), width=512)
    stream(w_in, [5120, 5376], 512, 2)
    stream(a["w_pool_branch"][0], [0, 512], rows_=(0, 512), width=512)
    stream(w_in, [0, 256], 512, 2, mod=(0, 0))
    stream(w_in, [1024, 1280], 512, 2, mod=(0, 4))
    stream(w_in, [2048, 2304], 512, 2, mod=(0, 8))
    stream(w_in, [4096, 4352], 512, 2)
    stream(a["w_attn_branch"][0], [0, 256], 512, 2)
    stream(a["w_out"][0], [0, 256], 512, 2)
    stream(a["w_up"][0], [0, D_FF], 256, D_FF // 256)
    stream_down(a["w_down"][0])
    ev = a["ev_w_in_2"][0]
    stream(ev, [0, 256], 1280, 2)
    stream(ev, [512, 1792])
    stream(ev, [768, 1024])
    stream(ev, [2048, 2304])
    stream(a["ev_w_out_2"][0], [0, 256], 512, 2)
    od = a["od_w_in_2"][0]
    stream(od, [0, 512], 256, 2)
    stream(od, [1536, 1792])
    stream(od, [2048, 2304])
    stream(od, [2560, 2816])
    stream(od, [3072, 3328])
    stream(od, [1024, 1280])
    stream(a["od_w_out_2"][0], [0, 256], 512, 2)

    with nc.Fori(0, sent[0] // 2, engines=[nc.gpsimd.engine]) as i:
        for p in range(2):
            nc.gpsimd.wait_ge(hi_done, 2 * i + p + 1)
            nc.gpsimd.tensor_tensor(wlo[p][:], raw[p][:], f(whi[p][:]), ALU.subtract).then_inc(lo_done, 1)

    norm_count = []

    def rstd_of_tiles(src_of, ready, tokens, sq):
        nb = tokens // P
        used = {}
        nc.scalar.preload_act_table(ACT.Sqrt)
        for t in range(DT):
            ACTE.need(used.get(t - 2), ready[t])
            PE.need(act(sq[t % 2][:, 0:tokens], src_of(t), ACT.Square))
            for b in range(nb):
                ins = nc.tensor.matmul(bank(7, 1, b), sq[t % 2][:, b * P:(b + 1) * P], ones[:, 0:1],
                                       start=t == 0 and b == 0, stop=t == DT - 1, skip_group_check=True)
            used[t] = PE.sig(ins)
        ACTE.need(used[DT - 1])
        DVE.need(act(st[:, 0:nb], bank(7, nb), ACT.Sqrt, scale=1.0 / D_MODEL, bias=eps))
        nc.scalar.preload_act_table(ACT.Exp)
        return DVE.sig(nc.vector.reciprocal(st[:, 8:8 + nb], st[:, 0:nb]))

    def spread_cols(tokens, dg, m, bank_=6):
        nb = tokens // P
        DVE.need(m)
        for b in range(nb):
            m = DVE.sig(nc.vector.tensor_scalar(dg[:, b * P:(b + 1) * P], ident[:], st[:, 8 + b:9 + b], None, ALU.mult))
        PE.need(m)
        return PE.sig(nc.tensor.matmul(bank(bank_, tokens), ones[:], dg[:, 0:tokens]))

    def sum_squares(src_of, n_tiles, tokens, sq, acc, after=()):
        ACTE.need(*after)
        DVE.need(*after)
        first = act(acc[:, 0:tokens], src_of(0), ACT.Square)
        added = {}
        for t in range(1, n_tiles):
            w = sq[t % 2][:, 0:tokens]
            ACTE.need(added.get(t - 2))
            DVE.need(act(w, src_of(t), ACT.Square), added.get(t - 1, first))
            added[t] = DVE.sig(nc.vector.tensor_tensor(acc[:, 0:tokens], acc[:, 0:tokens], w, ALU.add))
        return added[n_tiles - 1]

    def rstd_of_sum(acc, tokens, m, bank_=7, dim=D_MODEL):
        nb = tokens // P
        nc.scalar.preload_act_table(ACT.Sqrt)
        PE.need(m)
        for b in range(nb):
            ins = nc.tensor.matmul(bank(bank_, 1, b), acc[:, b * P:(b + 1) * P], ones[:, 0:1],
                                   start=b == 0, stop=True, skip_group_check=True)
        ACTE.need(PE.sig(ins))
        m = act(st[:, 0:nb], bank(bank_, nb), ACT.Sqrt, scale=1.0 / dim, bias=eps)
        DVE.need(m)
        nc.scalar.preload_act_table(ACT.Exp)
        return DVE.sig(nc.vector.reciprocal(st[:, 8:8 + nb], st[:, 0:nb]))

    class Norm:

        def __init__(self, src, tokens, hi, lo, gain_of, work, after, shift_of=None, ready=None, bank_=6, summed=None):
            self.src, self.tokens, self.hi, self.lo = src, tokens, hi, lo
            self.gain_of, self.shift_of, self.bank = gain_of, shift_of, bank_
            tag = str(len(norm_count))
            norm_count.append(0)
            self.dg = summed.acc if summed else work("dg_" + tag, [P, tokens])
            sq = [work(f"sq{n}_{tag}", [P, tokens]) for n in range(2)]
            self.tmp = [work(f"nt{n}_{tag}", [P, tokens]) for n in range(3)]
            self.rstd = None
            if ready:
                PE.need(*after)
                ACTE.need(*after)
            if summed:
                self.m = DVE.now()
            elif ready is None:
                self.m = sum_squares(lambda t: src[:, t, :], DT, tokens, sq, self.dg, after)
            else:
                self.rstd = rstd_of_tiles(lambda t: src[:, t, :], ready, tokens, sq)

        def finish(self):
            src, tokens, hi, lo = self.src, self.tokens, self.hi, self.lo
            gain_of, shift_of, tmp, spread_bank = self.gain_of, self.shift_of, self.tmp, self.bank
            rstd = self.rstd or rstd_of_sum(self.dg, tokens, self.m)
            spread = spread_cols(tokens, self.dg, rstd, spread_bank)
            rounded, done = {}, {}

            def low(t):
                DVE.need(rounded[t])
                w, h = tmp[t % 3][:], f(hi[:, t, 0:tokens])
                done[t] = DVE.sig(nc.vector.tensor_tensor(lo[:, t, 0:tokens], w, h, ALU.subtract) if shift_of is None
                                  else nc.vector.scalar_tensor_tensor(lo[:, t, 0:tokens], w, shift_of(t), h,
                                                                      ALU.add, ALU.subtract))

            DVE.need(spread)
            for t in range(DT):
                w = tmp[t % 3][:]
                DVE.need(done.get(t - 3))
                g = DVE.sig(nc.vector.scalar_tensor_tensor(w, src[:, t, :], gain_of(t), bank(spread_bank, tokens),
                                                           ALU.mult, ALU.mult))
                ACTE.need(g)
                rounded[t] = act(hi[:, t, 0:tokens], w) if shift_of is None else \
                    act(hi[:, t, 0:tokens], w, ACT.Identity, bias=shift_of(t))
                if t:
                    low(t - 1)
            low(DT - 1)
            return [done[t] for t in range(DT)]

    def norm_split(*args, **kw):
        return Norm(*args, **kw).finish()

    def split(hi_ap, lo_ap, src, m, src_is_act=False):
        ACTE.need(m)
        g = act(hi_ap, src)
        DVE.need(g)
        return g, DVE.sig(nc.vector.tensor_tensor(lo_ap, src, f(hi_ap), ALU.subtract))

    h_norm = Norm(xT, SEQ, hhi, hlo, lambda t: col("norm_mix_pre", t), region(R0), x_ready)

    need_inputs(PE, DVE, ACTE)
    PE.need(*x_ready)

    DVE.sig(nc.vector.tensor_tensor(lamrow[:, 0, :], lamrow[:, 0, :], lamrow[:, 1, :], ALU.mult))
    DVE.need(DVE.sig(nc.vector.tensor_tensor(lamrow[:, 2, :], lamrow[:, 2, :], lamrow[:, 3, :], ALU.mult)))
    m = DVE.sig(nc.vector.tensor_reduce(rowvec[0:1, 10:12], lamrow[:, 0:4:2, :], AX, ALU.add))
    ACTE.need(m)
    nc.scalar.preload_act_table(ACT.Exp)
    m = act(rowvec[0:1, 12:14], rowvec[0:1, 10:12], ACT.Exp)
    DVE.need(m)
    DVE.need(DVE.sig(nc.vector.tensor_tensor(rowvec[0:1, 14:15], rowvec[0:1, 12:13], rowvec[0:1, 13:14], ALU.subtract)))
    m = DVE.sig(nc.vector.tensor_scalar(rowvec[0:1, 0:1], rowvec[0:1, 14:15], LAM_INIT, None, ALU.add))
    PE.need(m)
    m = PE.sig(nc.tensor.matmul(bank(7, 16), ones[0:1, :], rowvec[0:1, :]))
    DVE.need(m)
    DVE.sig(nc.vector.tensor_scalar(nlam, bank(7, 1), -1.0, None, ALU.mult))
    DVE.sig(nc.vector.tensor_copy(sink, bank(7, 8, 1)))
    row_m = DVE.sig(nc.vector.tensor_scalar(nsink, bank(7, 8, 1), -1.0, None, ALU.mult))

    assert n_groups <= 6
    for g in range(n_groups):
        ACTE.need(PE.sig(nc.tensor.transpose(bank(g, P), rows[:, g, :], ident[:])))
        cols_set = act(cols[:, g * P:(g + 1) * P], bank(g, P))
    DVE.need(cols_set)
    DVE.sig(nc.vector.tensor_scalar(qgain, col("a_q_gain_2"), HEAD ** -0.5, None, ALU.mult))
    DVE.sig(nc.vector.tensor_scalar(subg, col("subln_g"), 1.0 - LAM_INIT, None, ALU.mult))

    mem_ready = to_feature_major(min_, CB, memT, (cols_set, row_m))
    ACTE.need(cols_set)
    for n, name in enumerate(("c_2", "c_ctx_2")):
        c0 = places[name]
        m = act(cond_tanh[:, :, n], cols[:, c0:c0 + DT], ACT.Tanh, scale=0.5)
    DVE.need(m)
    for n, name in enumerate(("c_2", "c_ctx_2")):
        c0 = places[name]
        DVE.need(DVE.sig(nc.vector.scalar_tensor_tensor(cond[:, :, n], cond_tanh[:, :, n], 1.0, cols[:, c0:c0 + DT],
                                                        ALU.add, ALU.mult)))
    cond_ready = DVE.sig(nc.vector.tensor_scalar(cond, cond, 0.5, None, ALU.mult))
    PE.need(cond_ready)
    for p in range(2):
        round_hi(p, p)
    h_ready = h_norm.finish()
    mem_work = region(R0 + 73728)
    mem_norm = Norm(memT, MEM, chi, clo, lambda t: col("norm_mem", t), mem_work, h_ready[-1:])

    put = region(R0)
    mixT = put("mix_T", [P, DT, SEQ])
    gate = put("gate", [P, DT, SEQ])
    kmT = put("km_T", [P, MEM_HEADS, MEM])
    vm = put("vm", [P, CB, MEM_HEADS * P])
    qmT = put("qm_T", [P, MEM_HEADS, SEQ])
    upT = put("up_T", [P, 4, POOL_PAD + SEQ])
    om = put("om", [P, NB, MEM_HEADS * P])
    bhi, blo = put("b_hi", [P, 4, SEQ], F32R), put("b_lo", [P, 4, SEQ], F32R)
    pre_end = put.end
    assert pre_end <= R_END, (pre_end, R_END)

    def owns(*signals):
        def mark(ev_):
            ev_.own = lambda u: signals[u % 2]
            return ev_
        return mark

    def evac_copy(dst_of, **kw):
        @owns((0, 1), (1, 0))
        def ev_(i, u, m):
            if u % 2:
                ACTE.need(m)
                return (act(dst_of(i, u), bank(u % 4, dst_of.n), **kw),)
            DVE.need(m)
            s = kw.get("scale")
            if s is None:
                return (DVE.sig(nc.vector.tensor_copy(dst_of(i, u), bank(u % 4, dst_of.n))),)
            return (DVE.sig(nc.vector.tensor_scalar(dst_of(i, u), bank(u % 4, dst_of.n), s, None, ALU.mult)),)
        return ev_

    def dest(t, n, lo_=0):
        def of(i, u):
            j = 4 * i + u
            if isinstance(j, int):
                return t[:, j, lo_:lo_ + n]
            return t[:, bass.ds(j, 1), lo_:lo_ + n].rearrange("p a n -> p (a n)")
        of.n = n
        return of

    X = [(hhi, hlo, SEQ)]
    C = [(chi, clo, CTX)]
    XC = X + C
    gemm(1, X, evac_copy(dest(qmT, SEQ), scale=P ** -0.5), ready=[h_ready], entry=mem_ready)
    entry = (ACTE.now(), DVE.now())
    m_ready = mem_norm.finish()
    gemm(1, X, evac_copy(dest(upT, SEQ, POOL_PAD)), entry=entry)
    gemm(1, C, evac_copy(dest(kmT, MEM)), ready=[m_ready])
    gemm_tokens(1, [(chi, clo, b) for b in range(CB)], vm, lambda i, p: p * 256)
    m_proj = (ACTE.now(), DVE.now())

    class Attention:

        def __init__(self, probs, probsT, scale=1.0):
            self.probs, self.probsT, self.scale = probs, probsT, scale
            self.exp, self.turned, self.copied, self.weighted, self.out, self.inv = {}, {}, {}, {}, {}, {}

        def run(self, units):
            n = len(units)
            act0, dve0 = ACTE.now(), DVE.now()
            PE.need(act0)
            for s in range(n + 4):
                if s == 1:
                    DVE.need(act0, dve0)
                if s == 2:
                    PE.need(dve0)
                if 0 <= s - 2 < n:
                    self.turn(s - 2, units[s - 2])
                if s < n:
                    self.scores(s, units[s])
                if 0 <= s - 1 < n:
                    self.softmax(s - 1, units[s - 1])
                if 0 <= s - 4 < n:
                    self.output(s - 4, units[s - 4])
                if 0 <= s - 2 < n:
                    self.copy(s - 2, units[s - 2])
                if 0 <= s - 3 < n:
                    self.values(s - 3, units[s - 3])

        @staticmethod
        def stats(s):
            return (sm[:, 4 * (s % 4) + j:4 * (s % 4) + j + 1] for j in range(4))

        def scores(self, s, u):
            PE.need(self.exp.get(s - 2))
            if "need" in u:
                PE.need(*u["need"]())
            b = 2 * (s % 2)
            for off, n, q, k in u["scores"]:
                ins = nc.tensor.matmul(ps[:, b * 512 + off:b * 512 + off + n], q, k, start=True, stop="added" not in u,
                                       skip_group_check="added" in u)
            for off, n, q, k in u.get("added", ()):
                ins = nc.tensor.matmul(ps[:, b * 512 + off:b * 512 + off + n], q, k, start=False, stop=True,
                                       skip_group_check=True)
            u["scored"] = PE.sig(ins)
            if "then" in u:
                u["then"]()

        def softmax(self, s, u):
            b, n = 2 * (s % 2), u["n"]
            S = ps[:, b * 512:b * 512 + n]
            neg_max, total, _, esink = self.stats(s)
            DVE.need(u["scored"])
            for off, w, bias in u.get("bias", ()):
                dst = ps[:, b * 512 + off:b * 512 + off + w]
                m = DVE.sig(nc.vector.tensor_tensor(dst, dst, bias, ALU.add))
            if u.get("bias"):
                DVE.need(m)
            DVE.need(self.exp.get(s - 4))
            m = DVE.sig(nc.vector.tensor_reduce(neg_max, S, AX, ALU.max, negate=True))
            if self.scale != 1.0:
                DVE.need(m)
                m = DVE.sig(nc.vector.tensor_scalar(neg_max, neg_max, self.scale, None, ALU.mult))
            if "sink" in u:
                DVE.need(m)
                m = DVE.sig(nc.vector.tensor_tensor(neg_max, neg_max, u["nsink"], ALU.min))
            ACTE.need(m, self.turned.get(s - 2), self.inv.get(s - 4))
            self.exp[s] = act(self.probs[s % 2][:, 0:n], S, ACT.Exp, bias=neg_max, scale=self.scale, accum_out=total)
            if "sink" in u:
                self.exp[s] = act(esink, u["sink"], ACT.Exp, bias=neg_max)

        def turn(self, s, u):
            nb = u["n"] // P
            h = (nb + 1) // 2
            PE.need(self.exp[s], *self.copied.get(s - 1, ()))
            for k in range(nb):
                ins = nc.tensor.transpose(bank(4, P, k * P) if k < h else bank(5, P, (k - h) * P),
                                          self.probs[s % 2][:, k * P:(k + 1) * P], ident[:])
            self.turned[s] = PE.sig(ins)

        def copy(self, s, u):
            n, half = u["n"], (u["n"] // P + 1) // 2 * P
            T = self.probsT[s % 2]
            _, total, inv, esink = self.stats(s)
            DVE.need(self.exp[s], self.out.get(s - 4))
            if "sink" in u:
                DVE.need(DVE.sig(nc.vector.tensor_tensor(total, total, esink, ALU.add)))
            self.inv[s] = DVE.sig(nc.vector.reciprocal(inv, total))
            DVE.need(self.turned[s], self.weighted.get(s - 2))
            c = [DVE.sig(nc.vector.tensor_copy(T[:, 0:half], bank(4, half)))]
            if half < n:
                ACTE.need(self.turned[s], self.weighted.get(s - 2))
                c.append(act(T[:, half:n], bank(5, n - half)))
            self.copied[s] = c

        def values(self, s, u):
            T, w, nb = self.probsT[s % 2], u["dh"], u["n"] // P
            PE.need(*self.copied[s], self.out.get(s - 2))
            for k in range(nb):
                ins = nc.tensor.matmul(bank(6 + s % 2, w), T[:, k * P:(k + 1) * P], u["values"][k],
                                       start=k == 0, stop=k == nb - 1)
            self.weighted[s] = PE.sig(ins)

        def output(self, s, u):
            _, _, inv, _ = self.stats(s)
            w = u["dh"]
            DVE.need(self.weighted[s], self.inv[s])
            self.out[s] = DVE.sig(nc.vector.tensor_scalar(u["out"], bank(6 + s % 2, w), inv, None, ALU.mult))

    awork = region(C0)
    probs = [awork(f"probs{n}", [P, MEM]) for n in range(2)]
    probsT = [awork(f"probsT{n}", [P, MEM]) for n in range(2)]
    qs = [awork(f"q_staged{n}", [P, SEQ]) for n in range(2)]
    assert awork.end <= C0 + 16384

    def dyn(t, j, sl):
        return t[:, bass.ds(j, 1), sl].rearrange("p a n -> p (a n)")

    for x_ in (PE, ACTE, DVE):
        x_.need(*m_proj)
    HEADS_A_TURN = 2
    n_u = HEADS_A_TURN * NB
    with loop(MEM_HEADS // HEADS_A_TURN, pe=3 * n_u, act=2 * n_u + HEADS_A_TURN, dve=4 * n_u) as it:
        ACTE.need(PE.now())
        units = []
        for e in range(HEADS_A_TURN):
            h = HEADS_A_TURN * it + e
            act(qs[e][:], dyn(qmT, h, slice(0, SEQ)))
            for i in range(NB):
                units.append(dict(scores=[(0, MEM, qs[e][:, i * P:(i + 1) * P], dyn(kmT, h, slice(0, MEM)))],
                                  n=MEM, dh=P, values=[vm[:, k, bass.ds(h * P, P)] for k in range(CB)],
                                  out=om[:, i, bass.ds(h * P, P)]))
        Attention(probs, probsT).run(units)
    att_done = (ACTE.now(), DVE.now(), PE.now())

    def token_to_split(src, n_tiles, nb, hi, lo, after, gain=None):
        PE.need(*after)
        ACTE.need(*after)
        DVE.need(*after)
        freed = {}
        for t in range(n_tiles):
            b = t % 4
            PE.need(*freed.get(b, ()))
            for k in range(nb):
                ins = nc.tensor.transpose(bank(b, P, k * P), src[:, k, t * P:(t + 1) * P], ident[:])
            m = PE.sig(ins)
            ACTE.need(m)
            g = act(hi[:, t, :], bank(b, nb * P), scale=1.0) if gain is None else \
                act(hi[:, t, :], bank(b, nb * P), ACT.Identity, scale=gain, bias=zero1)
            DVE.need(g)
            if gain is None:
                d = DVE.sig(nc.vector.tensor_tensor(lo[:, t, :], bank(b, nb * P), f(hi[:, t, :]), ALU.subtract))
            else:
                d = DVE.sig(nc.vector.scalar_tensor_tensor(lo[:, t, :], bank(b, nb * P), gain, f(hi[:, t, :]),
                                                           ALU.mult, ALU.subtract))
            freed[b] = (g, d)
        return ACTE.now(), DVE.now()

    @owns((1, 0), (1, 0))
    def evac_gate(i, u, m):
        ACTE.need(m)
        return (act(dest(gate, SEQ)(i, u), bank(u % 4), ACT.Tanh, scale=0.5),)

    gtmp = [region(C0)("gtmp0", [P, SEQ]), region(C0 + 2048)("gtmp1", [P, SEQ])]

    def evac_branch(first, tiles=4):
        @owns((0, 2), (0, 2))
        def ev_(i, u, m):
            j = tiles * i + u
            g, x_ = (gate[:, j, :], mixT[:, j, :]) if isinstance(j, int) else \
                (dyn(gate, j, slice(0, SEQ)), dyn(mixT, j, slice(0, SEQ)))
            DVE.need(m)
            m2 = DVE.sig(nc.vector.scalar_tensor_tensor(gtmp[u % 2][:], g, 1.0, bank(u % 4), ALU.add, ALU.mult))
            DVE.need(m2)
            if first:
                DVE.sig(nc.vector.tensor_scalar(x_, gtmp[u % 2][:], 0.5, None, ALU.mult))
            else:
                DVE.sig(nc.vector.scalar_tensor_tensor(x_, gtmp[u % 2][:], 0.5, x_, ALU.mult, ALU.add))
            return (m2,)
        return ev_

    om_ready = token_to_split(om, MEM_HEADS, NB, bhi, blo, att_done)
    poolw = region(C0 + 4096)
    pw = poolw("pool_w", [P, 4, P])
    edge = poolw("pool_edge", [P, 4, POOL_PAD])
    s1 = poolw("pool_s1", [P, POOL_PAD + SEQ])
    s2 = poolw("pool_s2", [P, POOL_PAD + SEQ])
    ACTE.need(*att_done)
    load(nc.scalar, pw[:], a["pool_w"][0].rearrange("g c d -> c g d"))
    load(nc.scalar, edge[:], a["t_pool_edge"].rearrange("p (g n) -> p g n", g=4))
    pool_landed = landed[0]
    gemm(2, X, evac_gate, per=(4, 0), after=om_ready)
    DVE.need(*att_done)
    DVE.sig(nc.vector.memset(upT[:, :, 0:POOL_PAD], 0.0))
    DVE.sig(nc.vector.memset(s1[:, 0:POOL_PAD], 0.0))
    DVE.need(DVE.sig(nc.vector.memset(s2[:, 0:POOL_PAD], 0.0)))
    DVE.e.wait_ge(sem_in, pool_landed)
    for g, w in enumerate(POOL_WINDOWS):
        cur, sh, n = upT[:, g, :], 1, 0
        while sh < w:
            nxt = (s1, s2)[n % 2]
            DVE.need(DVE.sig(nc.vector.tensor_tensor(nxt[:, POOL_PAD:], cur[:, POOL_PAD:],
                                                     cur[:, POOL_PAD - sh:POOL_PAD + SEQ - sh], ALU.add)))
            cur, sh, n = nxt, 2 * sh, n + 1
        DVE.need(DVE.sig(nc.vector.tensor_tensor(cur[:, POOL_PAD:2 * POOL_PAD], cur[:, POOL_PAD:2 * POOL_PAD],
                                                 edge[:, g, :], ALU.mult)))
        windows_done = DVE.sig(nc.vector.scalar_tensor_tensor(upT[:, g, POOL_PAD:], cur[:, POOL_PAD:], 1.0 / w,
                                                              upT[:, g, POOL_PAD:], ALU.mult, ALU.subtract))
        DVE.need(windows_done)
    DVE.need(ACTE.now())
    gemm(1, [(bhi, blo, SEQ)], evac_branch(True), kt=4, cols_=512, after=(ACTE.now(), DVE.now()))
    mem_branch = (PE.now(), DVE.now())

    PE.need(*mem_branch)
    PE.need(windows_done)
    PE.e.wait_ge(sem_in, pool_landed)
    ACTE.need(*mem_branch)
    for g in range(4):
        m = PE.sig(nc.tensor.matmul(bank(g), pw[:, g, :], upT[:, g, POOL_PAD:]))
        ACTE.need(m)
        sc = col("pool_scale", g)
        m = act(bhi[:, g, :], bank(g), ACT.Identity, scale=sc, bias=zero1)
        DVE.need(m)
        DVE.sig(nc.vector.scalar_tensor_tensor(blo[:, g, :], bank(g), sc, f(bhi[:, g, :]), ALU.mult, ALU.subtract))
    pool_ready = (ACTE.now(), DVE.now())
    ACTE.need(DVE.now())
    gemm(2, X, evac_gate, per=(4, 0), after=pool_ready)
    DVE.need(ACTE.now())
    gemm(1, [(bhi, blo, SEQ)], evac_branch(False), kt=4, cols_=512, after=(ACTE.now(), DVE.now()))

    put = region(R0 + 4 * DT * SEQ)
    qT = put("q_T", [P, DIFF_HEADS, SEQ])
    kT = put("k_T", [P, DIFF_HEADS, SEQ])
    vt = put("v_tok", [P, NB, D_MODEL])
    ao = put("attn_tok", [P, NB, D_MODEL])
    work = put
    m = meet()
    mod_open(put.end, *m)
    gemm(2, X, evac_copy(dest(qT, SEQ), scale=DIFF_DH ** -0.5), per=(2, 2 + 2 * MOD_SIGNALS), after=m, mod=(0, 0))
    gemm(2, X, evac_copy(dest(kT, SEQ)), per=(2, 2 + 2 * MOD_SIGNALS), mod=(0, 4))
    gemm_tokens(2, [(hhi, hlo, b) for b in range(NB)], vt, lambda i, p: i * 512 + p * 256, after=m, mod=(0, 8))
    m = meet()
    awork = region(C0)
    sc2 = [awork(f"diff_s{n}", [P, 2, SEQ]) for n in range(3)]
    aT = [awork(f"diff_aT{n}", [P, SEQ]) for n in range(2)]
    qs2 = work("q2_staged", [P, 2, 2, SEQ])
    assert awork.end <= C0 + 16384
    dist = work("distance", [P, SEQ])
    assert work.end <= R_END, work.end
    load(nc.scalar, dist[:], a["t_distance"])
    need_inputs(DVE)

    DVE.sig(nc.vector.memset(qs2[:], 0.0))
    HPI = 4
    with loop(DIFF_HEADS // HPI, pe=3 * HPI * NB, act=3 * HPI * NB, dve=2 * HPI + 7 * HPI * NB) as it:
        act0, dve0 = ACTE.now(), DVE.now()
        DVE.need(PE.now(), dve0)
        staged = {}

        def stage(e):
            for c in range(2):
                part = slice(c * DIFF_DH, (c + 1) * DIFF_DH)
                staged[e] = DVE.sig(nc.vector.tensor_copy(qs2[part, e % 2, c, :], qT[part, bass.ds(HPI * it + e, 1), :]
                                                          .rearrange("p a n -> p (a n)")))

        stage(0)
        PE.need(act0, dve0)
        biased, expd, comb, tdone, pvd, copied, outd, scored = {}, {}, {}, {}, {}, {}, {}, {}

        def where(u):
            return u % NB, u // NB, (u % NB + 1) * P

        def scores(u):
            (i, e, n), b = where(u), 2 * (u % 2)
            PE.need(biased.get(u - 2))
            if i == 0:
                PE.need(staged[e])
            for c in range(2):
                ins = nc.tensor.matmul(bank(b + c, n), qs2[:, e % 2, c, i * P:(i + 1) * P],
                                       dyn(kT, HPI * it + e, slice(0, n)))
            scored[u] = PE.sig(ins)

        def stats(u):
            return sm[:, 6 * (u % 5):6 * (u % 5) + 6]

        def softmax(u):
            (i, e, n), b, S, st_ = where(u), 2 * (u % 2), sc2[u % 3], stats(u)
            DVE.need(scored[u], tdone.get(u - 3), comb.get(u - 3), outd.get(u - 5))
            for c in range(2):
                m = DVE.sig(nc.vector.scalar_tensor_tensor(
                    S[:, c, 0:n], dist[:, (NB - 1 - i) * P:(NB - 1 - i) * P + n],
                    slopes[:, bass.ds(HPI * it + e, 1)], bank(b + c, n), ALU.mult, ALU.add))
            biased[u] = m
            DVE.need(m)
            m = DVE.sig(nc.vector.tensor_reduce(st_[:, 0:2], S[:, :, 0:n], AX, ALU.max, negate=True))
            ACTE.need(m)
            for c in range(2):
                expd[u] = act(S[:, c, 0:n], S[:, c, 0:n], ACT.Exp, bias=st_[:, c:c + 1], accum_out=st_[:, 2 + c:3 + c])

        def combine(u):
            (i, e, n), S, st_ = where(u), sc2[u % 3], stats(u)
            DVE.need(expd[u])
            m = DVE.sig(nc.vector.reciprocal(st_[:, 4:6], st_[:, 2:4]))
            DVE.need(m)
            m = DVE.sig(nc.vector.scalar_tensor_tensor(st_[:, 5:6], st_[:, 5:6], nlam, st_[:, 2:3], ALU.mult, ALU.mult))
            DVE.need(m)
            comb[u] = DVE.sig(nc.vector.scalar_tensor_tensor(S[:, 0, 0:n], S[:, 1, 0:n], st_[:, 5:6], S[:, 0, 0:n],
                                                             ALU.mult, ALU.add))

        def turn(u):
            (i, e, n), S = where(u), sc2[u % 3]
            PE.need(comb[u], copied.get(u - 1))
            for k in range(i + 1):
                ins = nc.tensor.transpose(bank(4, P, k * P), S[:, 0, k * P:(k + 1) * P], ident[:])
            tdone[u] = PE.sig(ins)
            ACTE.need(tdone[u], pvd.get(u - 2))
            copied[u] = act(aT[u % 2][:, 0:n], bank(4, n))

        def values(u):
            i, e, n = where(u)
            head = HPI * it + e
            PE.need(copied[u], outd.get(u - 2))
            for k in range(i + 1):
                ins = nc.tensor.matmul(bank(6 + u % 2, P), aT[u % 2][:, k * P:(k + 1) * P],
                                       vt[:, k, bass.ds(head * P, P)], start=k == 0, stop=k == i)
            pvd[u] = PE.sig(ins)

        def output(u):
            i, e, n = where(u)
            DVE.need(pvd[u])
            outd[u] = DVE.sig(nc.vector.tensor_scalar(ao[:, i, bass.ds((HPI * it + e) * P, P)], bank(6 + u % 2, P),
                                                      stats(u)[:, 4:5], None, ALU.mult))

        N_U = HPI * NB
        for s in range(N_U + 5):
            if s < N_U:
                scores(s)
            if 0 <= s - 1 < N_U:
                softmax(s - 1)
            if 0 <= s - 5 < N_U:
                output(s - 5)
            if s % NB == 1 and s // NB + 1 < HPI:
                DVE.need(scored.get(s - 2))
                stage(s // NB + 1)
            if 0 <= s - 2 < N_U:
                combine(s - 2)
            if 0 <= s - 3 < N_U:
                turn(s - 3)
            if 0 <= s - 4 < N_U:
                values(s - 4)
    attended = (ACTE.now(), DVE.now())
    m = DVE.now()
    DVE.need(m, PE.now(), ACTE.now())
    ao_h = ao[:].rearrange("p b (h d) -> p (b h) d", h=DIFF_HEADS)
    DVE.need(DVE.sig(nc.vector.tensor_tensor(qT[:].rearrange("p h n -> p (h n)"), ao[:].rearrange("p b n -> p (b n)"),
                                             ao[:].rearrange("p b n -> p (b n)"), ALU.mult)))
    hs = small[:, 96:128]
    m = DVE.sig(nc.vector.tensor_reduce(hs, qT[:].rearrange("p h (b d) -> p (h b) d", d=P), AX, ALU.add))
    ACTE.need(m)
    m = act(small[:, 128:160], hs, ACT.Sqrt, scale=1.0 / P, bias=eps)
    nc.scalar.preload_act_table(ACT.Exp)
    DVE.need(m)
    DVE.need(DVE.sig(nc.vector.reciprocal(hs, small[:, 128:160])))
    m = DVE.sig(nc.vector.tensor_tensor(ao_h, ao_h, hs.unsqueeze(2).to_broadcast([P, NB * DIFF_HEADS, P]),
                                        ALU.mult))
    put = region(R0 + 4 * DT * SEQ)
    ahi, alo = put("a_hi", [P, DT, SEQ], F32R), put("a_lo", [P, DT, SEQ], F32R)
    gate = region(R0 + 3 * 4 * DT * SEQ)("gate_attn", [P, DT, SEQ])
    gemm(2, X, evac_gate, per=(4, 0), entry=attended)
    a_ready = token_to_split(ao, DT, NB, ahi, alo, (ACTE.now(), DVE.now()), gain=subg)
    PE.need(*a_ready)
    DVE.need(ACTE.now())
    gemm(2, [(ahi, alo, SEQ)], evac_branch(False), per=(0, 8), after=(ACTE.now(), DVE.now()))
    m = (PE.now(), ACTE.now(), DVE.now())

    def split_tiles(src, hi, lo, n, after):
        ACTE.need(*after)
        DVE.need(*after)
        return [split(hi[:, t, :], lo[:, t, :], src[:, t, :], None)[1] for t in range(n)]

    class Summed:

        def __init__(self, place, tag):
            self.acc = place("sum_" + tag, [P, SEQ])
            self.sq = [place(f"square_{tag}{n}", [P, SEQ]) for n in range(2)]

        def clear(self):
            DVE.sig(nc.vector.memset(self.acc[:], 0.0))

        def add(self, u, src, *marks):
            ACTE.need(DVE.now(), *marks)
            g = act(self.sq[u % 2][:], src, ACT.Square)
            DVE.need(g, DVE.now())
            DVE.sig(nc.vector.tensor_tensor(self.acc[:], self.acc[:], self.sq[u % 2][:], ALU.add))
            return g

    def evac_summed(dst_of, total):
        @owns((2, 0), (2, 0))
        def ev_(i, u, m):
            ACTE.need(m)
            act(dst_of(i, u), bank(u % 4))
            return (total.add(u, bank(u % 4)),)
        return ev_

    def add_normed(y, gain_name, total, tag):
        w = region(C0)
        dg = w("dg" + tag, [P, SEQ])
        tmp = [w(f"t{n}{tag}", [P, SEQ]) for n in range(2)]
        m = spread_cols(SEQ, dg, rstd_of_sum(total.acc, SEQ, DVE.now()))
        DVE.need(m)
        scaled, ready = {}, []
        for t in range(DT + 1):
            if t < DT:
                DVE.need(ready[t - 2] if t >= 2 else None)
                scaled[t] = DVE.sig(nc.vector.scalar_tensor_tensor(tmp[t % 2][:], y[:, t, :], col(gain_name, t), bank(6),
                                                                   ALU.mult, ALU.mult))
            if t:
                DVE.need(scaled[t - 1])
                ready.append(DVE.sig(nc.vector.tensor_tensor(xT[:, t - 1, :], xT[:, t - 1, :], tmp[(t - 1) % 2][:],
                                                             ALU.add)))
        return ready

    mx_ready = split_tiles(mixT, ahi, alo, DT, m)
    yT = region(R0)("y_T", [P, DT, SEQ])
    ACTE.need(mx_ready[-1])
    mix_sum = Summed(region(C0 + 6144), "mix")
    mix_sum.clear()
    gemm(2, [(ahi, alo, SEQ)], evac_summed(dest(yT, SEQ), mix_sum), per=(8, 4), ready=[mx_ready], entry=m)
    x_tiles = add_normed(yT, "norm_mix_post", mix_sum, "_mix")

    h2 = norm_split(xT, SEQ, hhi, hlo, lambda t: col("norm_ffn_pre", t), region(R0 + 20480), (),
                    ready=x_tiles, bank_=5)
    put = region(R0)
    fhi, flo = put("f_hi", [P, FT, SEQ], F32R), put("f_lo", [P, FT, SEQ], F32R)
    assert put.end <= R_END, (put.end, R_END)
    cw = region(C0)
    cbuf = [cw(f"conv{n}", [P, SEQ]) for n in range(4)]
    gel = [cw(f"gel{n}", [P, SEQ]) for n in range(2)]
    ACTE.need(h2[-1])
    nc.scalar.preload_act_table(ACT.Gelu_apprx_tanh)

    conv_marks = {}

    def evac_ffn(i, u, m):
        t = 2 * i + u % 2 + (FT if u >= 2 else 0)
        w = cbuf[u]
        ACTE.need(m, DVE.now().minus(12 - (4 if u >= 2 else 2)), ACTE.now().minus(8 - 2))
        g = act(w[:], bank(u), ACT.Identity, scale=dyn_col("conv_w", t + 2 * 2 * FT), bias=dyn_col("conv_b", t))
        DVE.need(g)
        g = DVE.sig(nc.vector.scalar_tensor_tensor(w[:, 1:], bank(u, SEQ - 1), dyn_col("conv_w", t + 2 * FT), w[:, 1:],
                                                   ALU.mult, ALU.add))
        DVE.need(g)
        g = DVE.sig(nc.vector.scalar_tensor_tensor(w[:, 2:], bank(u, SEQ - 2), dyn_col("conv_w", t), w[:, 2:],
                                                   ALU.mult, ALU.add))
        if u < 2:
            ACTE.need(g, conv_marks["start"].minus(12 - (7 if u == 0 else 11)))
            conv_marks[u] = act(gel[u][:], w[:], ACT.Gelu_apprx_tanh)
            return (g,)
        DVE.need(g, conv_marks[u - 2])
        p_ = DVE.sig(nc.vector.tensor_tensor(w[:], w[:], gel[u - 2][:], ALU.mult))
        j = 2 * i + (u - 2)
        ACTE.need(p_)
        q_ = act(dyn(fhi, j, slice(0, SEQ)), w[:])
        DVE.need(q_)
        DVE.sig(nc.vector.tensor_tensor(dyn(flo, j, slice(0, SEQ)), w[:], f(dyn(fhi, j, slice(0, SEQ))), ALU.subtract))
        return (g,)

    base_chunk = chunk[0]
    with loop(D_FF // 256, pe=4, act=8, dve=12) as i:
        conv_marks["start"] = DVE.now()
        for p in range(2):
            PE.e.wait_ge(lo_done, base_chunk + p + 1 + 2 * i)
            hi = whi[p][:].rearrange("p (k n) -> p k n", k=DT)
            lo = wlo[p][:].rearrange("p (k n) -> p k n", k=DT)
            for o in range(2):
                PE.need(DVE.now().minus(12 - 2))
                for k in range(DT):
                    if p == 0 and o == 0:
                        PE.need(h2[k])
                    ins = mm3(bank(2 * p + o), hi[:, k, o * P:(o + 1) * P], lo[:, k, o * P:(o + 1) * P],
                              hhi[:, k, :], hlo[:, k, :], k == 0, k == DT - 1)
                m = PE.sig(ins)
                evac_ffn(i, 2 * p + o, m)
            ACTE.need(m)
            round_hi(p, base_chunk + p + 2, i, 2)
    chunk[0] += D_FF // 128
    nc.scalar.preload_act_table(ACT.Exp)

    ydn = nc.alloc_sbuf_tensor_at("y_down", [P, DT, SEQ], F32, offset=C0 - 2 * 16384)
    cin = nc.alloc_sbuf_tensor_at("ctx_in", [P, CB, D_MODEL], F32, offset=C0 - 16384)
    m = (PE.now(), ACTE.now(), DVE.now())
    nc.scalar.wait_ge(PE.sem, PE.n)
    load(nc.scalar, cin[:], a["ctx_2"][0].rearrange("(b p) d -> p b d", p=P))
    c_landed = landed[0]
    for x_ in (PE, ACTE, DVE):
        x_.need(*m)
    mod_open(C0 - 2048, *m)
    down_sum = Summed(region(C0 - 16384 + 4 * CB * D_MODEL), "down")
    down_sum.clear()
    base_chunk = chunk[0]
    with loop(2, pe=6, act=8, dve=4 + 6 * MOD_SIGNALS) as i:
        before = (ACTE.now(), DVE.now())
        mod_free = [DVE.now()] * 2
        PE.need(*before)
        for q in range(6):
            g, kk = divmod(q, 3)
            p = q % 2
            kt = min(8, FT - 8 * kk)
            PE.e.wait_ge(lo_done, base_chunk + q + 1 + 6 * i)
            hi = whi[p][:, 0:kt * 256].rearrange("p (k n) -> p k n", k=kt)
            lo = wlo[p][:, 0:kt * 256].rearrange("p (k n) -> p k n", k=kt)
            weighed = mod_weigh(1, q, i, 6)
            for o in range(2):
                for k in range(kt):
                    kf = 8 * kk + k
                    ins = mm3(bank(2 * g + o), hi[:, k, o * P:(o + 1) * P], lo[:, k, o * P:(o + 1) * P],
                              fhi[:, kf, :], flo[:, kf, :], kf == 0, kf == FT - 1)
            m = PE.sig(ins)
            mod_free[q % 2] = mod_product(1, q, i, 6, weighed, mod_free[q % 2])
            ACTE.need(m)
            round_hi(p, base_chunk + q + 2, i, 6)
            if kk == 2:
                for o in range(2):
                    act(dyn(ydn, 4 * i + 2 * g + o, slice(0, SEQ)), bank(2 * g + o))
                    down_sum.add(o, bank(2 * g + o))
    chunk[0] += 12
    m = (PE.now(), ACTE.now(), DVE.now())
    cT = nc.alloc_sbuf_tensor_at("ctx_T", [P, DT, CTX], F32, offset=R0)
    for x_ in (ACTE, DVE):
        x_.need(*m)
    PE.e.wait_ge(sem_in, c_landed)
    after_down = m
    x_tiles = add_normed(ydn, "norm_ffn_post", down_sum, "_ffn")
    c_ready = to_feature_major(cin, CB, cT, after_down, only_act=True)

    put = region(R0 + 4 * DT * CTX)
    MOVED_AT = dict(B=R0 + 4 * DT * CTX)
    qT3 = {x_: put(f"q_{x_}", [P, 4, ALL]) for x_ in "AB"}
    kk_ = {x_: put(f"k_{x_}", [P, ALL]) for x_ in "AB"}
    v3 = {x_: put(f"v_{x_}", [P, ALL // P, P]) for x_ in "AB"}
    probs2 = [put(f"probs2_{n}", [P, ALL]) for n in range(2)]
    probsT2 = [put(f"probsT2_{n}", [P, ALL]) for n in range(2)]
    ao2 = {x_: put(f"attn2_tok_{x_}", [P, ALL // P, 512]) for x_ in "AB"}
    rest = put.end
    MOVED_AT["A"] = rest - 4 * (ALL // P) * 512
    assert rest <= R_END, (rest, R_END)
    gsc = small[:, 160:192].rearrange("p (n t) -> p n t", n=4)

    def mod(layer, part, cond_):
        return modT[:, layer, part * DT:(part + 1) * DT, cond_]

    DVE.need(DVE.now())
    for layer in range(2):
        for cn in range(2):
            g0 = places["norm_g_2"] + layer * DT
            gm = DVE.sig(nc.vector.scalar_tensor_tensor(gsc[:, 2 * layer + cn, :], mod(layer, 1, cn), 1.0,
                                                        cols[:, g0:g0 + DT], ALU.add, ALU.mult))

    def modulated(layer, after, ready, summed=None):
        work = region(rest - 6 * 4096 + (4 * SEQ if summed else 0))
        hr = norm_split(xT, SEQ, hhi, hlo, lambda t: gsc[:, 2 * layer, t:t + 1], work,
                        (*after, gm), lambda t: modT[:, layer, t, 0:1], ready=ready, bank_=5, summed=summed)
        cr = Norm(cT, CTX, chi, clo, lambda t: gsc[:, 2 * layer + 1, t:t + 1], region(rest - 6 * 4096 + 12288),
                  (), lambda t: modT[:, layer, t, 1:2])
        return hr, cr

    hx, c_norm = modulated(0, c_ready, x_tiles)

    def evac_both(dst, scale):
        def ev_(i, u, m):
            ACTE.need(m)
            DVE.need(m)
            return (act(dst[:, u, CTX:], bank(u), scale=scale),
                    DVE.sig(nc.vector.tensor_scalar(dst[:, u, 0:CTX], bank(4 + u, CTX), scale, None, ALU.mult)))
        return ev_

    t2 = region(MOVED_AT["A"] - 12288)
    rms10 = t2("rms10", [P, ALL])
    inv10 = t2("inv10", [P, ALL])
    turned_ = [t2(f"rope_turned{n}", [P, SEQ]) for n in range(2)]
    assert t2.end <= MOVED_AT["A"]
    t3 = region(rest)
    cosT = t3("cos_T", [P, SEQ])
    sinT = t3("sin_T", [P, SEQ])
    rotm = t3("rotate", [P, P])
    gat = t3("head_gather", [P, 5, 10])
    spr = t3("head_spread", [P, 5, P])
    bl, br = t3("band_left", [P, P]), t3("band_right", [P, P])
    assert t3.end <= R_END
    sqw = region(MOVED_AT["A"] - 12288 - 4 * 4 * ALL)
    sq_tile = [sqw(f"q_squares{n}", [P, ALL]) for n in range(4)]

    gemm(1, XC, evac_both(qT3["A"], 1.0), ready=[hx, None], middle=c_norm.finish,
         entry=after_down)
    m = (ACTE.now(), DVE.now())
    nc.scalar.wait_ge(DVE.sem, DVE.n)
    load(nc.scalar, gat[:], a["t_head_gather"].rearrange("p (n c) -> p n c", n=5))
    load(nc.scalar, spr[:], a["t_head_spread"].rearrange("p (n c) -> p n c", n=5))
    load(nc.scalar, cosT[:], a["t_rope_cos"])
    load(nc.scalar, sinT[:], a["t_rope_sin"])
    load(nc.scalar, rotm[:], a["t_rotate"])
    load(nc.scalar, bl[:], a["t_band_left"])
    load(nc.scalar, br[:], a["t_band_right"])
    A_tiles = [qT3["A"][:, n, :] for n in range(4)] + [kk_["A"][:]]
    ACTE.need(ACTE.now(), DVE.now())
    squared_ = [act(sq_tile[n][:], A_tiles[n], ACT.Square) for n in range(4)]
    gemm(1, XC, evac_both(qT3["B"], HEAD ** -0.5), entry=m)

    def add_squares(n, w):
        nc.tensor.matmul(bank(6, 512, 0, 10), gat[:, n, :], w[:, 0:512], start=n == 0, stop=n == 4)
        return PE.sig(nc.tensor.matmul(bank(7, 256, 0, 10), gat[:, n, :], w[:, 512:ALL], start=n == 0, stop=n == 4))

    rope_free = {4: None, 5: None}

    def rope(tl, b, m):
        s = tl[:, CTX:]
        PE.need(m, rope_free[b])
        m = PE.sig(nc.tensor.matmul(bank(b), rotm[:], s))
        DVE.need(m)
        w = turned_[b % 2][:]
        g = DVE.sig(nc.vector.tensor_tensor(w, bank(b), sinT[:], ALU.mult))
        rope_free[b] = g
        DVE.need(DVE.sig(nc.vector.tensor_tensor(s, s, cosT[:], ALU.mult)), g)
        return DVE.sig(nc.vector.tensor_tensor(s, s, w, ALU.add))

    need_inputs(PE, DVE)
    PE.need(*squared_, ACTE.now(), DVE.now())
    for n in range(4):
        add_squares(n, sq_tile[n])
    kv_before = (ACTE.now(), DVE.now())

    def keys_values(p, x_, before, middle):
        PE.need(*before)
        PE.e.wait_ge(lo_done, chunk[0] + p + 1)
        hi = whi[p][:].rearrange("p (k n) -> p k n", k=DT)
        lo = wlo[p][:].rearrange("p (k n) -> p k n", k=DT)
        for n, (xh, xl, tok) in enumerate(XC):
            for k in range(DT):
                ins = mm3(bank(n, tok), hi[:, k, 0:P], lo[:, k, 0:P], xh[:, k, 0:tok], xl[:, k, 0:tok],
                          k == 0, k == DT - 1)
        m = PE.sig(ins)
        ACTE.need(m)
        act(kk_[x_][:, CTX:], bank(0))
        act(kk_[x_][:, 0:CTX], bank(1, CTX))
        k_there = ACTE.now()
        middle(k_there)
        blocks = [(hhi, hlo, b) for b in range(NB)] + [(chi, clo, b) for b in range(CB)]
        for n, (xh, xl, blk) in enumerate(blocks):
            ts = slice(blk * P, (blk + 1) * P)
            for k in range(DT):
                ins = mm3(bank(2 + n // NB, P, n % NB * P), hi[:, k, P:2 * P], lo[:, k, P:2 * P],
                          xh[:, k, ts], xl[:, k, ts], k == 0, k == DT - 1, flip=True)
        m = PE.sig(ins)
        ACTE.need(m)
        v_ = v3[x_][:].rearrange("p b n -> p (b n)")
        act(v_[:, CTX:], bank(2))
        act(v_[:, 0:CTX], bank(3, CTX))
        return k_there, ACTE.now()

    def middle_a(k_there):
        for n in (0, 1):
            rope(qT3["B"][:, n, :], 4 + n, None)

    def middle_b(k_there):
        ACTE.need(k_a)
        PE.need(act(sq_tile[0][:], kk_["A"][:], ACT.Square))
        ACTE.need(add_squares(4, sq_tile[0]))
        m = act(rms10[0:10, :], ps[0:10, 6 * 512:6 * 512 + ALL], ACT.Sqrt, bias=eps[0:10], scale=1.0)
        nc.scalar.preload_act_table(ACT.Exp)
        DVE.need(m)
        stat["inv"] = DVE.sig(nc.vector.reciprocal(inv10[0:10, :], rms10[0:10, :]))

    moved, keys_of = {}, {}
    for x_ in "AB":
        place = region(MOVED_AT[x_])
        moved[x_] = [place(f"keys_moved_{x_}{n}", [P, ALL]) for n in range(3)]
        keys_of[x_] = ((kk_[x_], moved[x_][0]), (moved[x_][1], moved[x_][2]))

    def clear_keys(x_):
        for kv, h in ((0, 1), (1, 0), (1, 1)):
            m = DVE.sig(nc.vector.memset(keys_of[x_][kv][h][(1 - h) * HEAD:(2 - h) * HEAD, :], 0.0))
        return m

    def move_keys(x_, m):
        K = kk_[x_]
        ACTE.need(m)
        for kv, h in ((0, 1), (1, 0), (1, 1)):
            m = act(keys_of[x_][kv][h][h * HEAD:(h + 1) * HEAD, :], K[kv * HEAD:(kv + 1) * HEAD, :])
        return m

    clear_keys("A")
    stat = {}
    k_a, v_a = keys_values(0, "A", kv_before, middle_a)
    round_hi(0, chunk[0] + 2)
    for n in (2, 3):
        rope(qT3["B"][:, n, :], 2 + n, None)
    k_b, v_b = keys_values(1, "B", (v_a,), middle_b)
    round_hi(1, chunk[0] + 3)
    chunk[0] += 2
    PE.need(stat["inv"], v_b)
    freed_, order = {}, (4, 0, 1, 2, 3)
    for n in range(6):
        if n < 5:
            b, t = (6, 0)[n % 2], order[n]
            PE.need(freed_.get(n - 2))
            nc.tensor.matmul(bank(b), spr[0:10, t, :], inv10[0:10, 0:512])
            m = PE.sig(nc.tensor.matmul(bank(b + 1, 256), spr[0:10, t, :], inv10[0:10, 512:ALL]))
            DVE.need(m)
            gcol = qgain if t < 4 else col("a_k_gain_2")
            freed_[n] = DVE.sig(nc.vector.scalar_tensor_tensor(A_tiles[t], A_tiles[t], gcol,
                                                               ps[:, b * 512:b * 512 + ALL], ALU.mult, ALU.mult))
        if n == 0:
            rope(kk_["B"][:], 4, k_b)
        else:
            m = rope(A_tiles[order[n - 1]], 4 + n % 2, freed_[n - 1])
        if n == 1:
            keys_moved = move_keys("A", m)
    DVE.need(keys_moved)
    DVE.sig(nc.vector.memset(kk_["A"][HEAD:2 * HEAD, :], 0.0))
    m = meet()

    tail = region(rest)
    qst = [tail(f"q3_staged{n}", [P, ALL]) for n in range(2)]

    def q_units(x_, kv, j, s):
        K = keys_of[x_][kv][s][:]
        us = []
        head = 4 * kv + 2 * j + s
        c0 = (2 * kv + j) * P + s * HEAD
        V = v3[x_]
        vs = slice(kv * HEAD, (kv + 1) * HEAD)
        extra = {} if x_ == "A" else dict(sink=sink[:, bass.ds(head, 1)], nsink=nsink[:, bass.ds(head, 1)])
        for i in range(NB):
            q = qst[kv][:, CTX + i * P:CTX + (i + 1) * P]
            if x_ == "A":
                sc = [(0, 512, q, K[:, 0:512]), (512, 256, q, K[:, 512:ALL])]
                us.append(dict(scores=sc, n=ALL, values=[V[:, k, vs] for k in range(6)]))
            else:
                b0, b1 = max(i - 1, 0), min(i + 2, NB)
                w = (b1 - b0) * P
                k0 = CTX + b0 * P
                w1 = min(w, 256)
                sc = [(0, CTX, q, K[:, 0:CTX]), (CTX, w1, q, K[:, k0:k0 + w1])]
                if w > w1:
                    sc.append((CTX + w1, w - w1, q, K[:, k0 + w1:k0 + w]))
                bias = []
                if i > 0:
                    bias.append((CTX, P, bl[:]))
                if i < NB - 1:
                    bias.append((CTX + w - P, P, br[:]))
                us.append(dict(scores=sc, n=CTX + w, bias=bias,
                               values=[V[:, k, vs] for k in (0, 1, *range(CB + b0, CB + b1))]))
            us[-1]["out"] = ao2[x_][:, CB + i, bass.ds(c0, HEAD)]
        for i in range(CB):
            q = qst[kv][:, i * P:(i + 1) * P]
            us.append(dict(scores=[(0, CTX, q, K[:, 0:CTX])], n=CTX,
                           values=[V[:, k, vs] for k in range(CB)], out=ao2[x_][:, i, bass.ds(c0, HEAD)]))
        for u_ in us:
            u_.update(dh=HEAD, **extra)
        return us

    for x_ in "AB":
        if x_ == "B":
            DVE.need(PE.now(), ACTE.now())
            DVE.need(move_keys("B", clear_keys("B")))
            PE.need(DVE.sig(nc.vector.memset(kk_["B"][HEAD:2 * HEAD, :], 0.0)))
        n_u = 4 * (NB + CB)
        acts, dves = (2 * n_u, 4 * n_u) if x_ == "A" else (3 * n_u, 6 * n_u + 4 * (2 * NB - 2))
        with loop(2, pe=3 * n_u, act=acts + 2, dve=dves) as j:
            ACTE.need(PE.now().minus(6))
            for kv in range(2):
                act(qst[kv][:], dyn(qT3[x_], 2 * kv + j, slice(0, ALL)))
            Attention(probs2, probsT2).run([u for kv in range(2) for h in range(2) for u in q_units(x_, kv, j, h)])
    m = meet()

    put = region(R0 + 8192)
    ghi = put("g_hi", [P, DT, ALL], F32R)
    gw = region(rest)
    silu_t = [gw(f"silu{n}", [P, ALL]) for n in range(2)]
    assert gw.end <= R_END
    glo_at = put.end
    assert glo_at + 4 * DT * ALL <= rest - 4 * 6 * D_MODEL
    glo = nc.alloc_sbuf_tensor_at("g_lo", [P, DT, ALL], F32R, offset=glo_at)

    def gated(tile_base, n_blocks, ao_, xs, hi_, lo_, tile_of, silu_, prod_, between={}):
        tot = n_blocks * P
        for p in range(2):
            PE.e.wait_ge(lo_done, chunk[0] + p + 1)
            hi = whi[p][:].rearrange("p (k n) -> p k n", k=DT)
            lo = wlo[p][:].rearrange("p (k n) -> p k n", k=DT)
            for o in range(2):
                u = 2 * p + o
                t = tile_base + u
                b = 4 * (u % 2)
                PE.need(gf.get(u % 2))
                pos = 0
                for n, (xh, xl, tok) in enumerate(xs):
                    for k in range(DT):
                        ins = mm3(bank(b + n, tok), hi[:, k, o * P:(o + 1) * P], lo[:, k, o * P:(o + 1) * P],
                                  xh[:, k, 0:tok], xl[:, k, 0:tok], k == 0, k == DT - 1)
                for k in range(n_blocks):
                    c, off = (b + 3, k * P) if n_blocks > NB and k < CB else (b + 2, (k - (n_blocks - NB)) * P)
                    ins = nc.tensor.transpose(bank(c, P, off), ao_[:, k, t * P:(t + 1) * P], ident[:])
                m = PE.sig(ins)
                if u in between:
                    between[u]()
                ACTE.need(m, gf.get(u % 2))
                parts = [(tot - SEQ, SEQ, b, b + 2)] + ([(0, CTX, b + 1, b + 3)] if tot > SEQ else [])
                S_, R_ = silu_[u % 2], prod_[u % 2]
                for off, n, gb, ab in parts:
                    g = act(S_[:, off:off + n], bank(gb, n), ACT.Tanh, scale=0.5)
                DVE.need(g)
                for off, n, gb, ab in parts:
                    g = DVE.sig(nc.vector.scalar_tensor_tensor(S_[:, off:off + n], S_[:, off:off + n], 1.0, bank(gb, n),
                                                               ALU.add, ALU.mult))
                DVE.need(g)
                for off, n, gb, ab in parts:
                    g = DVE.sig(nc.vector.scalar_tensor_tensor(R_[:, off:off + n], S_[:, off:off + n], 0.5, bank(ab, n),
                                                               ALU.mult, ALU.mult))
                _, gf[u % 2] = split(hi_[:, tile_of(u), :], lo_[:, tile_of(u), :], R_[:, 0:tot], g)
            ACTE.need(m)
            round_hi(p, chunk[0] + p + 2)
        chunk[0] += 2

    gf = {}
    gated(0, 6, ao2["A"], XC, ghi, glo, lambda u: u, silu_t, silu_t)
    gated(0, 6, ao2["B"], XC, ghi, glo, lambda u: 4 + u, silu_t, silu_t)
    m = (DVE.now(), ACTE.now(), PE.now())
    ACTE.need(*m)

    def evac_residual(layer, ctx, total):
        @owns(*[(0, 1 + ctx)] * 2)
        def ev_(i, u, m):
            j = 4 * i + u
            DVE.need(m)
            mf = modT[:].rearrange("p l t c -> p (l t) c")
            gl = mf[:, bass.ds(layer * 24 + 16 + j, 1), 0]
            r = [DVE.sig(nc.vector.scalar_tensor_tensor(dyn(xT, j, slice(0, SEQ)), bank(u), gl,
                                                        dyn(xT, j, slice(0, SEQ)), ALU.mult, ALU.add))]
            if ctx:
                gc = mf[:, bass.ds(layer * 24 + 16 + j, 1), 1]
                r.append(DVE.sig(nc.vector.scalar_tensor_tensor(dyn(cT, j, slice(0, CTX)), bank(4 + u, CTX), gc,
                                                                dyn(cT, j, slice(0, CTX)), ALU.mult, ALU.add)))
            total.add(u, dyn(xT, j, slice(0, SEQ)))
            return tuple(r)
        return ev_

    class Tail:

        def __init__(self, t, lo_):
            self.t, self.lo_ = t, lo_

        def __getitem__(self, k):
            a_, b_, c_ = k
            return self.t[a_, b_, self.lo_ + c_.start:self.lo_ + c_.stop]

    layer_sum = Summed(region(rest - 6 * 4096), "layer")
    layer_sum.clear()
    gemm(2, [(Tail(ghi, CTX), Tail(glo, CTX), SEQ), (Tail(ghi, 0), Tail(glo, 0), CTX)],
         evac_residual(0, True, layer_sum), per=(4, 12), after=m)
    m = meet()

    after_layer = m
    hx, c_norm = modulated(1, m, None, layer_sum)
    PADC = CONV_TAPS // 2
    O0 = R0 + 4 * DT * CTX
    put = region(O0)
    uT = put("u_T", [P, CT, SEQ + 2 * PADC + 2])
    yc = put("conv_y", [P, CT, SEQ])
    dq = put("dq_T", [P, 4, SEQ])
    dk = put("dk_T", [P, 4, ALL])
    dv = put("dv", [P, ALL // P, 512])
    aod = put("attn3_tok", [P, NB, 512])
    oend = put.end
    utmp = [nc.alloc_sbuf_tensor_at(f"u_tmp{n}", [P, SEQ], F32, offset=oend - 8192 + n * 2048) for n in range(2)]
    DVE.sig(nc.vector.memset(uT[:, :, 0:PADC], 0.0))
    DVE.sig(nc.vector.memset(uT[:, :, PADC + SEQ:], 0.0))
    u_marks = {}

    def evac_u(i, u, m):
        t = 2 * i + u % 2
        if u < 2:
            DVE.need(m)
            u_marks[u] = DVE.sig(nc.vector.tensor_copy(uT[:, t, PADC:PADC + SEQ], bank(u)))
            return (u_marks[u],)
        ACTE.need(m, u_marks.get("free%d" % u))
        g = act(utmp[u - 2][:], bank(u), ACT.Tanh, scale=0.5)
        DVE.need(g, u_marks[u - 2])
        w = uT[:, t, PADC:PADC + SEQ]
        DVE.need(DVE.sig(nc.vector.scalar_tensor_tensor(w, utmp[u - 2][:], 1.0, w, ALU.add, ALU.mult)))
        u_marks["free%d" % u] = DVE.sig(nc.vector.tensor_scalar(w, w, 0.5, None, ALU.mult))
        return (g,)

    gemm(1, X, evac_u, ready=[hx], entry=after_layer)
    u_banks = freed_banks[0]
    hc = c_norm.finish()
    gemm(1, X, lambda i, u, m: evac_u(1, u, m), before=u_banks)
    u_ready = DVE.now()
    def evac_act(dst_of, scale=1.0):
        def ev_(i, u, m):
            ACTE.need(m)
            return (act(dst_of(i, u), bank(u % 4, dst_of.n), scale=scale),)
        return ev_

    def evac_both_act(dst):
        def ev_(i, u, m):
            ACTE.need(m)
            act(dst[:, u, CTX:], bank(u))
            return (act(dst[:, u, 0:CTX], bank(4 + u, CTX)),)
        return ev_

    gemm(1, X, evac_act(dest(dq, SEQ), HEAD ** -0.5), after=(ACTE.now(), u_ready))
    gemm(1, XC, evac_both_act(dk), ready=[hx, hc])
    token_blocks = [(chi, clo, b) for b in range(CB)] + [(hhi, hlo, b) for b in range(NB)]
    gemm_tokens(1, token_blocks, dv, lambda i, p: p * 256, after=(ACTE.now(),), only_act=True)
    DVE.need(u_ready)
    conv_ready = []
    for n in range(CONV_TAPS):
        for t in range(CT):
            wcol = col("c_dw_w_2", n * CT + t)
            src = uT[:, t, n:n + SEQ]
            if n:
                DVE.need(conv_ready[t])
                g = DVE.sig(nc.vector.scalar_tensor_tensor(yc[:, t, :], src, wcol, yc[:, t, :], ALU.mult, ALU.add))
                conv_ready[t] = g
            else:
                conv_ready.append(DVE.sig(nc.vector.tensor_scalar(yc[:, t, :], src, wcol, col("c_dw_b_2", t),
                                                                  ALU.mult, ALU.add)))
    m = meet()

    SLOTS = 2 * NA_KH - 2
    W2 = SLOTS * GRID_W
    aw = region(C0)
    probs3 = [aw(f"probs3_{n}", [P, ALL]) for n in range(2)]
    qst3 = [aw(f"q4_staged{n}", [P, SEQ]) for n in range(2)]
    nmask = aw("near_mask", [P, GRID_W])
    rv = aw("reverse", [P, P])
    mean = aw("conv_mean", [P, SEQ])
    assert aw.end <= C0 + 16384, aw.end - C0
    bw = region(oend)
    grev = [bw(f"bias_reversed{n}", [P, W2]) for n in range(4)]
    probsT3 = [bw(f"probsT3_{n}", [P, ALL]) for n in range(2)]
    assert bw.end <= R_END, bw.end - R_END
    for t in range(CT):
        ins = nc.tensor.matmul(bank(7), ones[:], yc[:, t, :], start=t == 0, stop=t == CT - 1)
    summed = PE.sig(ins)
    load(nc.scalar, nmask[:], a["t_near_mask"])
    load(nc.scalar, rv[:], a["t_reverse"])
    sem_bias = [nc.alloc_semaphore(f"bias_landed{n}") for n in range(4)]
    LB = 2 * GRID_W - 1
    rp = a["rpb_padded"]

    def load_bias(head):
        for half in range(2):
            src = bass.AP(tensor=rp.tensor, offset=rp.offset + (head * (2 * NA_KH - 1) + 1 - half) * LB,
                          ap=[[1, GRID_W], [LB, SLOTS], [1, GRID_W]])
            nc.scalar.dma_start(grev[head % 4][half * 64:(half + 1) * 64, :].rearrange("p (d k) -> p d k", k=GRID_W),
                                src).then_inc(sem_bias[head % 4], 16)

    for head in range(4):
        load_bias(head)
    need_inputs(PE, DVE)
    for s in range(2):
        DVE.sig(nc.vector.memset(qst3[s][:], 0.0))
    head_ready = {}

    def prepare(head):
        s = head % 2
        part = slice(s * HEAD, (s + 1) * HEAD)
        if head >= 2:
            DVE.need(us[NB * (head - 1) - 1]["scored"])
        DVE.need(DVE.now())
        DVE.sig(nc.vector.tensor_copy(qst3[s][part, :], dq[part, head // 2, :]))
        DVE.e.wait_ge(sem_bias[head % 4], 32 * (head // 4 + 1))
        g = grev[head % 4][:].rearrange("p (d k) -> p d k", k=GRID_W)
        mk = bass.AP(tensor=nmask[:].tensor, offset=nmask[:].offset, ap=[list(nmask[:].ap[0]), [0, SLOTS], [1, GRID_W]])
        head_ready[head] = DVE.sig(nc.vector.tensor_tensor(g, g, mk, ALU.add))

    def next_head(head):
        if 4 <= head + 3 < 8:
            ACTE.need(us[NB * head - 1]["scored"])
            load_bias(head + 3)
        if head + 1 < 8:
            prepare(head + 1)

    prepare(0)
    ACTE.need(summed)
    m = act(mean[:], bank(7), scale=1.0 / 512)
    DVE.need(m)
    for t in range(CT):
        DVE.sig(nc.vector.tensor_tensor(yc[:, t, :], yc[:, t, :], mean[:], ALU.subtract))
    us = []
    for head in range(8):
        j, s = divmod(head, 2)
        c0 = head * HEAD
        for i in range(NB):
            q = qst3[s][:, i * P:(i + 1) * P]
            k0 = (NA_KH - 2 - 2 * i) * GRID_W
            u = dict(scores=[(0, 512, q, dk[:, j, 0:512]), (512, 256, q, dk[:, j, 512:ALL])], n=ALL,
                     added=[(CTX + h * 256, 256, rv[:], grev[head % 4][:, k0 + h * 256:k0 + (h + 1) * 256])
                            for h in range(2)], dh=HEAD, out=aod[:, i, c0:c0 + HEAD],
                     values=[dv[:, k, c0:c0 + HEAD] for k in range(6)])
            if i == 0:
                u["need"] = lambda head=head: (head_ready[head],)
            if i == 1:
                u["then"] = lambda head=head: next_head(head)
            us.append(u)
    Attention(probs3, probsT3).run(us)
    m = meet()

    ow = region(O0 + 8 * 2048 + 2304)
    ohi, olo = ow("o_hi", [P, DT, SEQ], F32R), ow("o_lo", [P, DT, SEQ], F32R)
    cg = region(C0)
    sg = [cg(f"sg{n}", [P, SEQ]) for n in range(2)]
    pg = [cg(f"pg{n}", [P, SEQ]) for n in range(2)]
    aod2 = nc.alloc_sbuf_tensor_at("attn3_moved", [P, NB, 512], F32, offset=ow.end + 8192)
    m = DVE.sig(nc.vector.tensor_copy(aod2[:], aod[:]))
    for x_ in (PE, ACTE, DVE):
        x_.need(m)
    fr = {}

    def evac_conv_gate(i, u, m):
        ACTE.need(m, fr.get(u - 2))
        g = act(sg[u % 2][:], bank(u), ACT.Tanh, scale=0.5)
        DVE.need(g)
        g = DVE.sig(nc.vector.scalar_tensor_tensor(sg[u % 2][:], sg[u % 2][:], 1.0, bank(u), ALU.add, ALU.mult))
        DVE.need(g)
        g2 = DVE.sig(nc.vector.scalar_tensor_tensor(pg[u % 2][:], sg[u % 2][:], 0.25, yc[:, u, :], ALU.mult, ALU.mult))
        _, fr[u] = split(ohi[:, u, :], olo[:, u, :], pg[u % 2][:], g2)
        return (g,)

    gf = {}
    lw = region(C0 + 8192)
    sqc = [lw(f"lsq{n}", [P, SEQ]) for n in range(CT)]
    dgl = sqc[0]
    ln, squared, scaled = {}, [], []
    for t in range(CT):
        y_ = yc[:, t, :]
        squared.append(DVE.sig(nc.vector.tensor_tensor(sqc[t][:], y_, y_, ALU.mult)) if t % 2 else
                       act(sqc[t][:], y_, ACT.Square))
    nc.scalar.preload_act_table(ACT.Sqrt)

    def ln_variance():
        for t in range(CT):
            PE.need(squared[t])
            for b in range(NB):
                ins = nc.tensor.matmul(bank(7, 1, b), sqc[t][:, b * P:(b + 1) * P], ones[:, 0:1],
                                       start=t == 0 and b == 0, stop=t == CT - 1, skip_group_check=True)
        ln["summed"] = PE.sig(ins)
        ACTE.need(ln["summed"])
        ln["rms"] = act(st[:, 0:NB], bank(7, NB), ACT.Sqrt, scale=1.0 / 512, bias=eps)
        nc.scalar.preload_act_table(ACT.Exp)

    def ln_scale():
        DVE.need(ln["rms"])
        m = DVE.sig(nc.vector.reciprocal(st[:, 8:8 + NB], st[:, 0:NB]))
        DVE.need(spread_cols(SEQ, dgl, m, 5))
        for t in range(CT):
            scaled.append(DVE.sig(nc.vector.scalar_tensor_tensor(yc[:, t, :], yc[:, t, :], col("c_ln_g_2", t), bank(5),
                                                                 ALU.mult, ALU.mult)))

    def ln_silu():
        turned = {}
        for t in range(CT):
            ACTE.need(scaled[t])
            ACTE.need(act(yc[:, t, :], yc[:, t, :], ACT.Identity, bias=col("c_ln_b_2", t)), turned.get(t - 2))
            DVE.need(act(sqc[2 + t % 2][:], yc[:, t, :], ACT.Tanh, scale=0.5))
            turned[t] = DVE.sig(nc.vector.scalar_tensor_tensor(yc[:, t, :], sqc[2 + t % 2][:], 1.0, yc[:, t, :],
                                                               ALU.add, ALU.mult))
    gated(0, NB, aod2, X, ohi, olo, lambda u: 4 + u, sg, pg, {0: ln_variance, 1: ln_scale, 2: ln_silu})
    m = meet()
    fr = {}
    gemm(1, X, evac_conv_gate)
    m = (PE.now(), ACTE.now(), DVE.now())
    final_sum = Summed(region(R0), "final")
    final_sum.clear()
    gemm(2, [(ohi, olo, SEQ)], evac_residual(1, False, final_sum), per=(4, 8), after=m, last=True)

    fw = region(O0)
    dgf = final_sum.acc
    tok = fw("out_tok", [P, NB, D_MODEL])
    sem_out = nc.alloc_semaphore("output_stored")
    m = spread_cols(SEQ, dgf, rstd_of_sum(dgf, SEQ, DVE.now()))
    ACTE.need(PE.now())
    DVE.need(m)
    for t in range(DT):
        m = DVE.sig(nc.vector.scalar_tensor_tensor(xT[:, t, :], xT[:, t, :], col("final_g_2", t), bank(6),
                                                   ALU.mult, ALU.mult))
        PE.need(m)
        if t >= 4:
            PE.need(back[t - 4])
        else:
            back = {} if t == 0 else back
        for k in range(NB):
            ins = nc.tensor.transpose(bank(t % 4, P, k * P), xT[:, t, k * P:(k + 1) * P], ident[:])
        m = PE.sig(ins)
        ACTE.need(m)
        back[t] = act(tok[:, :, t * P:(t + 1) * P], bank(t % 4).rearrange("p (b n) -> p b n", b=NB))
        if t % 4 == 3:
            SP.wait_ge(ACTE.sem, ACTE.n)
            half = slice((t - 3) * P, (t + 1) * P)
            SP.dma_start(a["out"][0][:, half].rearrange("(b p) d -> p b d", p=P), tok[:, :, half]).then_inc(sem_out, 16)
    SP.wait_ge(sem_out, 32)
    assert chunk[0] == sent[0], (chunk, sent)


INPUTS = ["x", "mem", "norm_mix_pre", "w_in", "lambda_q1", "lambda_k1", "lambda_q2", "lambda_k2", "subln_g",
          "w_attn_branch", "pool_w", "pool_scale", "w_pool_branch", "norm_mem", "w_mem_kv", "w_mem_branch", "w_out",
          "norm_mix_post", "norm_ffn_pre", "w_up", "conv_w", "conv_b", "w_down", "norm_ffn_post", "c_2", "ctx_2",
          "c_ctx_2", "mod_w_2", "mod_b_2", "norm_g_2", "ev_w_in_2", "ev_w_out_2", "a_q_gain_2", "a_k_gain_2",
          "b_sink_2", "od_w_in_2", "od_w_out_2", "c_dw_w_2", "c_dw_b_2", "c_ln_g_2", "c_ln_b_2", "final_g_2"]


def kernel(**inputs):
    import concourse.bacc as bacc
    from concourse.bass_utils import run_bass_kernel_spmd

    arrays = {n: np.ascontiguousarray(inputs[n]) for n in INPUTS}
    rpb = np.asarray(inputs["d_rpb_2"])[0]
    padded = np.zeros((rpb.shape[0], rpb.shape[1], 2 * GRID_W - 1), rpb.dtype)
    padded[:, :, GRID_W - NA_KW:GRID_W + NA_KW - 1] = rpb
    arrays["rpb_padded"] = padded
    for n, v in shape_tables().items():
        arrays["t_" + n] = np.ascontiguousarray(v)
    nc = bacc.Bacc("TRN2", target_bir_lowering=False, num_devices=1)
    aps = {n: nc.dram_tensor("in_" + n, v.shape, mybir.dt.from_np(v.dtype), kind="ExternalInput").ap()
           for n, v in arrays.items()}
    aps["out"] = nc.dram_tensor("out_0", (1, SEQ, D_MODEL), F32, kind="ExternalOutput").ap()
    build(nc, aps)
    r = run_bass_kernel_spmd(nc, [{"in_" + n: v for n, v in arrays.items()}], core_ids=[0])
    return r.results[0]["out_0"]
```
